# Optimizing a Trainium2 kernel written in Bass

```python
import math
import jax, jax.numpy as jnp
from jax import lax
import numpy as np

D_MODEL = 1024
BATCH = 1
SEQ = 1024
DEPTH = 1
DEC_BATCH = 8
DEC_SEQ = 8
PAST_LEN = 8192
PAGE_SIZE = 128

D_MIX = D_MODEL
D_A = D_MIX // 2
D_B = D_MIX - D_A
HEAD_DIM = 128
N_HEADS_A = D_A // HEAD_DIM
CONV_W = 4
CHUNK = 64
POOL_WINDOWS = (2, 4, 8, 16)
N_POOL_GROUPS = len(POOL_WINDOWS)
POOL_GROUP_DIM = D_B // N_POOL_GROUPS
POOL_BUF = max(POOL_WINDOWS) - 1
N_EXPERT_GROUPS = 4
EXPERTS_PER_GROUP = 8
TOP_K_FINE = 2
D_EXPERT = D_MODEL // 4
ALPHA = (2.0 * DEPTH) ** 0.25
BETA_INIT = (8.0 * DEPTH) ** -0.25
LN_EPS = 1e-5
RMS_EPS = 1e-6
L2_EPS = 1e-6
COL_Q = 0
COL_K = D_A
COL_V = 2 * D_A
COL_Z = 3 * D_A
COL_B = 4 * D_A
COL_A = 4 * D_A + N_HEADS_A
COL_P = 4 * D_A + 2 * N_HEADS_A
D_IN_PROJ = COL_P + D_B

kernel_name = "hymba_gdn_pool_hiermoe_deepnorm_step"

def layer_norm(x, g, b):
    xf = x.astype(jnp.float32)
    mu = jnp.mean(xf, -1, keepdims=True)
    var = jnp.mean(jnp.square(xf - mu), -1, keepdims=True)
    y = (xf - mu) * lax.rsqrt(var + LN_EPS) * g.astype(jnp.float32) + b.astype(jnp.float32)
    return y.astype(x.dtype)

def l2norm(x):
    return x * lax.rsqrt(jnp.sum(x * x, -1, keepdims=True) + L2_EPS)

def causal_conv(u, buf, w):
    L = u.shape[1]
    xp = jnp.concatenate([buf.astype(u.dtype), u], axis=1)
    y = sum(xp[:, j:j + L] * w[j] for j in range(CONV_W))
    return jax.nn.silu(y), xp[:, -(CONV_W - 1):]

def gated_delta_rule(q, k, v, g, beta, s0):
    B, L, H, DK = q.shape
    DV = v.shape[-1]
    pad = (-L) % CHUNK
    padt = lambda a: jnp.pad(a, [(0, 0), (0, pad)] + [(0, 0)] * (a.ndim - 2))
    q, k, v, g, beta = (padt(a) for a in (q, k, v, g, beta))
    n = (L + pad) // CHUNK

    def chunks(a):
        a = a.reshape((B, n, CHUNK) + a.shape[2:])
        return jnp.moveaxis(a, (1, 3), (0, 2))

    qc, kc, vc, gc, bc = (chunks(a) for a in (q, k, v, g, beta))
    gc = jnp.cumsum(gc, axis=-1)
    kb = kc * bc[..., None]
    vb = vc * bc[..., None]
    idx = jnp.arange(CHUNK)
    incl = idx[:, None] >= idx[None, :]
    strict = idx[:, None] > idx[None, :]
    diff = gc[..., :, None] - gc[..., None, :]
    decay = jnp.exp(jnp.where(incl, diff, -jnp.inf))
    a_strict = jnp.where(strict, jnp.einsum('nbhid,nbhjd->nbhij', kb, kc) * decay, 0.0)
    m = jnp.eye(CHUNK, dtype=jnp.float32) + a_strict
    rhs = jnp.concatenate([vb, kb * jnp.exp(gc)[..., None]], axis=-1)
    sol = lax.linalg.triangular_solve(m, rhs, left_side=True, lower=True, unit_diagonal=True)
    u_c = sol[..., :DV]
    w_c = sol[..., DV:]
    qk = jnp.einsum('nbhid,nbhjd->nbhij', qc, kc) * decay

    def step(S, xs):
        q_i, k_i, u_i, w_i, qk_i, g_i = xs
        v_new = u_i - jnp.einsum('bhcd,bhde->bhce', w_i, S)
        o = (jnp.einsum('bhcd,bhde->bhce', q_i * jnp.exp(g_i)[..., None], S)
             + jnp.einsum('bhij,bhje->bhie', qk_i, v_new))
        g_last = g_i[..., -1]
        S = (S * jnp.exp(g_last)[..., None, None]
             + jnp.einsum('bhcd,bhce->bhde', k_i * jnp.exp(g_last[..., None] - g_i)[..., None], v_new))
        return S, o

    s_fin, o = lax.scan(step, s0, (qc, kc, u_c, w_c, qk, gc))
    o = jnp.moveaxis(o, (0, 2), (1, 3)).reshape(B, n * CHUNK, H, DV)[:, :L]
    return o, s_fin

def gdn_mixer(proj, conv_buf, s0, conv_w, a_log, dt_bias, norm_w):
    B, L, _ = proj.shape
    qkv, conv_new = causal_conv(proj[..., COL_Q:COL_Q + 3 * D_A], conv_buf, conv_w)
    qkv = qkv.astype(jnp.float32).reshape(B, L, 3, N_HEADS_A, HEAD_DIM)
    q = l2norm(qkv[:, :, 0]) * (HEAD_DIM ** -0.5)
    k = l2norm(qkv[:, :, 1])
    v = qkv[:, :, 2]
    z = proj[..., COL_Z:COL_Z + D_A].astype(jnp.float32).reshape(B, L, N_HEADS_A, HEAD_DIM)
    beta = jax.nn.sigmoid(proj[..., COL_B:COL_B + N_HEADS_A].astype(jnp.float32))
    a = proj[..., COL_A:COL_A + N_HEADS_A].astype(jnp.float32)
    g = -jnp.exp(a_log.astype(jnp.float32)) * jax.nn.softplus(a + dt_bias.astype(jnp.float32))
    o, s_new = gated_delta_rule(q, k, v, g, beta, s0.astype(jnp.float32))
    o = o * lax.rsqrt(jnp.mean(o * o, -1, keepdims=True) + RMS_EPS) * norm_w.astype(jnp.float32)
    o = o * jax.nn.silu(z)
    return o.reshape(B, L, D_A).astype(proj.dtype), conv_new, s_new

def pool_mixer(u, buf, start, pool_w, pool_scale):
    B, L, _ = u.shape
    xp = jnp.concatenate([buf.astype(u.dtype), u], axis=1)
    c = jnp.cumsum(xp.astype(jnp.float32), axis=1)
    c = jnp.concatenate([jnp.zeros((B, 1, D_B), jnp.float32), c], axis=1)
    pos = start + jnp.arange(L)
    means = []
    for gi, w in enumerate(POOL_WINDOWS):
        sl = slice(gi * POOL_GROUP_DIM, (gi + 1) * POOL_GROUP_DIM)
        s = c[:, POOL_BUF + 1:POOL_BUF + 1 + L, sl] - c[:, POOL_BUF + 1 - w:POOL_BUF + 1 - w + L, sl]
        cnt = jnp.minimum(pos + 1, w).astype(jnp.float32)
        means.append(s / cnt[None, :, None])
    d = (jnp.concatenate(means, -1) - u.astype(jnp.float32)).astype(u.dtype)
    d = d.reshape(B, L, N_POOL_GROUPS, POOL_GROUP_DIM)
    y = jnp.einsum('blgc,gcd->blgd', d, pool_w).reshape(B, L, D_B) * pool_scale
    return y, xp[:, -POOL_BUF:]

def hier_moe(h, w_rg, b_rg, w_re, b_re, w_gate, w_up, w_down):
    B, L, _ = h.shape
    lg = (h @ w_rg).astype(jnp.float32) + b_rg.astype(jnp.float32)
    pg = jax.nn.softmax(lg, axis=-1)
    onehot_g = jax.nn.one_hot(jnp.argmax(lg, axis=-1), N_EXPERT_GROUPS, dtype=jnp.float32)
    pg_sel = jnp.sum(pg * onehot_g, -1)
    le = ((h @ w_re).astype(jnp.float32) + b_re.astype(jnp.float32)).reshape(
        B, L, N_EXPERT_GROUPS, EXPERTS_PER_GROUP)
    le_sel = jnp.einsum('blge,blg->ble', le, onehot_g)
    top_v, top_i = lax.top_k(le_sel, TOP_K_FINE)
    wk = jax.nn.softmax(top_v, axis=-1) * pg_sel[..., None]
    w_fine = jnp.einsum('blk,blke->ble', wk, jax.nn.one_hot(top_i, EXPERTS_PER_GROUP, dtype=jnp.float32))
    gate = (onehot_g[..., :, None] * w_fine[..., None, :]).astype(h.dtype)
    y = jnp.zeros_like(h)
    for gi in range(N_EXPERT_GROUPS):
        a = jnp.einsum('bld,edf->blef', h, w_gate[gi])
        b = jnp.einsum('bld,edf->blef', h, w_up[gi])
        act = jax.nn.silu(a) * b * gate[:, :, gi, :, None]
        y = y + jnp.einsum('blef,efd->bld', act, w_down[gi])
    return y

def decoder_layer(x, delta0, conv0, pool0, start, w_in, conv_w, a_log, dt_bias, gdn_norm_w,
                  pool_w, pool_scale, w_out, ln1_g, ln1_b, w_rg, b_rg, w_re, b_re,
                  w_gate, w_up, w_down, ln2_g, ln2_b):
    proj = x @ w_in
    ya, conv_new, delta_new = gdn_mixer(proj, conv0, delta0, conv_w, a_log, dt_bias, gdn_norm_w)
    yb, pool_new = pool_mixer(proj[..., COL_P:COL_P + D_B], pool0, start, pool_w, pool_scale)
    mix = jnp.concatenate([ya, yb], axis=-1) @ w_out
    h = layer_norm(ALPHA * x + mix, ln1_g, ln1_b)
    y = layer_norm(ALPHA * h + hier_moe(h, w_rg, b_rg, w_re, b_re, w_gate, w_up, w_down), ln2_g, ln2_b)
    return y, delta_new, conv_new, pool_new

def setup_inputs(seed: int = 0) -> dict:
    key = jax.random.key(seed)
    ks = jax.random.split(key, 24)
    nrm = lambda k, s, sc: jax.random.normal(k, s, jnp.float32) * sc
    G, E = N_EXPERT_GROUPS, EXPERTS_PER_GROUP
    dt = jnp.exp(jax.random.uniform(ks[6], (DEPTH, N_HEADS_A), minval=math.log(1e-3), maxval=math.log(1e-1)))
    return {
        "x_prompt": nrm(ks[0], (BATCH, SEQ, D_MODEL), 1.0),
        "x_sample": nrm(ks[1], (DEC_BATCH, DEC_SEQ, D_MODEL), 1.0),
        "state_delta": nrm(ks[2], (DEPTH, DEC_BATCH, N_HEADS_A, HEAD_DIM, HEAD_DIM), 0.5),
        "state_conv": nrm(ks[3], (DEPTH, DEC_BATCH, CONV_W - 1, 3 * D_A), 1.0),
        "state_pool": nrm(ks[4], (DEPTH, DEC_BATCH, POOL_BUF, D_B), 1.0),
        "w_in": nrm(ks[5], (DEPTH, D_MODEL, D_IN_PROJ), D_MODEL ** -0.5),
        "conv_w": nrm(ks[7], (DEPTH, CONV_W, 3 * D_A), CONV_W ** -0.5),
        "a_log": jnp.log(jax.random.uniform(ks[8], (DEPTH, N_HEADS_A), minval=1.0, maxval=16.0)),
        "dt_bias": dt + jnp.log(-jnp.expm1(-dt)),
        "gdn_norm_w": 1.0 + nrm(ks[9], (DEPTH, HEAD_DIM), 0.02),
        "pool_w": nrm(ks[10], (DEPTH, N_POOL_GROUPS, POOL_GROUP_DIM, POOL_GROUP_DIM), POOL_GROUP_DIM ** -0.5),
        "pool_scale": 1.0 + nrm(ks[11], (DEPTH, D_B), 0.02),
        "w_out": nrm(ks[12], (DEPTH, D_MIX, D_MODEL), BETA_INIT * D_MIX ** -0.5),
        "ln1_g": 1.0 + nrm(ks[13], (DEPTH, D_MODEL), 0.02),
        "ln1_b": nrm(ks[14], (DEPTH, D_MODEL), 0.02),
        "w_rg": nrm(ks[15], (DEPTH, D_MODEL, G), D_MODEL ** -0.5),
        "b_rg": nrm(ks[16], (DEPTH, G), 0.01),
        "w_re": nrm(ks[17], (DEPTH, D_MODEL, G * E), D_MODEL ** -0.5),
        "b_re": nrm(ks[18], (DEPTH, G * E), 0.01),
        "w_gate": nrm(ks[19], (DEPTH, G, E, D_MODEL, D_EXPERT), D_MODEL ** -0.5),
        "w_up": nrm(ks[20], (DEPTH, G, E, D_MODEL, D_EXPERT), D_MODEL ** -0.5),
        "w_down": nrm(ks[21], (DEPTH, G, E, D_EXPERT, D_MODEL), BETA_INIT * D_EXPERT ** -0.5),
        "ln2_g": 1.0 + nrm(ks[22], (DEPTH, D_MODEL), 0.02),
        "ln2_b": nrm(ks[23], (DEPTH, D_MODEL), 0.02),
    }

def reference(x_prompt, x_sample, state_delta, state_conv, state_pool, w_in, conv_w, a_log, dt_bias,
              gdn_norm_w, pool_w, pool_scale, w_out, ln1_g, ln1_b, w_rg, b_rg, w_re, b_re,
              w_gate, w_up, w_down, ln2_g, ln2_b):
    yp, ys = x_prompt, x_sample
    dp_l, cp_l, pp_l, ds_l, cs_l, ps_l = [], [], [], [], [], []
    for l in range(DEPTH):
        wts = (w_in[l], conv_w[l], a_log[l], dt_bias[l], gdn_norm_w[l], pool_w[l], pool_scale[l],
               w_out[l], ln1_g[l], ln1_b[l], w_rg[l], b_rg[l], w_re[l], b_re[l],
               w_gate[l], w_up[l], w_down[l], ln2_g[l], ln2_b[l])
        d0 = jnp.zeros((BATCH, N_HEADS_A, HEAD_DIM, HEAD_DIM), jnp.float32)
        c0 = jnp.zeros((BATCH, CONV_W - 1, 3 * D_A), x_prompt.dtype)
        p0 = jnp.zeros((BATCH, POOL_BUF, D_B), x_prompt.dtype)
        yp, dp, cp, pp = decoder_layer(yp, d0, c0, p0, 0, *wts)
        ys, ds, cs, ps = decoder_layer(ys, state_delta[l], state_conv[l], state_pool[l], PAST_LEN, *wts)
        dp_l.append(dp.astype(state_delta.dtype)); cp_l.append(cp.astype(state_conv.dtype))
        pp_l.append(pp.astype(state_pool.dtype)); ds_l.append(ds.astype(state_delta.dtype))
        cs_l.append(cs.astype(state_conv.dtype)); ps_l.append(ps.astype(state_pool.dtype))
    delta_prompt = jnp.stack(dp_l)
    conv_prompt = jnp.stack(cp_l)
    pool_prompt = jnp.stack(pp_l)
    delta_sample = jnp.stack(ds_l)
    conv_sample = jnp.stack(cs_l)
    pool_sample = jnp.stack(ps_l)
    return (yp, ys, delta_prompt, conv_prompt, pool_prompt, delta_sample, conv_sample, pool_sample)


_drawn_inputs = setup_inputs


def setup_inputs(seed=0):
    import zlib

    import numpy as np

    out = dict(_drawn_inputs(seed))
    spreads = {}
    factors = {'gdn_norm_w': 19.269,
     'pool_scale': 22.415,
     'b_rg': 20.809,
     'b_re': 15.648,
     'ln2_g': 22.529,
     'ln2_b': 23.184}
    for name, (base, spread) in spreads.items():
        noise = np.random.default_rng([zlib.crc32(name.encode()), seed]).standard_normal(out[name].shape)
        drawn = base * np.exp(spread * noise) if base else spread * noise
        out[name] = __import__('jax').numpy.asarray(drawn.astype(out[name].dtype))
    for name, factor in factors.items():
        out[name] = (out[name] * factor).astype(out[name].dtype)
    return out
```

```python
from contextlib import ExitStack

import numpy as np

import concourse.bass as bass
from concourse import mybir
from concourse.bass import ds

F32 = mybir.dt.float32
I32 = mybir.dt.int32
ALU = mybir.AluOpType
ACT = mybir.ActivationFunctionType
AX = mybir.AxisListType

P = 128
D = 1024
KT = D // P
SEQ = 1024
NSEQ, DSEQ = 8, 8
NS = NSEQ * DSEQ
T = SEQ + NS
PT = SEQ // P
NT = PT + 1
TP = NT * P
H = 4
HD = 128
DA = H * HD
CW = 4
CH = CW - 1
NCONV = 3 * DA // P
G = 4
PH = 15
NCH = NCONV + H + G
COL_BA = 4 * DA
COL_POOL = COL_BA + 2 * H
EPG = 8
NE = G * EPG
FE = 256
ALPHA = 2.0 ** 0.25
LN_EPS, RMS_EPS, L2_EPS = 1e-5, 1e-6, 1e-6
TAIL = 16
NTAIL = TAIL + NS
SLOTS = TP
NLIST = NE + 1
MAXOV = 20
NTILES = NE + MAXOV
SKIP = 1 << 20
CSEG = CH + DSEQ
CRAW = CH + SEQ + NSEQ * CSEG
CFLAT = CRAW - CH
PSEG = PH + DSEQ
PRAW = PH + SEQ + NSEQ * PSEG
NEG = -1e30

CONST = {}


def constants():
    i = np.arange(P)
    col, row = i[None, :], i[:, None]
    seq_r, seq_c = row // DSEQ, col // DSEQ
    same = (seq_r == seq_c) & (row < NS) & (col < NS)
    parts = {
        "ident": (row == col),
        "ones": np.ones((P, P)),
        "tri": row <= col,
        "tri_s": (row <= col) & same,
        "strict": row < col,
        "same": same,
        "neg": np.where(row <= col, 0.0, NEG),
        "neg_s": np.where((row <= col) & same, 0.0, NEG),
        "m1t": (col // 2 == row // 2) & (col % 2 == 1) & (row % 2 == 0),
    }
    for b in (2, 4, 8, 16, 32, 64):
        parts[f"m{b}"] = (row // (2 * b) == col // (2 * b)) & ((row // b) % 2 == 1) & ((col // b) % 2 == 0)
    parts["seqmask"] = (seq_r == np.arange(NSEQ)[None, :]) & (row < NS)
    rc = np.zeros((G, PH))
    for g in range(G):
        rc[g] = 1.0 / np.minimum(np.arange(PH) + 1, 2 << g)
    parts["rc"] = np.broadcast_to(rc.reshape(1, -1), (P, G * PH))
    parts["w4"] = np.broadcast_to(G - np.arange(G)[None, :], (P, G))
    parts["w8"] = np.broadcast_to(EPG - np.arange(EPG)[None, :], (P, EPG))
    parts["slot0"] = np.broadcast_to(SLOTS * np.arange(NE)[None, :], (P, NE))
    tok = np.arange(NT)[None, :] * P + row
    parts["token"] = tok
    parts["valid"] = tok < T
    parts["skip"] = np.where(tok < T, 0.0, float(SKIP))
    parts["rank"] = np.broadcast_to(np.arange(MAXOV)[None, :], (P, MAXOV))
    parts["even"] = np.broadcast_to(2.0 * np.arange(MAXOV // 2)[None, :], (P, MAXOV // 2))
    at, cols = 0, []
    for name, a in parts.items():
        a = np.broadcast_to(a, (P, a.shape[1])).astype(np.float32)
        CONST[name] = (at, a.shape[1])
        at += a.shape[1]
        cols.append(a)
    return np.ascontiguousarray(np.concatenate(cols, axis=1))


def build(nc, cst_d, x_d, xs_d, sdelta_d, sconv_d, spool_d, w_in_d, conv_w_d, a_log_d, dt_d, gnw_d, pool_w_d,
          pscale_d, w_out_d, ln1g_d, ln1b_d, wrg_d, brg_d, wre_d, bre_d, wg_d, wu_d, wd_d, ln2g_d, ln2b_d,
          yp_o, ys_o, dp_o, cp_o, pp_o, dsm_o, cs_o, ps_o, yb_d, h_d, y2_d, tab_d):
    pe, dve, act, pool, sp = nc.tensor, nc.vector, nc.scalar, nc.gpsimd, nc.sync
    whole = ExitStack()

    def sb(name, shape, dt=F32, ctx=whole):
        return ctx.enter_context(nc.sbuf_tensor(name, shape, dt))

    def pb(name, shape, ctx):
        return ctx.enter_context(nc.psum_tensor(name, shape, F32))

    def phase(stack):
        mine = []

        def sem(name):
            mine.append(nc.alloc_semaphore(name))
            return mine[-1]

        def give_back():
            nc.clear_and_free_semaphores(mine)
            nc.all_engine_barrier()
        stack.callback(give_back)
        return sem

    def bc(ap, n):
        return ap.unsqueeze(len(ap.shape)).broadcast_to(tuple(ap.shape) + (n,))

    def mid(ap, n):
        return ap.unsqueeze(1).broadcast_to((ap.shape[0], n) + tuple(ap.shape[1:]))

    def wait(e, semaphore, n):
        if not isinstance(n, int) or n > 0:
            e.wait_ge(semaphore, n)

    def turns(e, n, body):
        body(0)
        with e.Fori(1, n) as i:
            body(i)

    with whole:
        nconst = sum(n for _, n in CONST.values())
        cst = sb("cst", [P, nconst])

        def C(name):
            at, n = CONST[name]
            return cst[:, at:at + n]

        qkvT = sb("qkvT", [P, NCONV, TP])
        szT = sb("szT", [P, H, TP])
        beta = sb("beta", [P, NT, H])
        ngc = sb("ngc", [P, NT, H])
        egc = sb("egc", [P, NT, H])
        edec = sb("edec", [P, NT, H])
        gdec = sb("gdec", [P, NT, H])
        eglast = sb("eglast", [P, NT, H])
        eglast_s = sb("eglast_s", [P, NSEQ, H])
        gnw = sb("gnw", [P, 1])
        mhalf = sb("mhalf", [P, 16])
        logits = sb("logits", [P, NT, G + NE])

        with ExitStack() as c1:
            xin_tails = sb("xin_tails", [P, 2 * D], ctx=c1)
            xin = [xin_tails[:, i * D:(i + 1) * D] for i in range(2)]
            tails = xin_tails[0:NTAIL, :]
            xT = sb("xT", [P, KT, T], ctx=c1)
            ybT = sb("ybT", [P, G, TP], ctx=c1)
            wblk = [sb(f"wblk{i}", [P, KT, P], ctx=c1) for i in range(2)]
            wba = sb("wba", [P, KT, 2 * H], ctx=c1)
            sums_rows = sb("sums_rows", [P, 2 * PRAW], ctx=c1)
            crow = sums_rows[0:NSEQ * CH + CW, 0:NCONV * P]
            prow = sums_rows[0:NSEQ * PH + 1, NCONV * P:(NCONV + G) * P]
            psA, psB = sums_rows[:, 0:PRAW], sums_rows[:, PRAW:]
            ccol = sb("ccol", [P, NCONV, NSEQ * CH + CW], ctx=c1)
            pcol = sb("pcol", [P, G, NSEQ * PH + 1], ctx=c1)
            raw = [sb(f"raw{i}", [P, CRAW], ctx=c1) for i in range(2)]
            cv = sb("cv", [P, CRAW], ctx=c1)
            ub = [sb(f"ub{i}", [P, PRAW], ctx=c1) for i in range(2)]
            dif = [sb(f"dif{i}", [P, PRAW], ctx=c1) for i in range(2)]
            fix = sb("fix", [P, PH], ctx=c1)
            poolw = sb("poolw", [P, G, P], ctx=c1)
            tailT = sb("tailT", [P, NCONV + G, NTAIL], ctx=c1)
            ba = sb("ba", [P, NT, 2 * H], ctx=c1)
            dtb = sb("dtb", [P, H], ctx=c1)
            alog = sb("alog", [P, H], ctx=c1)
            g1 = sb("g1", [P, NT, H], ctx=c1)
            g2 = sb("g2", [P, NT, H], ctx=c1)
            g3 = sb("g3", [P, NT, H], ctx=c1)
            gseq = sb("gseq", [P, NSEQ, H], ctx=c1)
            pj = [pb(f"pj{i}", [P, 1536], c1) for i in range(2)]
            pc = pb("pc", [P, 512], c1)
            pd = pb("pd", [P, 512], c1)

            S = phase(c1)
            cst_in, rows_in, small_in = S("cst_in"), S("rows_in"), S("small_in")
            x_in = [S(f"x_in{i}") for i in range(2)]
            x_turned = [S(f"x_turned{i}") for i in range(2)]
            xT_ready = [S(f"xT_ready{i}") for i in range(2)]
            w_in_sem = [S(f"w_in{i}") for i in range(2)]
            proj_done = [S(f"proj_done{i}") for i in range(2)]
            proj_read = [S(f"proj_read{i}") for i in range(2)]
            hist_turned, hist_ready = S("hist_turned"), S("hist_ready")
            ba_done, ba_ready = S("ba_done"), S("ba_ready")
            zeroed = S("zeroed")
            seg_ready = [S(f"seg_ready{i}") for i in range(2)]
            tail_ready = [S(f"tail_ready{i}") for i in range(2)]
            taps, conv_done, conv_read = S("taps"), S("conv_done"), S("conv_read")
            poolc = S("poolc")
            dif_ready, mixed, yb_ready = S("dif_ready"), S("mixed"), S("yb_ready")
            tails_turned, tails_ready, state_out = S("tails_turned"), S("tails_ready"), S("state_out")
            exp1, gch = S("exp1"), S("gch")
            g_ready, gsum_done, gates_done = S("g_ready"), S("gsum_done"), S("gates_done")
            x_sample, xs_turned, xs_ready = S("x_sample"), S("xs_turned"), S("xs_ready")

            def raw_seg(par):
                return raw[par][:, CH + SEQ:CRAW].rearrange("p (s c) -> p s c", c=CSEG)

            def ub_seg(par):
                return ub[par][:, PH + SEQ:PRAW].rearrange("p (s c) -> p s c", c=PSEG)

            with nc.Block() as block:
                @block.sync
                def _(e):
                    sp.dma_start(cst[:, :], cst_d).then_inc(cst_in, 16)
                    x_v = x_d[0].rearrange("(t p) d -> t p d", p=P)

                    def load_x(i):
                        for par in range(2):
                            wait(e, x_turned[par], i)
                            sp.dma_start(xin[par], x_v[ds(2 * i + par, 1)].rearrange("a p d -> (a p) d")
                                         ).then_inc(x_in[par], 16)
                    turns(e, PT // 2, load_x)
                    e.wait_ge(x_turned[0], PT // 2)
                    sp.dma_start(xin[0][0:NS, :], xs_d.rearrange("s t d -> (s t) d")).then_inc(x_sample, 16)
                    w_v = w_in_d[0].rearrange("(k p) c -> p k c", p=P)

                    def block_of_columns(n, par, at):
                        wait(e, proj_done[par], n)
                        sp.dma_start(wblk[par][:, :, :], w_v[:, :, at]).then_inc(w_in_sem[par], 16)

                    def load_columns(i):
                        for par in range(2):
                            block_of_columns(i, par, ds((2 * i + par) * P, P))
                    turns(e, (NCONV + H) // 2, load_columns)
                    for g in range(G):
                        block_of_columns((NCONV + H + g) // 2, g % 2,
                                         slice(COL_POOL + g * P, COL_POOL + (g + 1) * P))
                    e.wait_ge(yb_ready, G)
                    sp.dma_start(yb_d.rearrange("g p t -> p g t"), ybT[:, :, :]).then_inc(state_out, 16)
                    e.wait_ge(tails_ready, 2)
                    sp.dma_start(cp_o[0, 0], tails[TAIL - CH:TAIL, 0:NCONV * P]).then_inc(state_out, 16)
                    sp.dma_start(pp_o[0, 0], tails[TAIL - PH:TAIL, NCONV * P:]).then_inc(state_out, 16)
                    for s in range(NSEQ):
                        r = TAIL + s * DSEQ
                        sp.dma_start(cs_o[0, s], tails[r + DSEQ - CH:r + DSEQ, 0:NCONV * P]).then_inc(state_out, 16)
                        sp.dma_start(ps_o[0, s, PH - DSEQ:, :], tails[r:r + DSEQ, NCONV * P:]
                                     ).then_inc(state_out, 16)
                    sp.dma_start(ps_o[0, :, 0:PH - DSEQ, :], spool_d[0, :, DSEQ:, :]).then_inc(state_out, 16)
                    e.wait_ge(state_out, 16 * (4 + 2 * NSEQ))

                @block.gpsimd
                def _(e):
                    e.dma_start(crow[0:NSEQ * CH, :], sconv_d[0].rearrange("s t c -> (s t) c")).then_inc(rows_in, 16)
                    e.dma_start(crow[NSEQ * CH:, :], conv_w_d[0]).then_inc(rows_in, 16)
                    e.dma_start(prow[0:NSEQ * PH, :], spool_d[0].rearrange("s t c -> (s t) c")).then_inc(rows_in, 16)
                    e.dma_start(prow[NSEQ * PH:, :], pscale_d).then_inc(rows_in, 16)
                    e.dma_start(wba[:, :, :], w_in_d[0, :, COL_BA:COL_POOL].rearrange("(k p) c -> p k c", p=P)
                                ).then_inc(small_in, 16)
                    e.dma_start(poolw[:, :, :], pool_w_d[0].rearrange("g c d -> c g d")).then_inc(small_in, 16)
                    e.dma_start(dtb[:, :], dt_d.broadcast_to((P, H))).then_inc(small_in, 16)
                    e.dma_start(alog[:, :], a_log_d.broadcast_to((P, H))).then_inc(small_in, 16)
                    e.dma_start(gnw[:, :], gnw_d.rearrange("a p -> p a")).then_inc(small_in, 16)
                    for par in range(2):
                        pool.memset(raw[par][:, 0:CH], 0.0)
                        pool.memset(ub[par][:, 0:PH], 0.0)
                    pool.memset(qkvT[:, :, T:], 0.0)
                    pool.memset(szT[:, :, T:], 0.0)
                    pool.memset(ybT[:, :, T:], 0.0)
                    pool.memset(ba[:, :, :], 0.0)
                    pool.memset(mhalf[:, :], -0.5).then_inc(zeroed, 1)
                    e.wait_ge(hist_ready, 2)

                    def conv_segments(par, c):
                        pool.tensor_copy(raw_seg(par)[:, :, 0:CH],
                                         ccol[:, c, 0:NSEQ * CH].rearrange("p a (s t) -> p (a s) t", t=CH)
                                         ).then_inc(seg_ready[par], 1)

                    def conv_tail(n, par, c):
                        e.wait_ge(proj_read[par], n)
                        pool.tensor_copy(tailT[:, c, 0:TAIL].rearrange("p a t -> p (a t)"),
                                         raw[par][:, CH + SEQ - TAIL:CH + SEQ])
                        pool.tensor_copy(tailT[:, c, TAIL:].rearrange("p a (s t) -> p (a s) t", t=DSEQ),
                                         raw_seg(par)[:, :, CH:]).then_inc(tail_ready[par], 1)

                    def conv_pair(i):
                        wait(e, conv_done, 2 * i)
                        for par in range(2):
                            conv_segments(par, ds(2 * i + par, 1))
                            conv_tail(i + 1, par, ds(2 * i + par, 1))
                    turns(e, NCONV // 2, conv_pair)
                    for g in range(G):
                        par = g % 2
                        if g >= 2:
                            e.wait_ge(dif_ready, g - 1)
                        pool.tensor_copy(ub_seg(par)[:, :, 0:PH],
                                         pcol[:, g, 0:NSEQ * PH].rearrange("p (s t) -> p s t", t=PH)
                                         ).then_inc(seg_ready[par], 1)
                        e.wait_ge(proj_read[par], (NCONV + H) // 2 + g // 2 + 1)
                        pool.tensor_copy(tailT[:, NCONV + g, 0:TAIL], ub[par][:, PH + SEQ - TAIL:PH + SEQ])
                        pool.tensor_copy(tailT[:, NCONV + g, TAIL:].rearrange("p (s t) -> p s t", t=DSEQ),
                                         ub_seg(par)[:, :, PH:]).then_inc(tail_ready[par], 1)

                @block.tensor
                def _(e):
                    e.wait_ge(cst_in, 16)
                    e.wait_ge(rows_in, 64)
                    nh, npr = NSEQ * CH + CW, NSEQ * PH + 1
                    for c in range(NCONV):
                        last = pe.transpose(pc[:, c * nh:(c + 1) * nh], crow[:, c * P:(c + 1) * P],
                                            C("ident")[0:nh, 0:nh])
                    last.then_inc(hist_turned, 1)
                    for g in range(G):
                        last = pe.transpose(pd[:, g * npr:(g + 1) * npr], prow[:, g * P:(g + 1) * P],
                                            C("ident")[0:npr, 0:npr])
                    last.then_inc(hist_turned, 1)

                    def turn_x(i):
                        for par in range(2):
                            e.wait_ge(x_in[par], 16 * i + 16)
                            wait(e, xT_ready[par], i)
                            for k in range(KT):
                                last = pe.transpose(pj[par][:, k * P:(k + 1) * P], xin[par][:, k * P:(k + 1) * P],
                                                    C("ident"))
                            last.then_inc(x_turned[par], 1)
                    turns(e, PT // 2, turn_x)
                    e.wait_ge(x_sample, 16)
                    e.wait_ge(xT_ready[0], PT // 2)
                    for k in range(KT):
                        last = pe.transpose(pj[0][:, k * NS:(k + 1) * NS], xin[0][0:NS, k * P:(k + 1) * P],
                                            C("ident")[0:NS, 0:NS])
                    last.then_inc(xs_turned, 1)
                    e.wait_ge(xT_ready[1], PT // 2)
                    e.wait_ge(xs_ready, 1)
                    e.wait_ge(small_in, 80)
                    e.wait_ge(hist_ready, 2)
                    for t in range(NT):
                        m = min(P, T - t * P)
                        for k in range(KT):
                            last = pe.matmul(pc[0:m, t * 2 * H:(t + 1) * 2 * H], xT[:, k, t * P:t * P + m],
                                             wba[:, k, :], start=(k == 0), stop=(k == KT - 1))
                    last.then_inc(ba_done, 1)

                    def project(par, n):
                        e.wait_ge(w_in_sem[par], 16 * n + 16)
                        wait(e, proj_read[par], n)
                        for k in range(KT):
                            for a, b in ((0, 512), (512, 1024), (1024, T)):
                                last = pe.matmul(pj[par][:, a:b], wblk[par][:, k, :], xT[:, k, a:b],
                                                 start=(k == 0), stop=(k == KT - 1))
                        last.then_inc(proj_done[par], 1)

                    project(0, 0)
                    project(1, 0)
                    e.wait_ge(g_ready, 1)
                    nprm = PT * H
                    prompt_g = gdec[:, 0:PT, :].rearrange("p t h -> p (t h)")
                    pe.matmul(pd[:, 0:nprm], C("tri"), prompt_g, start=True, stop=True)
                    pe.matmul(pd[:, nprm:nprm + H], C("tri_s"), gdec[:, PT, :], start=True, stop=True)
                    pe.matmul(pd[:, 64:64 + nprm], C("ones"), prompt_g, start=True, stop=True)
                    pe.matmul(pd[:, 64 + nprm:64 + nprm + H], C("same"), gdec[:, PT, :], start=True, stop=True)
                    pe.matmul(pd[:, 128:128 + NSEQ * H], C("ones"), gseq[:, :, :].rearrange("p s h -> p (s h)"),
                              start=True, stop=True).then_inc(gsum_done, 1)
                    with e.Fori(1, (NCONV + H) // 2) as i:
                        for par in range(2):
                            project(par, i)

                    def pool_map(g):
                        e.wait_ge(dif_ready, g + 1)
                        e.wait_ge(proj_read[g % 2], (NCONV + H) // 2 + g // 2 + 1)
                        segs = dif[g % 2][:, PH + SEQ:PRAW].rearrange("p (s c) -> p s c", c=PSEG)
                        for h in range(2):
                            pe.matmul(pj[g % 2][:, h * 512:(h + 1) * 512], poolw[:, g, :],
                                      dif[g % 2][:, PH + h * 512:PH + (h + 1) * 512], start=True, stop=True)
                        pe.matmul(pj[g % 2][:, SEQ:T].rearrange("p (s t) -> p s t", t=DSEQ), poolw[:, g, :],
                                  segs[:, :, PH:], start=True, stop=True).then_inc(mixed, 1)
                    n0 = (NCONV + H) // 2

                    def project_pool(g):
                        if g >= 2:
                            e.wait_ge(yb_ready, g - 1)
                        project(g % 2, n0 + g // 2)
                    for g in range(G):
                        project_pool(g)
                        if g >= 1:
                            pool_map(g - 1)
                    pool_map(G - 1)
                    e.wait_ge(yb_ready, G)
                    e.wait_ge(tail_ready[0], (NCONV + G) // 2)
                    e.wait_ge(tail_ready[1], (NCONV + G) // 2)
                    for c in range(NCONV + G):
                        bank, at = (pj[0], c * P) if c < NCONV else (pj[1], (c - NCONV) * P)
                        last = pe.transpose(bank[0:NTAIL, at:at + P], tailT[:, c, :], C("ident"))
                    last.then_inc(tails_turned, 1)

                @block.scalar
                def _(e):
                    e.wait_ge(hist_turned, 1)
                    act.activation(ccol[:, :, :].rearrange("p c n -> p (c n)"),
                                   pc[:, 0:NCONV * (NSEQ * CH + CW)], ACT.Copy).then_inc(hist_ready, 1)

                    with e.Fori(0, PT // 2) as i:
                        e.wait_ge(x_turned[0], i + 1)
                        act.activation(xT[:, :, ds(2 * i * P, P)],
                                       pj[0][:, 0:D].rearrange("p (k t) -> p k t", t=P), ACT.Copy
                                       ).then_inc(xT_ready[0], 1)
                    e.wait_ge(xs_turned, 1)
                    act.activation(xT[:, :, SEQ:T], pj[0][:, 0:KT * NS].rearrange("p (k t) -> p k t", t=NS),
                                   ACT.Copy).then_inc(xs_ready, 1)
                    e.wait_ge(ba_ready, 1)
                    act.activation(g2[:, :, :], ba[:, :, 0:H], ACT.Exp, scale=-1.0)
                    act.activation(g3[:, :, :], g1[:, :, :], ACT.Exp, scale=-1.0)
                    act.activation(alog[:, :], alog[:, :], ACT.Exp).then_inc(exp1, 1)
                    e.wait_ge(exp1, 1)
                    act.activation(g1[:, :, :], g3[:, :, :], ACT.Ln, bias=1.0).then_inc(exp1, 1)
                    e.wait_ge(gsum_done, 1)
                    sums = pd[:, 0:NT * H].rearrange("p (t h) -> p t h", h=H)
                    act.activation(egc[:, :, :], sums, ACT.Exp)
                    act.activation(ngc[:, :, :], sums, ACT.Copy, scale=-1.0).then_inc(gates_done, 1)
                    act.activation(eglast[:, :, :], pd[:, 64:64 + NT * H].rearrange("p (t h) -> p t h", h=H), ACT.Exp)
                    act.activation(eglast_s[:, :, :],
                                   pd[:, 128:128 + NSEQ * H].rearrange("p (s h) -> p s h", h=H), ACT.Exp
                                   ).then_inc(gates_done, 1)
                    e.wait_ge(gates_done, 3)
                    act.activation(edec[:, :, :], edec[:, :, :], ACT.Exp).then_inc(gates_done, 1)
                    def conv_io(i):
                        for par in range(2):
                            e.wait_ge(proj_done[par], i + 1)
                            wait(e, conv_done, 2 * i)
                            wait(e, tail_ready[par], i)
                            act.activation(raw[par][:, CH:CH + SEQ], pj[par][:, 0:SEQ], ACT.Copy)
                            act.activation(raw_seg(par)[:, :, CH:],
                                           pj[par][:, SEQ:T].rearrange("p (s t) -> p s t", t=DSEQ), ACT.Copy
                                           ).then_inc(proj_read[par], 1)
                            e.wait_ge(conv_done, 2 * i + par + 1)
                            c = ds(2 * i + par, 1)
                            act.activation(qkvT[:, c, 0:SEQ].rearrange("p a t -> p (a t)"), cv[:, 0:SEQ], ACT.Silu)
                            act.activation(qkvT[:, c, SEQ:T].rearrange("p a (s t) -> p (a s) t", t=DSEQ),
                                           cv[:, CH + SEQ:].rearrange("p (s c) -> p s c", c=CSEG)[:, :, 0:DSEQ],
                                           ACT.Silu).then_inc(conv_read, 1)
                    turns(e, NCONV // 2, conv_io)
                    with e.Fori(0, H // 2) as i:
                        for par in range(2):
                            e.wait_ge(proj_done[par], i + NCONV // 2 + 1)
                            act.activation(szT[:, ds(2 * i + par, 1), 0:T].rearrange("p a t -> p (a t)"),
                                           pj[par][:, 0:T], ACT.Silu).then_inc(proj_read[par], 1)

                    def pool_out(g):
                        e.wait_ge(mixed, g + 1)
                        act.activation(ybT[:, g, 0:T], pj[g % 2][:, 0:T], ACT.Copy,
                                       scale=pcol[:, g, NSEQ * PH:NSEQ * PH + 1]).then_inc(yb_ready, 1)
                    for g in range(G):
                        par = g % 2
                        if g >= 2:
                            e.wait_ge(tail_ready[par], NCONV // 2 + g // 2)
                            e.wait_ge(dif_ready, g - 1)
                        e.wait_ge(proj_done[par], (NCONV + H) // 2 + g // 2 + 1)
                        act.activation(ub[par][:, PH:PH + SEQ], pj[par][:, 0:SEQ], ACT.Copy)
                        act.activation(ub_seg(par)[:, :, PH:],
                                       pj[par][:, SEQ:T].rearrange("p (s t) -> p s t", t=DSEQ), ACT.Copy
                                       ).then_inc(proj_read[par], 1)
                        if g >= 1:
                            pool_out(g - 1)
                    pool_out(G - 1)
                    e.wait_ge(tails_turned, 1)
                    act.activation(tails[:, 0:NCONV * P], pj[0][0:NTAIL, :], ACT.Copy).then_inc(tails_ready, 1)

                @block.vector
                def _(e):
                    e.wait_ge(hist_turned, 2)
                    dve.tensor_copy(pcol[:, :, :].rearrange("p c n -> p (c n)"),
                                    pd[:, 0:G * (NSEQ * PH + 1)]).then_inc(hist_ready, 1)
                    with e.Fori(0, PT // 2) as i:
                        e.wait_ge(x_turned[1], i + 1)
                        dve.tensor_copy(xT[:, :, ds((2 * i + 1) * P, P)],
                                        pj[1][:, 0:D].rearrange("p (k t) -> p k t", t=P)).then_inc(xT_ready[1], 1)
                    chain = [0]

                    def link(ins):
                        chain[0] += 1
                        ins.then_inc(gch, 1)
                        e.wait_ge(gch, chain[0])
                    e.wait_ge(ba_done, 1)
                    e.wait_ge(zeroed, 1)
                    dve.tensor_copy(ba[:, 0:PT, :].rearrange("p t c -> p (t c)"), pc[:, 0:PT * 2 * H])
                    link(dve.tensor_copy(ba[0:NS, PT, :], pc[0:NS, PT * 2 * H:NT * 2 * H]))
                    link(dve.tensor_tensor(g2[:, :, :], ba[:, :, H:], mid(dtb[:, :], NT), ALU.add))
                    link(dve.tensor_scalar(gdec[:, :, :], g2[:, :, :], 0.0, None, ALU.max))
                    dve.scalar_tensor_tensor(out=g1[:, :, :], in0=gdec[:, :, :], scalar=2.0, in1=g2[:, :, :],
                                             op0=ALU.mult, op1=ALU.subtract).then_inc(ba_ready, 1)
                    e.wait_ge(exp1, 2)
                    link(dve.tensor_scalar(g2[:, :, :], g2[:, :, :], 1.0, None, ALU.add))
                    link(dve.reciprocal(beta[:, :, :], g2[:, :, :]))
                    link(dve.tensor_tensor(gdec[:, :, :], gdec[:, :, :], g1[:, :, :], ALU.add))
                    link(dve.scalar_tensor_tensor(out=gdec[:, :, :], in0=gdec[:, :, :], scalar=-1.0,
                                                  in1=mid(alog[:, :], NT), op0=ALU.mult, op1=ALU.mult))
                    link(dve.tensor_scalar(gdec[:, PT, :], gdec[:, PT, :], C("valid")[:, PT:PT + 1], None,
                                           ALU.mult))
                    dve.tensor_tensor(gseq[:, :, :], bc(C("seqmask"), H), mid(gdec[:, PT, :], NSEQ), ALU.mult
                                      ).then_inc(g_ready, 1)
                    e.wait_ge(gates_done, 2)
                    dve.tensor_tensor(edec[:, :, :], pd[:, 64:64 + NT * H].rearrange("p (t h) -> p t h", h=H),
                                      ngc[:, :, :], ALU.add).then_inc(gates_done, 1)

                    def convolve(i):
                        for par in range(2):
                            c = 2 * i + par
                            e.wait_ge(proj_read[par], i + 1)
                            e.wait_ge(seg_ready[par], i + 1)
                            wait(e, conv_read, c)
                            for j in range(CW):
                                w = ccol[:, ds(c, 1), NSEQ * CH + j:NSEQ * CH + j + 1].rearrange("p a b -> p (a b)")
                                out = cv[:, 0:CFLAT]
                                if j == 0:
                                    ins = dve.tensor_scalar(out, raw[par][:, 0:CFLAT], w, None, ALU.mult)
                                else:
                                    ins = dve.scalar_tensor_tensor(out=out, in0=raw[par][:, j:CFLAT + j],
                                                                   scalar=w, in1=out, op0=ALU.mult, op1=ALU.add)
                                if j < CW - 1:
                                    ins.then_inc(taps, 1)
                                    e.wait_ge(taps, c * CH + j + 1)
                            ins.then_inc(conv_done, 1)
                    turns(e, NCONV // 2, convolve)
                    chain2 = [0]

                    def plink(ins):
                        chain2[0] += 1
                        ins.then_inc(poolc, 1)
                        e.wait_ge(poolc, chain2[0])
                    for g in range(G):
                        par = g % 2
                        e.wait_ge(proj_read[par], (NCONV + H) // 2 + g // 2 + 1)
                        e.wait_ge(seg_ready[par], NCONV // 2 + g // 2 + 1)
                        if g >= 2:
                            e.wait_ge(mixed, g - 1)
                        src, bufs = ub[par], [psA, psB]
                        for lv in range(g + 1):
                            sh, dst = 1 << lv, bufs[lv % 2]
                            lo = (2 << lv) - 1
                            plink(dve.tensor_tensor(dst[:, lo:], src[:, lo:], src[:, lo - sh:PRAW - sh], ALU.add))
                            src = dst
                        plink(dve.scalar_tensor_tensor(out=dif[par][:, PH:], in0=src[:, PH:], scalar=1.0 / (2 << g),
                                                       in1=ub[par][:, PH:], op0=ALU.mult, op1=ALU.subtract))
                        plink(dve.tensor_tensor(fix[:, :], src[:, PH:2 * PH], C("rc")[:, g * PH:(g + 1) * PH],
                                                ALU.mult))
                        dve.tensor_tensor(dif[par][:, PH:2 * PH], fix[:, :], ub[par][:, PH:2 * PH], ALU.subtract
                                          ).then_inc(dif_ready, 1)
                    e.wait_ge(tails_turned, 1)
                    dve.tensor_copy(tails[:, NCONV * P:], pj[1][0:NTAIL, 0:G * P]).then_inc(tails_ready, 1)

        with ExitStack() as c2:
            def mat(name):
                return sb(name, [P, H, P], ctx=c2)
            wout = sb("wout", [P, 2 * H, D], ctx=c2)
            wr = sb("wr", [P, KT, G + NE], ctx=c2)
            brt = sb("brt", [P, G + NE], ctx=c2)
            lng = sb("lng", [P, D], ctx=c2)
            lnb = sb("lnb", [P, D], ctx=c2)
            stage = sb("stage", [P, NCONV, P], ctx=c2)
            sq = sb("sq", [P, 2 * DA], ctx=c2)
            ssq, rn, osum, ro = (sb(n, [P, 2 * H], ctx=c2) for n in ("ssq", "rn", "osum", "ro"))
            sc = sb("sc", [P, 4, H], ctx=c2)
            kh, kb, kbg, kd, qh, qg, vb = (mat(n) for n in ("kh", "kb", "kbg", "kd", "qh", "qg", "vb"))
            khT, kbT, qhT, qgT = (mat(n) for n in ("khT", "kbT", "qhT", "qgT"))
            gtri, dT, aT, qk, X, XT, Y = (mat(n) for n in ("gtri", "dT", "aT", "qk", "X", "XT", "Y"))
            nwT, st, vn, on, yaT, ybt = (mat(n) for n in ("nwT", "st", "vn", "on", "yaT", "ybt"))
            xt = sb("xt", [P, D], ctx=c2)
            h = sb("h", [P, D], ctx=c2)
            hT = sb("hT", [P, KT, P], ctx=c2)
            stats = sb("stats", [P, 2, 6], ctx=c2)
            mv = sb("mv", [P, 2], ctx=c2)
            rstd = sb("rstd", [P, 1], ctx=c2)
            spare = sb("spare", [P, 1], ctx=c2)
            late = qkvT[:, :, 0:SEQ]
            DIAG = NSEQ * (NS + DSEQ)
            st_s = late[:, 0:H, :].rearrange("p h (s e) -> p h s e", e=P)
            nwD, qgD = late[:, H:2 * H, 0:DIAG], late[:, 2 * H:3 * H, 0:DIAG]
            vseq = hT[0:NS, :, :]
            b = [pb(f"b{i}", [P, 512], c2) for i in range(8)]

            def heads(bank):
                return bank[:, :].rearrange("p (h d) -> p h d", d=P)

            S = phase(c2)
            LV = (2, 4, 8, 16, 32, 64)
            LV_S = (2, 4)
            wo_in, wr_in, ln_in = S("wo_in"), S("wr_in"), S("ln_in")
            stage_in, back_in = S("stage_in"), S("back_in")
            turned, sq_ready, ssq_ready, rn_ready = S("turned"), S("sq_ready"), S("ssq_ready"), S("rn_ready")
            scc, tok_ready, kk_ready = S("scc"), S("tok_ready"), S("kk_ready")
            gtri_ready, decay_sum, decay_ready = S("gtri_ready"), S("decay_sum"), S("decay_ready")
            turned2, ch_ready, qg_ready = S("turned2"), S("ch_ready"), S("qg_ready")
            ak_done, a_ready, m1c, xt_first, x_turned2 = S("ak_done"), S("a_ready"), S("m1c"), S("xt_first"), S("x_turned2")
            y_done = [S(f"y_done{l}") for l in LV]
            y_ready = [S(f"y_ready{l}") for l in LV]
            p_done = [S(f"p_done{l}") for l in LV]
            x_ready = [S(f"x_ready{l}") for l in LV]
            xt_ready = [S(f"xt_ready{l}") for l in LV]
            w_done, nw_ready, vn_done, vn_ready = S("w_done"), S("nw_ready"), S("vn_done"), S("vn_ready")
            o_done, sd_done, st_ready = S("o_done"), S("sd_done"), S("st_ready")
            osq_ready, osum1, osum_ready, ro_ready, on_ready = (S(n) for n in (
                "osq_ready", "osum1", "osum_ready", "ro_ready", "on_ready"))
            on_turned, ya_ready, mix_done = S("on_turned"), S("ya_ready"), S("mix_done")
            stat1, mv_ready, mv2, rstd_ready, norm_ready = (S(n) for n in (
                "stat1", "mv_ready", "mv2", "rstd_ready", "norm_ready"))
            hg, h_ready, h_out, h_turned, hT_ready = S("hg"), S("h_ready"), S("h_out"), S("h_turned"), S("hT_ready")
            lg_done, lg_ready, delta_out, sst_in = S("lg_done"), S("lg_ready"), S("delta_out"), S("sst_in")
            diag0, vseq_ready, ds_done, ds_ready, dsc = (S(n) for n in (
                "diag0", "vseq_ready", "ds_done", "ds_ready", "dsc"))

            def tiles(e, step):
                step(0, "prompt", False)
                with e.Fori(1, PT) as t:
                    step(t, "prompt", True)
                step(PT, "sample", True)
                step(NT, None, True)

            with nc.Block() as block:
                @block.sync
                def _(e):
                    sp.dma_start(wout[:, :, :], w_out_d[0].rearrange("(k p) n -> p k n", p=P)).then_inc(wo_in, 16)

                    def step(t, front, back):
                        if front:
                            wait(e, turned, t)
                            sp.dma_start(stage[:, :, :], qkvT[:, :, ds(t * P, P)]).then_inc(stage_in, 16)
                            if front == "sample":
                                e.wait_ge(stage_in, 16 * NT)
                                for s in range(NSEQ):
                                    sp.dma_start(st_s[:, :, s, :], sdelta_d[0, s].rearrange("h d e -> d h e")
                                                 ).then_inc(sst_in, 16)
                            wait(e, mix_done, t)
                            sp.dma_start(ybt[:, :, :], yb_d[:, :, ds(t * P, P)].rearrange("g p t -> p g t")
                                         ).then_inc(back_in, 16)
                            wait(e, norm_ready, t)
                            if front == "prompt":
                                sp.dma_start(xt[:, :], x_d[0, ds(t * P, P), :]).then_inc(back_in, 16)
                            else:
                                sp.dma_start(xt[0:NS, :], xs_d.rearrange("s t d -> (s t) d")).then_inc(back_in, 16)
                        if front == "sample":
                            e.wait_ge(st_ready, PT + 1)
                            sp.dma_start(dp_o[0, 0].rearrange("h d e -> d h e"), st[:, :, :]).then_inc(delta_out, 16)
                        if back:
                            e.wait_ge(h_ready, t)
                            sp.dma_start(h_d[ds(t * P - P, P), :], h[:, :]).then_inc(h_out, 16)
                    tiles(e, step)
                    for hh in range(H):
                        e.wait_ge(ds_ready, hh + 1)
                        sp.dma_start(dsm_o[0, :, hh].rearrange("s d e -> d s e"), st_s[:, hh, :, :]
                                     ).then_inc(delta_out, 16)
                    e.wait_ge(delta_out, 16 * (1 + H))
                    e.wait_ge(h_out, 16 * NT)

                @block.gpsimd
                def _(e):
                    e.dma_start(wr[:, :, 0:G], wrg_d[0].rearrange("(k p) n -> p k n", p=P)).then_inc(wr_in, 16)
                    e.dma_start(wr[:, :, G:], wre_d[0].rearrange("(k p) n -> p k n", p=P)).then_inc(wr_in, 16)
                    e.dma_start(brt[:, 0:G], brg_d.broadcast_to((P, G))).then_inc(wr_in, 16)
                    e.dma_start(brt[:, G:], bre_d.broadcast_to((P, NE))).then_inc(wr_in, 16)
                    e.dma_start(lng[:, :], ln1g_d.broadcast_to((P, D))).then_inc(ln_in, 16)
                    e.dma_start(lnb[:, :], ln1b_d.broadcast_to((P, D))).then_inc(ln_in, 16)
                    pool.memset(st[:, :, :], 0.0).then_inc(st_ready, 1)

                    def step(t, front, back):
                        n = t + 1
                        if front:
                            wait(e, decay_sum, t)
                            tri = C("tri") if front == "prompt" else C("tri_s")
                            g = gdec[:, ds(t, 1), :].rearrange("p a h -> p (a h)")
                            pool.tensor_tensor(gtri[:, :, :], mid(tri, H), bc(g, P), ALU.mult).then_inc(gtri_ready, 1)
                            e.wait_ge(ssq_ready, n)
                            pool.tensor_tensor(rn[:, :], ssq[:, :], mhalf[:, 0:2 * H], ALU.pow).then_inc(rn_ready, 1)
                            e.wait_ge(tok_ready, n)
                            eg = egc[:, ds(t, 1), :].rearrange("p a h -> p (a h)")
                            ed = edec[:, ds(t, 1), :].rearrange("p a h -> p (a h)")
                            wait(e, sd_done, t)
                            pool.tensor_tensor(kbg[:, :, :], kb[:, :, :], bc(eg, P), ALU.mult)
                            pool.tensor_tensor(kd[:, :, :], kh[:, :, :], bc(ed, P), ALU.mult).then_inc(kk_ready, 1)
                        if front == "sample":
                            e.wait_ge(stage_in, 16 * NT)
                            pool.memset(nwD, 0.0)
                            pool.memset(qgD, 0.0).then_inc(diag0, 1)
                        if back:
                            e.wait_ge(mv2, t)
                            pool.tensor_tensor(rstd[:, :], mv[:, 1:2], mhalf[:, 0:1], ALU.pow).then_inc(rstd_ready, 1)
                            e.wait_ge(ln_in, 32)
                            e.wait_ge(norm_ready, t)
                            pool.tensor_tensor(h[:, :], h[:, :], lng[:, :], ALU.mult).then_inc(hg, 1)
                            e.wait_ge(hg, t)
                            pool.tensor_tensor(h[:, :], h[:, :], lnb[:, :], ALU.add).then_inc(h_ready, 1)
                        if front:
                            e.wait_ge(osum_ready, n)
                            pool.tensor_tensor(ro[:, 0:H], osum[:, 0:H], mhalf[:, 0:H], ALU.pow).then_inc(ro_ready, 1)
                    tiles(e, step)

                @block.tensor
                def _(e):
                    def step(t, front, back):
                        n = t + 1
                        m = NS if front == "sample" else P

                        def mix(pieces):
                            for k in pieces:
                                src, kk = (ybt, k - H) if k >= H else (yaT, k)
                                for half in range(2):
                                    last = pe.matmul(b[6 + half][:, :], src[:, kk, :],
                                                     wout[:, k, half * 512:(half + 1) * 512],
                                                     start=(k == H), stop=(k == H - 1))
                            return last
                        if front:
                            e.wait_ge(stage_in, 16 * n)
                            for j in range(3):
                                for hh in range(H):
                                    last = pe.transpose(b[j][:, hh * P:(hh + 1) * P], stage[:, j * H + hh, :],
                                                        C("ident"))
                            last.then_inc(turned, 1)
                            e.wait_ge(gtri_ready, n)
                            neg = C("neg") if front == "prompt" else C("neg_s")
                            pe.matmul(b[4][:, :], C("ones"), gtri[:, :, :].rearrange("p h t -> p (h t)"),
                                      start=True, stop=False)
                            pe.matmul(heads(b[4]), C("ident"), mid(neg, H), start=False, stop=True
                                      ).then_inc(decay_sum, 1)
                        if back:
                            e.wait_ge(on_ready, t)
                            e.wait_ge(st_ready, t + 1 if front == "prompt" else PT + 1)
                            if front is None:
                                e.wait_ge(ds_ready, H)
                            for hh in range(H):
                                last = pe.transpose(b[3][:, hh * P:(hh + 1) * P], on[:, hh, :], C("ident"))
                            last.then_inc(on_turned, 1)
                            e.wait_ge(wo_in, 16)
                            e.wait_ge(back_in, 32 * t)
                            mix(range(H, 2 * H))
                            e.wait_ge(ya_ready, t)
                        rest = list(range(H)) if back else []
                        if front:
                            e.wait_ge(tok_ready, n)
                            for bank, src in ((b[0], kh), (b[1], kb), (b[2], qh), (b[5], qg)):
                                for hh in range(H):
                                    last = pe.transpose(bank[:, hh * P:(hh + 1) * P], src[:, hh, :], C("ident"))
                            last.then_inc(turned2, 1)
                            e.wait_ge(ch_ready, n)
                            for bank, src in ((b[0], kbT), (b[1], qhT)):
                                for hh in range(H):
                                    last = pe.matmul(bank[:, hh * P:(hh + 1) * P], khT[:, hh, :], src[:, hh, :],
                                                     start=True, stop=True)
                            last.then_inc(ak_done, 1)
                            e.wait_ge(xt_first, n)
                            for hh in range(H):
                                last = pe.transpose(b[2][:, hh * P:(hh + 1) * P], XT[:, hh, :], C("ident"))
                            last.then_inc(x_turned2, 1)
                            levels = LV if front == "prompt" else LV_S
                            for l in range(len(levels)):
                                e.wait_ge(x_ready[l], n)
                                for hh in range(H):
                                    last = pe.matmul(b[0][:, hh * P:(hh + 1) * P], aT[:, hh, :], X[:, hh, :],
                                                     start=True, stop=True)
                                last.then_inc(y_done[l], 1)
                                if rest:
                                    done = mix([rest.pop(0)])
                                    if not rest:
                                        done.then_inc(mix_done, 1)
                                e.wait_ge(y_ready[l], n)
                                if l > 0:
                                    e.wait_ge(xt_ready[l - 1], n)
                                if l < len(levels) - 1:
                                    for hh in range(H):
                                        pe.matmul(b[1][:, hh * P:(hh + 1) * P], XT[:, hh, :], Y[:, hh, :],
                                                  start=True, stop=True)
                                for hh in range(H):
                                    last = pe.matmul(b[2][:, hh * P:(hh + 1) * P], Y[:, hh, :], XT[:, hh, :],
                                                     start=True, stop=True)
                                last.then_inc(p_done[l], 1)
                        while rest:
                            done = mix([rest.pop(0)])
                            if not rest:
                                done.then_inc(mix_done, 1)
                        if front:
                            e.wait_ge(xt_ready[len(levels) - 1], n)
                            e.wait_ge(kk_ready, n)
                            for hh in range(H):
                                last = pe.matmul(b[3][:, hh * P:(hh + 1) * P], kbg[:, hh, :], XT[:, hh, :],
                                                 start=True, stop=True)
                            last.then_inc(w_done, 1)
                            e.wait_ge(nw_ready, n)
                        if front == "prompt":
                            e.wait_ge(st_ready, n)
                            for hh in range(H):
                                c = slice(hh * P, (hh + 1) * P)
                                pe.matmul(b[4][:, c], XT[:, hh, :], vb[:, hh, :], start=True, stop=False)
                                last = pe.matmul(b[4][:, c], nwT[:, hh, :], st[:, hh, :], start=False, stop=True)
                            last.then_inc(vn_done, 1)
                            e.wait_ge(vn_ready, n)
                            e.wait_ge(qg_ready, n)
                            for hh in range(H):
                                c = slice(hh * P, (hh + 1) * P)
                                pe.matmul(b[5][:, c], qgT[:, hh, :], st[:, hh, :], start=True, stop=False)
                                last = pe.matmul(b[5][:, c], qk[:, hh, :], vn[:, hh, :], start=False, stop=True)
                            last.then_inc(o_done, 1)
                            for hh in range(H):
                                last = pe.matmul(b[3][:, hh * P:(hh + 1) * P], kd[:, hh, :], vn[:, hh, :],
                                                 start=True, stop=True)
                            last.then_inc(sd_done, 1)
                        if front == "sample":
                            e.wait_ge(sst_in, 16 * NSEQ)
                            for hh in range(H):
                                c = slice(hh * P, (hh + 1) * P)
                                pe.matmul(b[4][0:m, c], XT[:, hh, 0:m], vb[:, hh, :], start=True, stop=False)
                                for s in range(NSEQ):
                                    last = pe.matmul(b[4][0:m, c], nwD[:, hh, s * NS:(s + 1) * NS],
                                                     st_s[:, hh, s, :], start=False, stop=(s == NSEQ - 1))
                            last.then_inc(vn_done, 1)
                            e.wait_ge(vn_ready, n)
                            e.wait_ge(qg_ready, n)
                            for hh in range(H):
                                c = slice(hh * P, (hh + 1) * P)
                                pe.matmul(b[5][0:m, c], qk[0:m, hh, 0:m], vn[0:m, hh, :], start=True, stop=False)
                                for s in range(NSEQ):
                                    last = pe.matmul(b[5][0:m, c], qgD[:, hh, s * NS:(s + 1) * NS],
                                                     st_s[:, hh, s, :], start=False, stop=(s == NSEQ - 1))
                            last.then_inc(o_done, 1)
                        if back:
                            e.wait_ge(h_ready, t)
                            for k in range(KT):
                                bank, at = b[6 + k // H], (k % H) * P
                                last = pe.transpose(bank[:, at:at + P], h[:, k * P:(k + 1) * P], C("ident"))
                            last.then_inc(h_turned, 1)
                            e.wait_ge(hT_ready, t)
                            e.wait_ge(wr_in, 64)
                            for k in range(KT):
                                last = pe.matmul(b[4][:, 0:G + NE], hT[:, k, :], wr[:, k, :],
                                                 start=(k == 0), stop=(k == KT - 1))
                            last.then_inc(lg_done, 1)
                            e.wait_ge(lg_ready, t)
                        if front == "sample":
                            for hh in range(H):
                                e.wait_ge(vseq_ready, hh + 1)
                                for half in range(2):
                                    last = pe.matmul(b[half][:, :], kd[0:m, hh, :],
                                                     vseq[:, half * H:(half + 1) * H, :].rearrange("p s e -> p (s e)"),
                                                     start=True, stop=True)
                                last.then_inc(ds_done, 1)
                                e.wait_ge(ds_ready, hh + 1)
                    tiles(e, step)

                @block.scalar
                def _(e):
                    def flat(a):
                        return a[:, :, :].rearrange("p h d -> p (h d)")

                    def step(t, front, back):
                        n = t + 1
                        if front:
                            e.wait_ge(turned, n)
                            if back:
                                e.wait_ge(osum_ready, t)
                            act.activation(sq[:, 0:DA], b[0][:, :], ACT.Square)
                            act.activation(sq[:, DA:], b[1][:, :], ACT.Square).then_inc(sq_ready, 1)
                            e.wait_ge(decay_sum, n)
                            for hh in range(H):
                                bias = ngc[:, ds(t, 1), hh:hh + 1].rearrange("p a h -> p (a h)")
                                last = act.activation(dT[:, hh, :], b[4][:, hh * P:(hh + 1) * P], ACT.Exp, bias=bias)
                            last.then_inc(decay_ready, 1)
                            e.wait_ge(turned2, n)
                            act.activation(flat(khT), b[0][:, :], ACT.Copy)
                            act.activation(flat(kbT), b[1][:, :], ACT.Copy)
                            act.activation(flat(qhT), b[2][:, :], ACT.Copy).then_inc(ch_ready, 1)
                            if front == "prompt":
                                act.activation(flat(qgT), b[5][:, :], ACT.Copy).then_inc(qg_ready, 1)
                            else:
                                e.wait_ge(diag0, 1)
                                for hh in range(H):
                                    last = act.activation(
                                        qgD[:, hh, :].rearrange("p (s c) -> p s c", c=NS + DSEQ)[:, :, 0:DSEQ],
                                        b[5][:, hh * P:hh * P + NS].rearrange("p (s r) -> p s r", r=DSEQ), ACT.Copy)
                                last.then_inc(qg_ready, 1)
                            e.wait_ge(x_turned2, n)
                            act.activation(flat(X), b[2][:, :], ACT.Copy).then_inc(x_ready[0], 1)
                            e.wait_ge(w_done, n)
                            if front == "prompt":
                                act.activation(flat(nwT), b[3][:, :], ACT.Copy, scale=-1.0).then_inc(nw_ready, 1)
                            else:
                                for hh in range(H):
                                    last = act.activation(
                                        nwD[:, hh, :].rearrange("p (s c) -> p s c", c=NS + DSEQ)[:, :, 0:DSEQ],
                                        b[3][:, hh * P:hh * P + NS].rearrange("p (s r) -> p s r", r=DSEQ), ACT.Copy,
                                        scale=-1.0)
                                last.then_inc(nw_ready, 1)
                            m = P if front == "prompt" else NS
                            e.wait_ge(vn_done, n)
                            act.activation(flat(vn)[0:m], b[4][0:m, :], ACT.Copy).then_inc(vn_ready, 1)
                            e.wait_ge(o_done, n)
                            act.activation(sq[0:m, 0:DA], b[5][0:m, :], ACT.Square).then_inc(osq_ready, 1)
                        if back:
                            e.wait_ge(h_turned, t)
                            act.activation(hT[:, 0:H, :].rearrange("p k t -> p (k t)"), b[6][:, :], ACT.Copy)
                            act.activation(hT[:, H:, :].rearrange("p k t -> p (k t)"), b[7][:, :], ACT.Copy
                                           ).then_inc(hT_ready, 1)
                    tiles(e, step)

                @block.vector
                def _(e):
                    def col(a, t):
                        return a[:, ds(t, 1), :].rearrange("p a h -> p (a h)")

                    def step(t, front, back):
                        n = t + 1
                        u = t - 1
                        if back:
                            e.wait_ge(on_turned, t)
                            dve.scalar_tensor_tensor(out=yaT[:, :, :], in0=heads(b[3]), scalar=gnw[:, :],
                                                     in1=szT[:, :, ds(u * P, P)], op0=ALU.mult, op1=ALU.mult
                                                     ).then_inc(ya_ready, 1)
                        if front:
                            e.wait_ge(sq_ready, n)
                            dve.tensor_reduce(ssq[:, :], sq[:, :].rearrange("p (h d) -> p h d", d=P), AX.X, ALU.add
                                              ).then_inc(scc, 1)
                            e.wait_ge(scc, 3 * t + 1)
                            dve.tensor_scalar(ssq[:, :], ssq[:, :], L2_EPS, None, ALU.add).then_inc(ssq_ready, 1)
                            e.wait_ge(rn_ready, n)
                            dve.tensor_scalar(sc[:, 0, :], rn[:, 0:H], HD ** -0.5, None, ALU.mult).then_inc(scc, 1)
                            dve.tensor_tensor(sc[:, 2, :], rn[:, H:], col(beta, t), ALU.mult)
                            e.wait_ge(scc, 3 * t + 2)
                            dve.tensor_tensor(sc[:, 1, :], sc[:, 0, :], col(egc, t), ALU.mult).then_inc(scc, 1)
                            dve.tensor_tensor(kh[:, :, :], heads(b[1]), bc(rn[:, H:], P), ALU.mult)
                            dve.tensor_tensor(qh[:, :, :], heads(b[0]), bc(sc[:, 0, :], P), ALU.mult)
                            e.wait_ge(scc, 3 * t + 3)
                            dve.tensor_tensor(kb[:, :, :], heads(b[1]), bc(sc[:, 2, :], P), ALU.mult)
                            dve.tensor_tensor(qg[:, :, :], heads(b[0]), bc(sc[:, 1, :], P), ALU.mult)
                            dve.tensor_tensor(vb[:, :, :], heads(b[2]), bc(col(beta, t), P), ALU.mult
                                              ).then_inc(tok_ready, 1)
                            e.wait_ge(ak_done, n)
                            e.wait_ge(decay_ready, n)
                            dve.tensor_tensor(aT[:, :, :], heads(b[0]), dT[:, :, :], ALU.mult).then_inc(a_ready, 1)
                            dve.tensor_tensor(qk[:, :, :], heads(b[1]), dT[:, :, :], ALU.mult)
                            e.wait_ge(a_ready, n)
                            dve.tensor_tensor(Y[:, :, :], aT[:, :, :], mid(C("m1t"), H), ALU.mult).then_inc(m1c, 1)
                            e.wait_ge(m1c, n)
                            dve.tensor_tensor(XT[:, :, :], mid(C("ident"), H), Y[:, :, :], ALU.subtract
                                              ).then_inc(xt_first, 1)
                            levels = LV if front == "prompt" else LV_S
                            for l, size in enumerate(levels):
                                e.wait_ge(y_done[l], n)
                                dve.tensor_tensor(Y[:, :, :], heads(b[0]), mid(C(f"m{size}"), H), ALU.mult
                                                  ).then_inc(y_ready[l], 1)
                                e.wait_ge(p_done[l], n)
                                if l < len(levels) - 1:
                                    dve.tensor_tensor(X[:, :, :], X[:, :, :], heads(b[1]), ALU.subtract
                                                      ).then_inc(x_ready[l + 1], 1)
                                dve.tensor_tensor(XT[:, :, :], XT[:, :, :], heads(b[2]), ALU.subtract
                                                  ).then_inc(xt_ready[l], 1)
                        if back:
                            e.wait_ge(mix_done, t)
                            for half in range(2):
                                c = slice(half * 512, (half + 1) * 512)
                                last = dve.scalar_tensor_tensor(out=xt[:, c], in0=xt[:, c], scalar=ALPHA,
                                                                in1=b[6 + half][:, :], op0=ALU.mult, op1=ALU.add)
                                last.then_inc(stat1, 1)
                            for half in range(2):
                                e.wait_ge(stat1, 3 * t - 2 + half)
                                last = dve.bn_stats(stats[:, half, :], xt[:, half * 512:(half + 1) * 512])
                            last.then_inc(stat1, 1)
                            e.wait_ge(stat1, 3 * t)
                            dve.memset(spare[:, :], 0.0)
                            dve.bn_aggr(mv[:, :], stats[:, :, :].rearrange("p a b -> p (a b)")).then_inc(mv_ready, 1)
                            e.wait_ge(mv_ready, t)
                            dve.tensor_scalar(mv[:, 1:2], mv[:, 1:2], LN_EPS, None, ALU.add).then_inc(mv2, 1)
                            e.wait_ge(rstd_ready, t)
                            dve.tensor_scalar(h[:, :], xt[:, :], mv[:, 0:1], rstd[:, :], ALU.subtract, ALU.mult
                                              ).then_inc(norm_ready, 1)
                        if front:
                            m = P if front == "prompt" else NS
                            if front == "prompt":
                                e.wait_ge(sd_done, n)
                                for hh in range(H):
                                    last = dve.scalar_tensor_tensor(
                                        out=st[:, hh, :], in0=st[:, hh, :],
                                        scalar=eglast[:, ds(t, 1), hh:hh + 1].rearrange("p a h -> p (a h)"),
                                        in1=b[3][:, hh * P:(hh + 1) * P], op0=ALU.mult, op1=ALU.add)
                                last.then_inc(st_ready, 1)
                            e.wait_ge(osq_ready, n)
                            dve.tensor_reduce(osum[0:m, 0:H], sq[0:m, 0:DA].rearrange("p (h d) -> p h d", d=P), AX.X,
                                              ALU.add).then_inc(osum1, 1)
                            e.wait_ge(osum1, n)
                            dve.tensor_scalar(osum[0:m, 0:H], osum[0:m, 0:H], 1.0 / HD, RMS_EPS, ALU.mult, ALU.add
                                              ).then_inc(osum_ready, 1)
                            e.wait_ge(ro_ready, n)
                            dve.tensor_tensor(on[0:m], heads(b[5])[0:m], bc(ro[0:m, 0:H], P), ALU.mult
                                              ).then_inc(on_ready, 1)
                        if back:
                            e.wait_ge(lg_done, t)
                            dve.tensor_tensor(col(logits, u), b[4][:, 0:G + NE], brt[:, :], ALU.add
                                              ).then_inc(lg_ready, 1)
                            e.wait_ge(h_out, 16 * t)
                        if front == "sample":
                            for hh in range(H):
                                dve.tensor_tensor(vseq, mid(vn[0:NS, hh, :], NSEQ), bc(C("seqmask")[0:NS], P),
                                                  ALU.mult).then_inc(vseq_ready, 1)
                                eg = eglast_s[:, :, hh:hh + 1].rearrange("p s h -> p (s h)")
                                if hh == 0:
                                    e.wait_ge(o_done, NT)
                                dve.tensor_tensor(st_s[:, hh], st_s[:, hh], bc(eg, P), ALU.mult).then_inc(dsc, 1)
                                e.wait_ge(ds_done, hh + 1)
                                e.wait_ge(dsc, hh + 1)
                                for half in range(2):
                                    c = slice(half * H, (half + 1) * H)
                                    last = dve.tensor_tensor(st_s[:, hh, c, :], st_s[:, hh, c, :], heads(b[half]),
                                                             ALU.add)
                                last.then_inc(ds_ready, 1)
                    tiles(e, step)

        order = sb("order", [1, NTILES, 2], I32)
        pairs = sb("pairs", [1, 1], I32)
        wgu = [sb(f"wgu{i}", [P, KT, 2 * FE]) for i in range(2)]
        wdn = [sb(f"wdn{i}", [P, FE // P, D]) for i in range(2)]
        kept = phase(whole)
        gu_in, dn_in = ([kept(f"{n}{i}") for i in range(2)] for n in ("gu_in", "dn_in"))
        wgu_v = [w[0].rearrange("g n (k p) f -> (g n) p k f", p=P) for w in (wg_d, wu_d)]
        wdn_v = wd_d[0].rearrange("g n (k p) f -> (g n) p k f", p=P)

        def load_gu(k, expert):
            for j in range(2):
                sp.dma_start(wgu[k][:, :, j * FE:(j + 1) * FE],
                             wgu_v[j][ds(expert, 1)].rearrange("a p k f -> (a p) k f")).then_inc(gu_in[k], 16)

        def load_dn(k, expert):
            sp.dma_start(wdn[k][:, :, :], wdn_v[ds(expert, 1)].rearrange("a p k f -> (a p) k f")
                         ).then_inc(dn_in[k], 16)

        with ExitStack() as c3:
            def tmp(name, shape, dt=F32):
                return sb(name, shape, dt, ctx=c3)
            NG = [P, NT, G]
            mx, sm, pg, dl, ex = (tmp(n, [P, NT]) for n in ("mx", "sm", "pg", "dl", "ex"))
            ga, gb, ohg = tmp("ga", NG), tmp("gb", NG), tmp("ohg", NG)
            lem = tmp("lem", [P, NT, G, EPG])
            les, ea, oh1, oh2 = (tmp(n, [P, NT, EPG]) for n in ("les", "ea", "oh1", "oh2"))
            pick = [tmp(f"pick{k}", [P, NT, NE]) for k in range(2)]
            both, pos, work = (tmp(n, [P, NT, NE]) for n in ("both", "pos", "work"))
            base = tmp("base", [P, NT + 1, NE])
            slotf = tmp("slotf", [P, 2, NT])
            sloti = tmp("sloti", [P, 2, NT], I32)
            entry = tmp("entry", [P, 2, NT, 4], I32)
            nov, cuma, cumb = (tmp(n, [P, NE]) for n in ("nov", "cuma", "cumb"))
            cmpm = tmp("cmpm", [P, MAXOV, NE])
            ove, ovs = tmp("ove", [P, MAXOV]), tmp("ovs", [P, MAXOV])
            par1 = tmp("par1", [P, MAXOV // 2])
            par2 = tmp("par2", [P, 1])
            empty = tmp("empty", [P, NLIST * SLOTS // P, 4], I32)
            pp = pb("pp", [P, NT * NE], c3)
            pt = pb("pt", [P, NT * NE], c3)
            S = phase(c3)
            chn, filled, emptied = S("chn"), S("filled"), S("emptied")
            ga_ready, ex_ready, dl_ready, eex_ready = S("ga_ready"), S("ex_ready"), S("dl_ready"), S("eex_ready")
            both_ready, counted, entries_ready, listed = S("both_ready"), S("counted"), S("entries_ready"), S("listed")

            with nc.Block() as block:
                @block.sync
                def _(e):
                    e.wait_ge(filled, 2)
                    sp.dma_start(tab_d.rearrange("(p n) c -> p (n c)", p=P),
                                 empty[:, :, :].rearrange("p n c -> p (n c)")).then_inc(emptied, 16)
                    for k in range(2):
                        load_gu(k, k)
                        load_dn(k, k)
                    e.wait_ge(emptied, 16)

                @block.gpsimd
                def _(e):
                    pool.memset(empty[:, :, 0:2], SKIP).then_inc(filled, 1)
                    pool.memset(empty[:, :, 2:4], 0).then_inc(filled, 1)
                    e.wait_ge(emptied, 16)
                    e.wait_ge(entries_ready, 4)
                    for t in range(NT):
                        for k in range(2):
                            pool.indirect_dma_start(tab_d, bass.IndirectOffsetOnAxis(ap=sloti[:, k, t:t + 1], axis=0),
                                                    entry[:, k, t, :], None, bounds_check=NLIST * SLOTS - 1,
                                                    oob_is_err=False).then_inc(listed, 16)
                    e.wait_ge(listed, 16 * 2 * NT)

                @block.tensor
                def _(e):
                    e.wait_ge(both_ready, 1)
                    flat = both[:, :, :].rearrange("p t n -> p (t n)")
                    pe.matmul(pp[:, :], C("strict"), flat, start=True, stop=True)
                    pe.matmul(pt[:, :], C("ones"), flat, start=True, stop=True).then_inc(counted, 1)

                @block.scalar
                def _(e):
                    e.wait_ge(ga_ready, 1)
                    act.activation(gb[:, :, :], ga[:, :, :], ACT.Exp).then_inc(ex_ready, 1)
                    e.wait_ge(dl_ready, 1)
                    act.activation(ex[:, :], dl[:, :], ACT.Exp).then_inc(eex_ready, 1)

                @block.vector
                def _(e):
                    chain = [0]

                    def link(ins):
                        chain[0] += 1
                        ins.then_inc(chn, 1)
                        e.wait_ge(chn, chain[0])

                    def wide(a, m):
                        return mid(a, NT)

                    def first_max(values, n, top, scratch, onehot):
                        link(dve.tensor_reduce(top, values, AX.X, ALU.max))
                        link(dve.tensor_tensor(scratch, values, bc(top, n), ALU.is_equal))
                        link(dve.tensor_tensor(scratch, scratch, mid(C(f"w{n}"), NT), ALU.mult))
                        link(dve.tensor_reduce(sm[:, :], scratch, AX.X, ALU.max))
                        link(dve.tensor_tensor(onehot, scratch, bc(sm[:, :], n), ALU.is_equal))

                    lg = logits[:, :, 0:G]
                    first_max(lg, G, mx[:, :], ga[:, :, :], ohg[:, :, :])
                    dve.tensor_tensor(ga[:, :, :], lg, bc(mx[:, :], G), ALU.subtract).then_inc(ga_ready, 1)
                    e.wait_ge(ex_ready, 1)
                    link(dve.tensor_reduce(pg[:, :], gb[:, :, :], AX.X, ALU.add))
                    link(dve.reciprocal(pg[:, :], pg[:, :]))
                    le = logits[:, :, G:].rearrange("p t (g n) -> p t g n", n=EPG)
                    for t in range(NT):
                        last = dve.tensor_tensor(lem[:, t], le[:, t], bc(ohg[:, t, :], EPG), ALU.mult)
                    link(last)
                    link(dve.tensor_tensor(les[:, :, :], lem[:, :, 0, :], lem[:, :, 1, :], ALU.add))
                    link(dve.tensor_tensor(les[:, :, :], les[:, :, :], lem[:, :, 2, :], ALU.add))
                    link(dve.tensor_tensor(les[:, :, :], les[:, :, :], lem[:, :, 3, :], ALU.add))
                    first_max(les[:, :, :], EPG, mx[:, :], ea[:, :, :], oh1[:, :, :])
                    link(dve.tensor_copy(dl[:, :], mx[:, :]))
                    link(dve.scalar_tensor_tensor(out=les[:, :, :], in0=oh1[:, :, :], scalar=NEG, in1=les[:, :, :],
                                                  op0=ALU.mult, op1=ALU.add))
                    first_max(les[:, :, :], EPG, mx[:, :], ea[:, :, :], oh2[:, :, :])
                    dve.tensor_tensor(dl[:, :], mx[:, :], dl[:, :], ALU.subtract).then_inc(dl_ready, 1)
                    for k, oh in enumerate((oh1, oh2)):
                        for t in range(NT):
                            p4 = pick[k][:, t, :].rearrange("p (g n) -> p g n", n=EPG)
                            last = dve.tensor_tensor(p4, bc(ohg[:, t, :], EPG), mid(oh[:, t, :], G), ALU.mult)
                    link(last)
                    for k in range(2):
                        last = dve.tensor_scalar(pick[k][:, PT, :], pick[k][:, PT, :], C("valid")[:, PT:PT + 1], None,
                                                 ALU.mult)
                    link(last)
                    dve.tensor_tensor(both[:, :, :], pick[0][:, :, :], pick[1][:, :, :], ALU.add
                                      ).then_inc(both_ready, 1)
                    e.wait_ge(eex_ready, 1)
                    link(dve.tensor_scalar(sm[:, :], ex[:, :], 1.0, None, ALU.add))
                    link(dve.reciprocal(sm[:, :], sm[:, :]))
                    link(dve.tensor_tensor(sm[:, :], sm[:, :], pg[:, :], ALU.mult))
                    dve.tensor_copy(entry[:, 0, :, 2].bitcast(F32), sm[:, :])
                    dve.tensor_tensor(entry[:, 1, :, 2].bitcast(F32), sm[:, :], ex[:, :], ALU.mult
                                      ).then_inc(entries_ready, 1)
                    for k in range(2):
                        dve.tensor_copy(entry[:, k, :, 3], C("token"))
                        dve.tensor_copy(entry[:, k, :, 1], C("token"))
                        last = dve.tensor_scalar(entry[:, k, :, 0], C("token"), 2.0, float(k), ALU.mult, ALU.add)
                    last.then_inc(entries_ready, 1)
                    e.wait_ge(counted, 1)
                    tot = pt[:, :].rearrange("p (t n) -> p t n", n=NE)
                    link(dve.memset(base[:, 0, :], 0.0))
                    for t in range(NT):
                        link(dve.tensor_tensor(base[:, t + 1, :], base[:, t, :], tot[:, t, :], ALU.add))
                    link(dve.tensor_tensor(pos[:, :, :], base[:, 0:NT, :],
                                           pp[:, :].rearrange("p (t n) -> p t n", n=NE), ALU.add))
                    link(dve.tensor_tensor(pos[:, :, :], pos[:, :, :], mid(C("slot0"), NT), ALU.add))
                    for k in range(2):
                        link(dve.tensor_tensor(work[:, :, :], pick[k][:, :, :], pos[:, :, :], ALU.mult))
                        link(dve.tensor_reduce(slotf[:, k, :], work[:, :, :], AX.X, ALU.add))
                        link(dve.tensor_tensor(slotf[:, k, :], slotf[:, k, :], C("skip"), ALU.add))
                    dve.tensor_copy(sloti[:, :, :], slotf[:, :, :]).then_inc(entries_ready, 2)

                    cnt = base[:, NT, :]
                    link(dve.memset(nov[:, :], 0.0))
                    for j in range(1, NT):
                        link(dve.scalar_tensor_tensor(out=nov[:, :], in0=cnt, scalar=float(j * P), in1=nov[:, :],
                                                      op0=ALU.is_gt, op1=ALU.add))
                    src, dst = cuma, cumb
                    link(dve.tensor_copy(src[:, :], nov[:, :]))
                    for sh in (1, 2, 4, 8, 16):
                        dve.tensor_copy(dst[:, 0:sh], src[:, 0:sh])
                        link(dve.tensor_tensor(dst[:, sh:], src[:, sh:], src[:, 0:NE - sh], ALU.add))
                        src, dst = dst, src
                    link(dve.tensor_tensor(cmpm[:, :, :], mid(src[:, :], MAXOV), bc(C("rank"), NE), ALU.is_le))
                    link(dve.tensor_reduce(ove[:, :], cmpm[:, :, :], AX.X, ALU.add))
                    link(dve.tensor_tensor(cmpm[:, :, :], cmpm[:, :, :], mid(nov[:, :], MAXOV), ALU.mult))
                    link(dve.tensor_reduce(ovs[:, :], cmpm[:, :, :], AX.X, ALU.add))
                    link(dve.tensor_tensor(ovs[:, :], C("rank"), ovs[:, :], ALU.subtract))
                    link(dve.tensor_scalar(ovs[:, :], ovs[:, :], float(P), float(P), ALU.mult, ALU.add))
                    link(dve.scalar_tensor_tensor(out=ovs[:, :], in0=ove[:, :], scalar=float(SLOTS), in1=ovs[:, :],
                                                  op0=ALU.mult, op1=ALU.add))
                    link(dve.tensor_scalar(ovs[:, :], ovs[:, :], float(NE * SLOTS), None, ALU.min))
                    link(dve.tensor_scalar(ove[:, :], ove[:, :], float(NE - 1), None, ALU.min))
                    dve.tensor_copy(order[0:1, NE:, 0], ove[0:1, :])
                    dve.tensor_copy(order[0:1, NE:, 1], ovs[0:1, :])
                    dve.tensor_copy(order[0:1, 0:NE, 1], C("slot0")[0:1, :])
                    link(dve.tensor_scalar(order[0:1, 0:NE, 0], C("slot0")[0:1, :], 1.0 / SLOTS, 0.25, ALU.mult,
                                           ALU.add))
                    link(dve.tensor_tensor(par1[:, :], src[:, NE - 1:NE].broadcast_to((P, MAXOV // 2)), C("even"),
                                           ALU.is_gt))
                    link(dve.tensor_reduce(par2[:, :], par1[:, :], AX.X, ALU.add))
                    link(dve.tensor_scalar(pairs[0:1, :], par2[0:1, :], float(NE // 2 - 1), None, ALU.add))

        with ExitStack() as c4:
            pr = range(2)

            def two(name, shape, dt=F32):
                return [sb(f"{name}{k}", shape, dt, ctx=c4) for k in pr]
            idg, ids = two("idg", [P, 4], I32), two("ids", [P, 4], I32)
            xg, xgT = two("xg", [P, D]), two("xgT", [P, KT, P])
            sg, ac, acT = two("sg", [P, FE]), two("ac", [P, FE]), two("acT", [P, FE // P, P])
            yo = two("yo", [P, D])
            spare = sb("spare4", [P, 4], ctx=c4)
            b = [pb(f"e{i}", [P, 512], c4) for i in range(8)]
            S = phase(c4)
            S2 = lambda n: [S(f"{n}{i}") for i in pr]
            idg_in, ids_in, gathered, cleared = S2("idg_in"), S2("ids_in"), S2("gathered"), S("cleared")
            xg_turned, xgT_ready, gu_done, silu_ready = S2("xg_turned"), S2("xgT_ready"), S2("gu_done"), S2("silu_ready")
            ac_ready, ac_turned, acT_ready, dn_done = S2("ac_ready"), S2("ac_turned"), S2("acT_ready"), S2("dn_done")
            yo_ready, scattered, carried = S2("yo_ready"), S2("scattered"), S("carried")

            def pair_loop(e, head, body, tail=None):
                last = e.value_load(pairs[0:1, 0:1], min_val=NE // 2 - 1, max_val=(NTILES - 2) // 2 - 1)
                head()
                body(1)
                with e.Fori(2, last + 1) as i:
                    body(i)
                if tail:
                    tail(last)

            def tile_entry(e, i, k, field, top):
                return e.value_load(order[0:1, ds(2 * i + k, 1), field], min_val=0, max_val=top)

            with nc.Block() as block:
                @block.sync
                def _(e):
                    def load_ids(i, k):
                        row = tile_entry(e, i, k, 1, NE * SLOTS)
                        wait(e, scattered[k], 16 * i)
                        sp.dma_start(ids[k][:, :], tab_d[ds(row, P), :]).then_inc(ids_in[k], 16)

                    def head():
                        load_ids(0, 0)
                        load_ids(0, 1)
                        e.wait_ge(gu_done[0], 1)
                        load_gu(0, tile_entry(e, 1, 0, 0, NE - 1))

                    def body(i):
                        first, second, third = (tile_entry(e, i, 1, 0, NE - 1), tile_entry(e, i, 0, 0, NE - 1),
                                                tile_entry(e, i + 1, 0, 0, NE - 1))
                        e.wait_ge(gu_done[1], i)
                        load_gu(1, first)
                        e.wait_ge(dn_done[0], i)
                        load_dn(0, second)
                        load_ids(i, 0)
                        e.wait_ge(gu_done[0], i + 1)
                        load_gu(0, third)
                        e.wait_ge(dn_done[1], i)
                        load_dn(1, first)
                        load_ids(i, 1)
                    pair_loop(e, head, body)

                @block.gpsimd
                def _(e):
                    for k in pr:
                        pool.memset(xg[k][:, :], 0.0).then_inc(cleared, 1)
                    e.wait_ge(cleared, 2)

                    def carry_wait(c):
                        pool.tensor_tensor(spare[:, c:c + 1], mhalf[:, 0:1], mhalf[:, 0:1], ALU.mult).then_inc(carried, 1)

                    def gather(i, k):
                        e.wait_ge(idg_in[k], 16 * i + 16)
                        wait(e, xg_turned[k], i)
                        carry_wait(k)
                        pool.indirect_dma_start(xg[k][:, :], None, h_d,
                                                bass.IndirectOffsetOnAxis(ap=idg[k][:, 1:2], axis=0),
                                                bounds_check=TP - 1, oob_is_err=False).then_inc(gathered[k], 16)

                    def scatter(i, k):
                        e.wait_ge(yo_ready[k], 2 * i + 2)
                        carry_wait(2 + k)
                        pool.indirect_dma_start(y2_d, bass.IndirectOffsetOnAxis(ap=ids[k][:, 0:1], axis=0),
                                                yo[k][:, :], None, bounds_check=2 * TP - 1, oob_is_err=False
                                                ).then_inc(scattered[k], 16)

                    def head():
                        gather(0, 0)
                        gather(0, 1)
                        e.wait_ge(carried, 2)
                        gather(1, 0)
                        gather(1, 1)

                    def body(i):
                        e.wait_ge(carried, 4 * i)
                        gather(i + 1, 0)
                        scatter(i - 1, 0)
                        gather(i + 1, 1)
                        scatter(i - 1, 1)

                    def tail(m):
                        e.wait_ge(carried, 4 * m + 4)
                        scatter(m, 0)
                        scatter(m, 1)
                        for k in pr:
                            e.wait_ge(scattered[k], 16 * m + 16)
                            e.wait_ge(gathered[k], 16 * m + 32)
                    pair_loop(e, head, body, tail)

                @block.tensor
                def _(e):
                    def turn_x(i, k):
                        e.wait_ge(gathered[k], 16 * i + 16)
                        wait(e, xgT_ready[1 - k], 2 * i if k == 0 else 2 * i + 2)
                        for c in range(KT):
                            bank, at = b[c // H], (c % H) * P
                            last = pe.transpose(bank[:, at:at + P], xg[k][:, c * P:(c + 1) * P], C("ident"))
                        last.then_inc(xg_turned[k], 1)

                    def gate_up(i, k):
                        e.wait_ge(xgT_ready[k], 2 * i + 2)
                        e.wait_ge(gu_in[k], 32 * i + 32)
                        for c in range(KT):
                            last = pe.matmul(b[2 + k][:, :], xgT[k][:, c, :], wgu[k][:, c, :],
                                             start=(c == 0), stop=(c == KT - 1))
                        last.then_inc(gu_done[k], 1)

                    def turn_ac(i, k):
                        e.wait_ge(ac_ready[k], i + 1)
                        for c in range(FE // P):
                            last = pe.transpose(b[4 + k][:, c * P:(c + 1) * P], ac[k][:, c * P:(c + 1) * P],
                                                C("ident"))
                        last.then_inc(ac_turned[k], 1)

                    def down(i, k):
                        e.wait_ge(acT_ready[k], i + 1)
                        e.wait_ge(dn_in[k], 16 * i + 16)
                        wait(e, yo_ready[1 - k], 2 * i if k == 0 else 2 * i + 2)
                        for half in range(2):
                            for c in range(FE // P):
                                last = pe.matmul(b[6 + half][:, :], acT[k][:, c, :],
                                                 wdn[k][:, c, half * 512:(half + 1) * 512],
                                                 start=(c == 0), stop=(c == FE // P - 1))
                        last.then_inc(dn_done[k], 1)

                    def head():
                        turn_x(0, 0)
                        turn_x(0, 1)
                        gate_up(0, 0)
                        turn_ac(0, 0)

                    def body(i):
                        turn_x(i, 0)
                        gate_up(i - 1, 1)
                        down(i - 1, 0)
                        turn_ac(i - 1, 1)
                        turn_x(i, 1)
                        gate_up(i, 0)
                        down(i - 1, 1)
                        turn_ac(i, 0)

                    def tail(m):
                        gate_up(m, 1)
                        down(m, 0)
                        turn_ac(m, 1)
                        down(m, 1)
                    pair_loop(e, head, body, tail)

                def x_turned_s(e, i, k):
                    e.wait_ge(xg_turned[k], i + 1)
                    act.activation(xgT[k][:, 0:H, :].rearrange("p c t -> p (c t)"), b[0][:, :], ACT.Copy
                                   ).then_inc(xgT_ready[k], 1)
                    act.dma_start(idg[k][:, :], tab_d[ds(tile_entry(e, i + 1, k, 1, NE * SLOTS), P), :]
                                  ).then_inc(idg_in[k], 16)

                def silu(e, i, k):
                    e.wait_ge(gu_done[k], i + 1)
                    act.activation(sg[k][:, :], b[2 + k][:, 0:FE], ACT.Silu).then_inc(silu_ready[k], 1)

                def ac_turned_s(e, i, k):
                    e.wait_ge(ac_turned[k], i + 1)
                    act.activation(acT[k][:, :, :].rearrange("p c t -> p (c t)"), b[4 + k][:, 0:FE], ACT.Copy
                                   ).then_inc(acT_ready[k], 1)

                def out_s(e, i, k):
                    e.wait_ge(dn_done[k], i + 1)
                    wait(e, scattered[k], 16 * i)
                    act.activation(yo[k][:, 0:512], b[6][:, :], ACT.Copy).then_inc(yo_ready[k], 1)

                @block.scalar
                def _(e):
                    def head():
                        for k in pr:
                            act.dma_start(idg[k][:, :], tab_d[k * SLOTS:k * SLOTS + P, :]).then_inc(idg_in[k], 16)
                        x_turned_s(e, 0, 0)
                        x_turned_s(e, 0, 1)
                        silu(e, 0, 0)
                        ac_turned_s(e, 0, 0)

                    def body(i):
                        x_turned_s(e, i, 0)
                        silu(e, i - 1, 1)
                        out_s(e, i - 1, 0)
                        ac_turned_s(e, i - 1, 1)
                        x_turned_s(e, i, 1)
                        silu(e, i, 0)
                        out_s(e, i - 1, 1)
                        ac_turned_s(e, i, 0)

                    def tail(m):
                        silu(e, m, 1)
                        out_s(e, m, 0)
                        ac_turned_s(e, m, 1)
                        out_s(e, m, 1)
                    pair_loop(e, head, body, tail)

                def x_turned_v(e, i, k):
                    e.wait_ge(xg_turned[k], i + 1)
                    dve.tensor_copy(xgT[k][:, H:, :].rearrange("p c t -> p (c t)"), b[1][:, :]
                                    ).then_inc(xgT_ready[k], 1)

                def gate(e, i, k):
                    e.wait_ge(silu_ready[k], i + 1)
                    e.wait_ge(ids_in[k], 16 * i + 16)
                    dve.scalar_tensor_tensor(out=ac[k][:, :], in0=sg[k][:, :],
                                             scalar=ids[k][:, 2:3].bitcast(F32), in1=b[2 + k][:, FE:],
                                             op0=ALU.mult, op1=ALU.mult).then_inc(ac_ready[k], 1)

                def out_v(e, i, k):
                    e.wait_ge(dn_done[k], i + 1)
                    wait(e, scattered[k], 16 * i)
                    dve.tensor_copy(yo[k][:, 512:], b[7][:, :]).then_inc(yo_ready[k], 1)

                @block.vector
                def _(e):
                    def head():
                        x_turned_v(e, 0, 0)
                        x_turned_v(e, 0, 1)
                        gate(e, 0, 0)

                    def body(i):
                        x_turned_v(e, i, 0)
                        gate(e, i - 1, 1)
                        out_v(e, i - 1, 0)
                        x_turned_v(e, i, 1)
                        gate(e, i, 0)
                        out_v(e, i - 1, 1)

                    def tail(m):
                        gate(e, m, 1)
                        e.wait_ge(gu_in[0], 32 * m + 64)
                        out_v(e, m, 0)
                        out_v(e, m, 1)
                    pair_loop(e, head, body, tail)

        with ExitStack() as c5:
            pr = range(2)
            hh_, y0, res = ([sb(f"{n}{i}", [P, m * D], ctx=c5) for i in pr] for n, m in (("hin", 1), ("y0", 2), ("res", 1)))
            lng = sb("ln2g", [P, D], ctx=c5)
            lnb = sb("ln2b", [P, D], ctx=c5)
            stats = [sb(f"stats2{i}", [P, 2, 6], ctx=c5) for i in pr]
            mv = [sb(f"mv2{i}", [P, 2], ctx=c5) for i in pr]
            rstd = [sb(f"rstd2{i}", [P, 1], ctx=c5) for i in pr]
            S = phase(c5)
            S2 = lambda n: [S(f"{n}{i}") for i in pr]
            ln_in, in_ready, res_ready, chn = S("ln2_in"), S2("in_ready"), S2("res_ready"), S("chn2")
            var_ready, rstd_ready, norm_ready, out_ready, stored, gmul = (S2(n) for n in (
                "var_ready2", "rstd_ready2", "norm_ready2", "out_ready", "stored", "gmul"))

            with nc.Block() as block:
                @block.sync
                def _(e):
                    sp.dma_start(lng[:, :], ln2g_d.broadcast_to((P, D))).then_inc(ln_in, 16)
                    sp.dma_start(lnb[:, :], ln2b_d.broadcast_to((P, D))).then_inc(ln_in, 16)
                    y2_v = y2_d.rearrange("(t k) d -> t (k d)", k=2)

                    def load(t, k, m=P):
                        sp.dma_start(hh_[k][0:m, :], h_d[ds(t * P, m), :]).then_inc(in_ready[k], 16)
                        sp.dma_start(y0[k][0:m, :], y2_v[ds(t * P, m), :]).then_inc(in_ready[k], 16)
                    for k in pr:
                        load(k, k)

                    def store(i, k):
                        e.wait_ge(out_ready[k], i + 1)
                        sp.dma_start(yp_o[0, ds((2 * i + k) * P, P), :], res[k][:, :]).then_inc(stored[k], 16)
                    with e.Fori(0, PT // 2 - 1) as i:
                        for k in pr:
                            store(i, k)
                            load(2 * i + k + 2, k)
                    store(PT // 2 - 1, 0)
                    load(PT, 0, NS)
                    store(PT // 2 - 1, 1)
                    e.wait_ge(out_ready[0], PT // 2 + 1)
                    sp.dma_start(ys_o.rearrange("s t d -> (s t) d"), res[0][0:NS, :]).then_inc(stored[0], 16)
                    e.wait_ge(stored[0], 16 * (PT // 2 + 1))
                    e.wait_ge(stored[1], 16 * (PT // 2))

                def tiles5(e, step):
                    def body(i):
                        for k in pr:
                            step(i, k, P)
                    turns(e, PT // 2, body)
                    step(PT // 2, 0, NS)

                @block.gpsimd
                def _(e):
                    e.wait_ge(ln_in, 32)

                    def step(i, k, m):
                        e.wait_ge(var_ready[k], i + 1)
                        pool.tensor_tensor(rstd[k][0:m, :], mv[k][0:m, 1:2], mhalf[0:m, 0:1], ALU.pow
                                           ).then_inc(rstd_ready[k], 1)
                        e.wait_ge(norm_ready[k], i + 1)
                        pool.tensor_tensor(res[k][0:m, :], res[k][0:m, :], lnb[0:m, :], ALU.add
                                           ).then_inc(out_ready[k], 1)
                    tiles5(e, step)

                @block.vector
                def _(e):
                    e.wait_ge(ln_in, 32)

                    def step(i, k, m):
                        at = (2 * i + k) * 5 if m == P else PT * 5
                        ln = [0]

                        def link(ins):
                            ln[0] += 1
                            ins.then_inc(chn, 1)
                            e.wait_ge(chn, at + ln[0])
                        e.wait_ge(in_ready[k], 32 * i + 32)
                        wait(e, stored[k], 16 * i)
                        y, r = y0[k], res[k][0:m, :]
                        link(dve.scalar_tensor_tensor(out=r, in0=hh_[k][0:m, :], scalar=ALPHA, in1=y[0:m, 0:D],
                                                      op0=ALU.mult, op1=ALU.add))
                        link(dve.tensor_tensor(r, r, y[0:m, D:], ALU.add))
                        for half in range(2):
                            last = dve.bn_stats(stats[k][0:m, half, :], r[:, half * 512:(half + 1) * 512])
                        link(last)
                        dve.memset(y0[k][:, 0:1], 0.0)
                        link(dve.bn_aggr(mv[k][0:m, :], stats[k][0:m].rearrange("p a b -> p (a b)")))
                        dve.tensor_scalar(mv[k][0:m, 1:2], mv[k][0:m, 1:2], LN_EPS, None, ALU.add
                                          ).then_inc(var_ready[k], 1)
                        e.wait_ge(rstd_ready[k], i + 1)
                        link(dve.tensor_scalar(r, r, mv[k][0:m, 0:1], rstd[k][0:m, :], ALU.subtract, ALU.mult))
                        dve.tensor_tensor(r, r, lng[0:m, :], ALU.mult).then_inc(norm_ready[k], 1)
                    tiles5(e, step)


INPUTS = ["x_prompt", "x_sample", "state_delta", "state_conv", "state_pool", "w_in", "conv_w", "a_log", "dt_bias",
          "gdn_norm_w", "pool_w", "pool_scale", "w_out", "ln1_g", "ln1_b", "w_rg", "b_rg", "w_re", "b_re",
          "w_gate", "w_up", "w_down", "ln2_g", "ln2_b"]
OUTPUTS = [(1, SEQ, D), (NSEQ, DSEQ, D), (1, 1, H, HD, HD), (1, 1, CH, 3 * DA), (1, 1, PH, G * P),
           (1, NSEQ, H, HD, HD), (1, NSEQ, CH, 3 * DA), (1, NSEQ, PH, G * P)]


def kernel(**inputs):
    import concourse.bacc as bacc
    from concourse.bass_utils import run_bass_kernel_spmd

    nc = bacc.Bacc("TRN2", target_bir_lowering=False, num_devices=1)
    arrays = {"in_constants_dram": constants()}
    for name in INPUTS:
        arrays[f"in_{name}_dram"] = np.ascontiguousarray(inputs[name])
    args = [nc.dram_tensor(name, a.shape, mybir.dt.from_np(a.dtype), kind="ExternalInput").ap()
            for name, a in arrays.items()]
    for i, shape in enumerate(OUTPUTS):
        args.append(nc.dram_tensor(f"out_{i}_dram", shape, F32, kind="ExternalOutput").ap())
    args.append(nc.dram_tensor("pooled_dram", (G, P, TP), F32, kind="Internal").ap())
    args.append(nc.dram_tensor("h_dram", (TP, D), F32, kind="Internal").ap())
    args.append(nc.dram_tensor("picked_dram", (2 * TP, D), F32, kind="Internal").ap())
    args.append(nc.dram_tensor("lists_dram", (NLIST * SLOTS, 4), I32, kind="Internal").ap())
    build(nc, *args)
    r = run_bass_kernel_spmd(nc, [arrays], core_ids=[0])
    return tuple(r.results[0][f"out_{i}_dram"] for i in range(len(OUTPUTS)))
```

```python
from contextlib import ExitStack

import numpy as np

import concourse.bass as bass
from concourse import mybir
from concourse.bass import ds

F32 = mybir.dt.float32
I32 = mybir.dt.int32
ALU = mybir.AluOpType
ACT = mybir.ActivationFunctionType
AX = mybir.AxisListType

P = 128
D = 1024
KT = D // P
SEQ = 1024
NSEQ, DSEQ = 8, 8
NS = NSEQ * DSEQ
T = SEQ + NS
PT = SEQ // P
NT = PT + 1
TP = NT * P
H = 4
HD = 128
DA = H * HD
CW = 4
CH = CW - 1
NCONV = 3 * DA // P
G = 4
PH = 15
NCH = NCONV + H + G
COL_BA = 4 * DA
COL_POOL = COL_BA + 2 * H
EPG = 8
NE = G * EPG
FE = 256
ALPHA = 2.0 ** 0.25
LN_EPS, RMS_EPS, L2_EPS = 1e-5, 1e-6, 1e-6
TAIL = 16
NTAIL = TAIL + NS
SLOTS = TP
NLIST = NE + 1
MAXOV = 20
NTILES = NE + MAXOV
SKIP = 1 << 20
CSEG = CH + DSEQ
CRAW = CH + SEQ + NSEQ * CSEG
CFLAT = CRAW - CH
PSEG = PH + DSEQ
PRAW = PH + SEQ + NSEQ * PSEG
NEG = -1e30

CONST = {}


def constants():
    i = np.arange(P)
    col, row = i[None, :], i[:, None]
    seq_r, seq_c = row // DSEQ, col // DSEQ
    same = (seq_r == seq_c) & (row < NS) & (col < NS)
    parts = {
        "ident": (row == col),
        "ones": np.ones((P, P)),
        "tri": row <= col,
        "tri_s": (row <= col) & same,
        "strict": row < col,
        "same": same,
        "neg": np.where(row <= col, 0.0, NEG),
        "neg_s": np.where((row <= col) & same, 0.0, NEG),
        "m1t": (col // 2 == row // 2) & (col % 2 == 1) & (row % 2 == 0),
    }
    for b in (2, 4, 8, 16, 32, 64):
        parts[f"m{b}"] = (row // (2 * b) == col // (2 * b)) & ((row // b) % 2 == 1) & ((col // b) % 2 == 0)
    parts["seqmask"] = (seq_r == np.arange(NSEQ)[None, :]) & (row < NS)
    rc = np.zeros((G, PH))
    for g in range(G):
        rc[g] = 1.0 / np.minimum(np.arange(PH) + 1, 2 << g)
    parts["rc"] = np.broadcast_to(rc.reshape(1, -1), (P, G * PH))
    parts["w4"] = np.broadcast_to(G - np.arange(G)[None, :], (P, G))
    parts["w8"] = np.broadcast_to(EPG - np.arange(EPG)[None, :], (P, EPG))
    parts["slot0"] = np.broadcast_to(SLOTS * np.arange(NE)[None, :], (P, NE))
    tok = np.arange(NT)[None, :] * P + row
    parts["token"] = tok
    parts["valid"] = tok < T
    parts["skip"] = np.where(tok < T, 0.0, float(SKIP))
    parts["rank"] = np.broadcast_to(np.arange(MAXOV)[None, :], (P, MAXOV))
    parts["even"] = np.broadcast_to(2.0 * np.arange(MAXOV // 2)[None, :], (P, MAXOV // 2))
    at, cols = 0, []
    for name, a in parts.items():
        a = np.broadcast_to(a, (P, a.shape[1])).astype(np.float32)
        CONST[name] = (at, a.shape[1])
        at += a.shape[1]
        cols.append(a)
    return np.ascontiguousarray(np.concatenate(cols, axis=1))


def build(nc, cst_d, x_d, xs_d, sdelta_d, sconv_d, spool_d, w_in_d, conv_w_d, a_log_d, dt_d, gnw_d, pool_w_d,
          pscale_d, w_out_d, ln1g_d, ln1b_d, wrg_d, brg_d, wre_d, bre_d, wg_d, wu_d, wd_d, ln2g_d, ln2b_d,
          yp_o, ys_o, dp_o, cp_o, pp_o, dsm_o, cs_o, ps_o, yb_d, h_d, y2_d, tab_d):
    pe, dve, act, pool, sp = nc.tensor, nc.vector, nc.scalar, nc.gpsimd, nc.sync
    whole = ExitStack()

    def sb(name, shape, dt=F32, ctx=whole):
        return ctx.enter_context(nc.sbuf_tensor(name, shape, dt))

    def pb(name, shape, ctx):
        return ctx.enter_context(nc.psum_tensor(name, shape, F32))

    def phase(stack):
        mine = []

        def sem(name):
            mine.append(nc.alloc_semaphore(name))
            return mine[-1]

        def give_back():
            nc.clear_and_free_semaphores(mine)
            nc.all_engine_barrier()
        stack.callback(give_back)
        return sem

    def bc(ap, n):
        return ap.unsqueeze(len(ap.shape)).broadcast_to(tuple(ap.shape) + (n,))

    def mid(ap, n):
        return ap.unsqueeze(1).broadcast_to((ap.shape[0], n) + tuple(ap.shape[1:]))

    def wait(e, semaphore, n):
        if not isinstance(n, int) or n > 0:
            e.wait_ge(semaphore, n)

    def turns(e, n, body):
        body(0)
        with e.Fori(1, n) as i:
            body(i)

    with whole:
        nconst = sum(n for _, n in CONST.values())
        cst = sb("cst", [P, nconst])

        def C(name):
            at, n = CONST[name]
            return cst[:, at:at + n]

        qkvT = sb("qkvT", [P, NCONV, TP])
        szT = sb("szT", [P, H, TP])
        beta = sb("beta", [P, NT, H])
        ngc = sb("ngc", [P, NT, H])
        egc = sb("egc", [P, NT, H])
        edec = sb("edec", [P, NT, H])
        gdec = sb("gdec", [P, NT, H])
        eglast = sb("eglast", [P, NT, H])
        eglast_s = sb("eglast_s", [P, NSEQ, H])
        gnw = sb("gnw", [P, 1])
        mhalf = sb("mhalf", [P, 16])
        logits = sb("logits", [P, NT, G + NE])

        with ExitStack() as c1:
            xin_tails = sb("xin_tails", [P, 2 * D], ctx=c1)
            xin = [xin_tails[:, i * D:(i + 1) * D] for i in range(2)]
            tails = xin_tails[0:NTAIL, :]
            xT = sb("xT", [P, KT, T], ctx=c1)
            ybT = sb("ybT", [P, G, TP], ctx=c1)
            wblk = [sb(f"wblk{i}", [P, KT, P], ctx=c1) for i in range(2)]
            wba = sb("wba", [P, KT, 2 * H], ctx=c1)
            sums_rows = sb("sums_rows", [P, 2 * PRAW], ctx=c1)
            crow = sums_rows[0:NSEQ * CH + CW, 0:NCONV * P]
            prow = sums_rows[0:NSEQ * PH + 1, NCONV * P:(NCONV + G) * P]
            psA, psB = sums_rows[:, 0:PRAW], sums_rows[:, PRAW:]
            ccol = sb("ccol", [P, NCONV, NSEQ * CH + CW], ctx=c1)
            pcol = sb("pcol", [P, G, NSEQ * PH + 1], ctx=c1)
            raw = [sb(f"raw{i}", [P, CRAW], ctx=c1) for i in range(2)]
            cv = sb("cv", [P, CRAW], ctx=c1)
            ub = [sb(f"ub{i}", [P, PRAW], ctx=c1) for i in range(2)]
            dif = [sb(f"dif{i}", [P, PRAW], ctx=c1) for i in range(2)]
            fix = sb("fix", [P, PH], ctx=c1)
            poolw = sb("poolw", [P, G, P], ctx=c1)
            tailT = sb("tailT", [P, NCONV + G, NTAIL], ctx=c1)
            ba = sb("ba", [P, NT, 2 * H], ctx=c1)
            dtb = sb("dtb", [P, H], ctx=c1)
            alog = sb("alog", [P, H], ctx=c1)
            g1 = sb("g1", [P, NT, H], ctx=c1)
            g2 = sb("g2", [P, NT, H], ctx=c1)
            g3 = sb("g3", [P, NT, H], ctx=c1)
            gseq = sb("gseq", [P, NSEQ, H], ctx=c1)
            pj = [pb(f"pj{i}", [P, 1536], c1) for i in range(2)]
            pc = pb("pc", [P, 512], c1)
            pd = pb("pd", [P, 512], c1)

            S = phase(c1)
            cst_in, rows_in, small_in = S("cst_in"), S("rows_in"), S("small_in")
            x_in = [S(f"x_in{i}") for i in range(2)]
            x_turned = [S(f"x_turned{i}") for i in range(2)]
            xT_ready = [S(f"xT_ready{i}") for i in range(2)]
            w_in_sem = [S(f"w_in{i}") for i in range(2)]
            proj_done = [S(f"proj_done{i}") for i in range(2)]
            proj_read = [S(f"proj_read{i}") for i in range(2)]
            hist_turned, hist_ready = S("hist_turned"), S("hist_ready")
            ba_done, ba_ready = S("ba_done"), S("ba_ready")
            zeroed = S("zeroed")
            seg_ready = [S(f"seg_ready{i}") for i in range(2)]
            tail_ready = [S(f"tail_ready{i}") for i in range(2)]
            taps, conv_done, conv_read = S("taps"), S("conv_done"), S("conv_read")
            poolc = S("poolc")
            dif_ready, mixed, yb_ready = S("dif_ready"), S("mixed"), S("yb_ready")
            tails_turned, tails_ready, state_out = S("tails_turned"), S("tails_ready"), S("state_out")
            exp1, gch = S("exp1"), S("gch")
            g_ready, gsum_done, gates_done = S("g_ready"), S("gsum_done"), S("gates_done")
            x_sample, xs_turned, xs_ready = S("x_sample"), S("xs_turned"), S("xs_ready")

            def raw_seg(par):
                return raw[par][:, CH + SEQ:CRAW].rearrange("p (s c) -> p s c", c=CSEG)

            def ub_seg(par):
                return ub[par][:, PH + SEQ:PRAW].rearrange("p (s c) -> p s c", c=PSEG)

            with nc.Block() as block:
                @block.sync
                def _(e):
                    sp.dma_start(cst[:, :], cst_d).then_inc(cst_in, 16)
                    x_v = x_d[0].rearrange("(t p) d -> t p d", p=P)

                    def load_x(i):
                        for par in range(2):
                            wait(e, x_turned[par], i)
                            sp.dma_start(xin[par], x_v[ds(2 * i + par, 1)].rearrange("a p d -> (a p) d")
                                         ).then_inc(x_in[par], 16)
                    turns(e, PT // 2, load_x)
                    e.wait_ge(x_turned[0], PT // 2)
                    sp.dma_start(xin[0][0:NS, :], xs_d.rearrange("s t d -> (s t) d")).then_inc(x_sample, 16)
                    w_v = w_in_d[0].rearrange("(k p) c -> p k c", p=P)

                    def block_of_columns(n, par, at):
                        wait(e, proj_done[par], n)
                        sp.dma_start(wblk[par][:, :, :], w_v[:, :, at]).then_inc(w_in_sem[par], 16)

                    def load_columns(i):
                        for par in range(2):
                            block_of_columns(i, par, ds((2 * i + par) * P, P))
                    turns(e, (NCONV + H) // 2, load_columns)
                    for g in range(G):
                        block_of_columns((NCONV + H + g) // 2, g % 2,
                                         slice(COL_POOL + g * P, COL_POOL + (g + 1) * P))
                    e.wait_ge(yb_ready, G)
                    sp.dma_start(yb_d.rearrange("g p t -> p g t"), ybT[:, :, :]).then_inc(state_out, 16)
                    e.wait_ge(tails_ready, 2)
                    sp.dma_start(cp_o[0, 0], tails[TAIL - CH:TAIL, 0:NCONV * P]).then_inc(state_out, 16)
                    sp.dma_start(pp_o[0, 0], tails[TAIL - PH:TAIL, NCONV * P:]).then_inc(state_out, 16)
                    for s in range(NSEQ):
                        r = TAIL + s * DSEQ
                        sp.dma_start(cs_o[0, s], tails[r + DSEQ - CH:r + DSEQ, 0:NCONV * P]).then_inc(state_out, 16)
                        sp.dma_start(ps_o[0, s, PH - DSEQ:, :], tails[r:r + DSEQ, NCONV * P:]
                                     ).then_inc(state_out, 16)
                    sp.dma_start(ps_o[0, :, 0:PH - DSEQ, :], spool_d[0, :, DSEQ:, :]).then_inc(state_out, 16)
                    e.wait_ge(state_out, 16 * (4 + 2 * NSEQ))

                @block.gpsimd
                def _(e):
                    e.dma_start(crow[0:NSEQ * CH, :], sconv_d[0].rearrange("s t c -> (s t) c")).then_inc(rows_in, 16)
                    e.dma_start(crow[NSEQ * CH:, :], conv_w_d[0]).then_inc(rows_in, 16)
                    e.dma_start(prow[0:NSEQ * PH, :], spool_d[0].rearrange("s t c -> (s t) c")).then_inc(rows_in, 16)
                    e.dma_start(prow[NSEQ * PH:, :], pscale_d).then_inc(rows_in, 16)
                    e.dma_start(wba[:, :, :], w_in_d[0, :, COL_BA:COL_POOL].rearrange("(k p) c -> p k c", p=P)
                                ).then_inc(small_in, 16)
                    e.dma_start(poolw[:, :, :], pool_w_d[0].rearrange("g c d -> c g d")).then_inc(small_in, 16)
                    e.dma_start(dtb[:, :], dt_d.broadcast_to((P, H))).then_inc(small_in, 16)
                    e.dma_start(alog[:, :], a_log_d.broadcast_to((P, H))).then_inc(small_in, 16)
                    e.dma_start(gnw[:, :], gnw_d.rearrange("a p -> p a")).then_inc(small_in, 16)
                    for par in range(2):
                        pool.memset(raw[par][:, 0:CH], 0.0)
                        pool.memset(ub[par][:, 0:PH], 0.0)
                    pool.memset(qkvT[:, :, T:], 0.0)
                    pool.memset(szT[:, :, T:], 0.0)
                    pool.memset(ybT[:, :, T:], 0.0)
                    pool.memset(ba[:, :, :], 0.0)
                    pool.memset(mhalf[:, :], -0.5).then_inc(zeroed, 1)
                    e.wait_ge(hist_ready, 2)

                    def conv_segments(par, c):
                        pool.tensor_copy(raw_seg(par)[:, :, 0:CH],
                                         ccol[:, c, 0:NSEQ * CH].rearrange("p a (s t) -> p (a s) t", t=CH)
                                         ).then_inc(seg_ready[par], 1)

                    def conv_tail(n, par, c):
                        e.wait_ge(proj_read[par], n)
                        pool.tensor_copy(tailT[:, c, 0:TAIL].rearrange("p a t -> p (a t)"),
                                         raw[par][:, CH + SEQ - TAIL:CH + SEQ])
                        pool.tensor_copy(tailT[:, c, TAIL:].rearrange("p a (s t) -> p (a s) t", t=DSEQ),
                                         raw_seg(par)[:, :, CH:]).then_inc(tail_ready[par], 1)

                    def conv_pair(i):
                        wait(e, conv_done, 2 * i)
                        for par in range(2):
                            conv_segments(par, ds(2 * i + par, 1))
                            conv_tail(i + 1, par, ds(2 * i + par, 1))
                    turns(e, NCONV // 2, conv_pair)
                    for g in range(G):
                        par = g % 2
                        if g >= 2:
                            e.wait_ge(dif_ready, g - 1)
                        pool.tensor_copy(ub_seg(par)[:, :, 0:PH],
                                         pcol[:, g, 0:NSEQ * PH].rearrange("p (s t) -> p s t", t=PH)
                                         ).then_inc(seg_ready[par], 1)
                        e.wait_ge(proj_read[par], (NCONV + H) // 2 + g // 2 + 1)
                        pool.tensor_copy(tailT[:, NCONV + g, 0:TAIL], ub[par][:, PH + SEQ - TAIL:PH + SEQ])
                        pool.tensor_copy(tailT[:, NCONV + g, TAIL:].rearrange("p (s t) -> p s t", t=DSEQ),
                                         ub_seg(par)[:, :, PH:]).then_inc(tail_ready[par], 1)

                @block.tensor
                def _(e):
                    e.wait_ge(cst_in, 16)
                    e.wait_ge(rows_in, 64)
                    nh, npr = NSEQ * CH + CW, NSEQ * PH + 1
                    for c in range(NCONV):
                        last = pe.transpose(pc[:, c * nh:(c + 1) * nh], crow[:, c * P:(c + 1) * P],
                                            C("ident")[0:nh, 0:nh])
                    last.then_inc(hist_turned, 1)
                    for g in range(G):
                        last = pe.transpose(pd[:, g * npr:(g + 1) * npr], prow[:, g * P:(g + 1) * P],
                                            C("ident")[0:npr, 0:npr])
                    last.then_inc(hist_turned, 1)

                    def turn_x(i):
                        for par in range(2):
                            e.wait_ge(x_in[par], 16 * i + 16)
                            wait(e, xT_ready[par], i)
                            for k in range(KT):
                                last = pe.transpose(pj[par][:, k * P:(k + 1) * P], xin[par][:, k * P:(k + 1) * P],
                                                    C("ident"))
                            last.then_inc(x_turned[par], 1)
                    turns(e, PT // 2, turn_x)
                    e.wait_ge(x_sample, 16)
                    e.wait_ge(xT_ready[0], PT // 2)
                    for k in range(KT):
                        last = pe.transpose(pj[0][:, k * NS:(k + 1) * NS], xin[0][0:NS, k * P:(k + 1) * P],
                                            C("ident")[0:NS, 0:NS])
                    last.then_inc(xs_turned, 1)
                    e.wait_ge(xT_ready[1], PT // 2)
                    e.wait_ge(xs_ready, 1)
                    e.wait_ge(small_in, 80)
                    e.wait_ge(hist_ready, 2)
                    for t in range(NT):
                        m = min(P, T - t * P)
                        for k in range(KT):
                            last = pe.matmul(pc[0:m, t * 2 * H:(t + 1) * 2 * H], xT[:, k, t * P:t * P + m],
                                             wba[:, k, :], start=(k == 0), stop=(k == KT - 1))
                    last.then_inc(ba_done, 1)

                    def project(par, n):
                        e.wait_ge(w_in_sem[par], 16 * n + 16)
                        wait(e, proj_read[par], n)
                        for k in range(KT):
                            for a, b in ((0, 512), (512, 1024), (1024, T)):
                                last = pe.matmul(pj[par][:, a:b], wblk[par][:, k, :], xT[:, k, a:b],
                                                 start=(k == 0), stop=(k == KT - 1))
                        last.then_inc(proj_done[par], 1)

                    project(0, 0)
                    project(1, 0)
                    e.wait_ge(g_ready, 1)
                    nprm = PT * H
                    prompt_g = gdec[:, 0:PT, :].rearrange("p t h -> p (t h)")
                    pe.matmul(pd[:, 0:nprm], C("tri"), prompt_g, start=True, stop=True)
                    pe.matmul(pd[:, nprm:nprm + H], C("tri_s"), gdec[:, PT, :], start=True, stop=True)
                    pe.matmul(pd[:, 64:64 + nprm], C("ones"), prompt_g, start=True, stop=True)
                    pe.matmul(pd[:, 64 + nprm:64 + nprm + H], C("same"), gdec[:, PT, :], start=True, stop=True)
                    pe.matmul(pd[:, 128:128 + NSEQ * H], C("ones"), gseq[:, :, :].rearrange("p s h -> p (s h)"),
                              start=True, stop=True).then_inc(gsum_done, 1)
                    with e.Fori(1, (NCONV + H) // 2) as i:
                        for par in range(2):
                            project(par, i)

                    def pool_map(g):
                        e.wait_ge(dif_ready, g + 1)
                        e.wait_ge(proj_read[g % 2], (NCONV + H) // 2 + g // 2 + 1)
                        segs = dif[g % 2][:, PH + SEQ:PRAW].rearrange("p (s c) -> p s c", c=PSEG)
                        for h in range(2):
                            pe.matmul(pj[g % 2][:, h * 512:(h + 1) * 512], poolw[:, g, :],
                                      dif[g % 2][:, PH + h * 512:PH + (h + 1) * 512], start=True, stop=True)
                        pe.matmul(pj[g % 2][:, SEQ:T].rearrange("p (s t) -> p s t", t=DSEQ), poolw[:, g, :],
                                  segs[:, :, PH:], start=True, stop=True).then_inc(mixed, 1)
                    n0 = (NCONV + H) // 2

                    def project_pool(g):
                        if g >= 2:
                            e.wait_ge(yb_ready, g - 1)
                        project(g % 2, n0 + g // 2)
                    for g in range(G):
                        project_pool(g)
                        if g >= 1:
                            pool_map(g - 1)
                    pool_map(G - 1)
                    e.wait_ge(yb_ready, G)
                    e.wait_ge(tail_ready[0], (NCONV + G) // 2)
                    e.wait_ge(tail_ready[1], (NCONV + G) // 2)
                    for c in range(NCONV + G):
                        bank, at = (pj[0], c * P) if c < NCONV else (pj[1], (c - NCONV) * P)
                        last = pe.transpose(bank[0:NTAIL, at:at + P], tailT[:, c, :], C("ident"))
                    last.then_inc(tails_turned, 1)

                @block.scalar
                def _(e):
                    e.wait_ge(hist_turned, 1)
                    act.activation(ccol[:, :, :].rearrange("p c n -> p (c n)"),
                                   pc[:, 0:NCONV * (NSEQ * CH + CW)], ACT.Copy).then_inc(hist_ready, 1)

                    with e.Fori(0, PT // 2) as i:
                        e.wait_ge(x_turned[0], i + 1)
                        act.activation(xT[:, :, ds(2 * i * P, P)],
                                       pj[0][:, 0:D].rearrange("p (k t) -> p k t", t=P), ACT.Copy
                                       ).then_inc(xT_ready[0], 1)
                    e.wait_ge(xs_turned, 1)
                    act.activation(xT[:, :, SEQ:T], pj[0][:, 0:KT * NS].rearrange("p (k t) -> p k t", t=NS),
                                   ACT.Copy).then_inc(xs_ready, 1)
                    e.wait_ge(ba_ready, 1)
                    act.activation(g2[:, :, :], ba[:, :, 0:H], ACT.Exp, scale=-1.0)
                    act.activation(g3[:, :, :], g1[:, :, :], ACT.Exp, scale=-1.0)
                    act.activation(alog[:, :], alog[:, :], ACT.Exp).then_inc(exp1, 1)
                    e.wait_ge(exp1, 1)
                    act.activation(g1[:, :, :], g3[:, :, :], ACT.Ln, bias=1.0).then_inc(exp1, 1)
                    e.wait_ge(gsum_done, 1)
                    sums = pd[:, 0:NT * H].rearrange("p (t h) -> p t h", h=H)
                    act.activation(egc[:, :, :], sums, ACT.Exp)
                    act.activation(ngc[:, :, :], sums, ACT.Copy, scale=-1.0).then_inc(gates_done, 1)
                    act.activation(eglast[:, :, :], pd[:, 64:64 + NT * H].rearrange("p (t h) -> p t h", h=H), ACT.Exp)
                    act.activation(eglast_s[:, :, :],
                                   pd[:, 128:128 + NSEQ * H].rearrange("p (s h) -> p s h", h=H), ACT.Exp
                                   ).then_inc(gates_done, 1)
                    e.wait_ge(gates_done, 3)
                    act.activation(edec[:, :, :], edec[:, :, :], ACT.Exp).then_inc(gates_done, 1)
                    def conv_io(i):
                        for par in range(2):
                            e.wait_ge(proj_done[par], i + 1)
                            wait(e, conv_done, 2 * i)
                            wait(e, tail_ready[par], i)
                            act.activation(raw[par][:, CH:CH + SEQ], pj[par][:, 0:SEQ], ACT.Copy)
                            act.activation(raw_seg(par)[:, :, CH:],
                                           pj[par][:, SEQ:T].rearrange("p (s t) -> p s t", t=DSEQ), ACT.Copy
                                           ).then_inc(proj_read[par], 1)
                            e.wait_ge(conv_done, 2 * i + par + 1)
                            c = ds(2 * i + par, 1)
                            act.activation(qkvT[:, c, 0:SEQ].rearrange("p a t -> p (a t)"), cv[:, 0:SEQ], ACT.Silu)
                            act.activation(qkvT[:, c, SEQ:T].rearrange("p a (s t) -> p (a s) t", t=DSEQ),
                                           cv[:, CH + SEQ:].rearrange("p (s c) -> p s c", c=CSEG)[:, :, 0:DSEQ],
                                           ACT.Silu).then_inc(conv_read, 1)
                    turns(e, NCONV // 2, conv_io)
                    with e.Fori(0, H // 2) as i:
                        for par in range(2):
                            e.wait_ge(proj_done[par], i + NCONV // 2 + 1)
                            act.activation(szT[:, ds(2 * i + par, 1), 0:T].rearrange("p a t -> p (a t)"),
                                           pj[par][:, 0:T], ACT.Silu).then_inc(proj_read[par], 1)

                    def pool_out(g):
                        e.wait_ge(mixed, g + 1)
                        act.activation(ybT[:, g, 0:T], pj[g % 2][:, 0:T], ACT.Copy,
                                       scale=pcol[:, g, NSEQ * PH:NSEQ * PH + 1]).then_inc(yb_ready, 1)
                    for g in range(G):
                        par = g % 2
                        if g >= 2:
                            e.wait_ge(tail_ready[par], NCONV // 2 + g // 2)
                            e.wait_ge(dif_ready, g - 1)
                        e.wait_ge(proj_done[par], (NCONV + H) // 2 + g // 2 + 1)
                        act.activation(ub[par][:, PH:PH + SEQ], pj[par][:, 0:SEQ], ACT.Copy)
                        act.activation(ub_seg(par)[:, :, PH:],
                                       pj[par][:, SEQ:T].rearrange("p (s t) -> p s t", t=DSEQ), ACT.Copy
                                       ).then_inc(proj_read[par], 1)
                        if g >= 1:
                            pool_out(g - 1)
                    pool_out(G - 1)
                    e.wait_ge(tails_turned, 1)
                    act.activation(tails[:, 0:NCONV * P], pj[0][0:NTAIL, :], ACT.Copy).then_inc(tails_ready, 1)

                @block.vector
                def _(e):
                    e.wait_ge(hist_turned, 2)
                    dve.tensor_copy(pcol[:, :, :].rearrange("p c n -> p (c n)"),
                                    pd[:, 0:G * (NSEQ * PH + 1)]).then_inc(hist_ready, 1)
                    with e.Fori(0, PT // 2) as i:
                        e.wait_ge(x_turned[1], i + 1)
                        dve.tensor_copy(xT[:, :, ds((2 * i + 1) * P, P)],
                                        pj[1][:, 0:D].rearrange("p (k t) -> p k t", t=P)).then_inc(xT_ready[1], 1)
                    chain = [0]

                    def link(ins):
                        chain[0] += 1
                        ins.then_inc(gch, 1)
                        e.wait_ge(gch, chain[0])
                    e.wait_ge(ba_done, 1)
                    e.wait_ge(zeroed, 1)
                    dve.tensor_copy(ba[:, 0:PT, :].rearrange("p t c -> p (t c)"), pc[:, 0:PT * 2 * H])
                    link(dve.tensor_copy(ba[0:NS, PT, :], pc[0:NS, PT * 2 * H:NT * 2 * H]))
                    link(dve.tensor_tensor(g2[:, :, :], ba[:, :, H:], mid(dtb[:, :], NT), ALU.add))
                    link(dve.tensor_scalar(gdec[:, :, :], g2[:, :, :], 0.0, None, ALU.max))
                    dve.scalar_tensor_tensor(out=g1[:, :, :], in0=gdec[:, :, :], scalar=2.0, in1=g2[:, :, :],
                                             op0=ALU.mult, op1=ALU.subtract).then_inc(ba_ready, 1)
                    e.wait_ge(exp1, 2)
                    link(dve.tensor_scalar(g2[:, :, :], g2[:, :, :], 1.0, None, ALU.add))
                    link(dve.reciprocal(beta[:, :, :], g2[:, :, :]))
                    link(dve.tensor_tensor(gdec[:, :, :], gdec[:, :, :], g1[:, :, :], ALU.add))
                    link(dve.scalar_tensor_tensor(out=gdec[:, :, :], in0=gdec[:, :, :], scalar=-1.0,
                                                  in1=mid(alog[:, :], NT), op0=ALU.mult, op1=ALU.mult))
                    link(dve.tensor_scalar(gdec[:, PT, :], gdec[:, PT, :], C("valid")[:, PT:PT + 1], None,
                                           ALU.mult))
                    dve.tensor_tensor(gseq[:, :, :], bc(C("seqmask"), H), mid(gdec[:, PT, :], NSEQ), ALU.mult
                                      ).then_inc(g_ready, 1)
                    e.wait_ge(gates_done, 2)
                    dve.tensor_tensor(edec[:, :, :], pd[:, 64:64 + NT * H].rearrange("p (t h) -> p t h", h=H),
                                      ngc[:, :, :], ALU.add).then_inc(gates_done, 1)

                    def convolve(i):
                        for par in range(2):
                            c = 2 * i + par
                            e.wait_ge(proj_read[par], i + 1)
                            e.wait_ge(seg_ready[par], i + 1)
                            wait(e, conv_read, c)
                            for j in range(CW):
                                w = ccol[:, ds(c, 1), NSEQ * CH + j:NSEQ * CH + j + 1].rearrange("p a b -> p (a b)")
                                out = cv[:, 0:CFLAT]
                                if j == 0:
                                    ins = dve.tensor_scalar(out, raw[par][:, 0:CFLAT], w, None, ALU.mult)
                                else:
                                    ins = dve.scalar_tensor_tensor(out=out, in0=raw[par][:, j:CFLAT + j],
                                                                   scalar=w, in1=out, op0=ALU.mult, op1=ALU.add)
                                if j < CW - 1:
                                    ins.then_inc(taps, 1)
                                    e.wait_ge(taps, c * CH + j + 1)
                            ins.then_inc(conv_done, 1)
                    turns(e, NCONV // 2, convolve)
                    chain2 = [0]

                    def plink(ins):
                        chain2[0] += 1
                        ins.then_inc(poolc, 1)
                        e.wait_ge(poolc, chain2[0])
                    for g in range(G):
                        par = g % 2
                        e.wait_ge(proj_read[par], (NCONV + H) // 2 + g // 2 + 1)
                        e.wait_ge(seg_ready[par], NCONV // 2 + g // 2 + 1)
                        if g >= 2:
                            e.wait_ge(mixed, g - 1)
                        src, bufs = ub[par], [psA, psB]
                        for lv in range(g + 1):
                            sh, dst = 1 << lv, bufs[lv % 2]
                            lo = (2 << lv) - 1
                            plink(dve.tensor_tensor(dst[:, lo:], src[:, lo:], src[:, lo - sh:PRAW - sh], ALU.add))
                            src = dst
                        plink(dve.scalar_tensor_tensor(out=dif[par][:, PH:], in0=src[:, PH:], scalar=1.0 / (2 << g),
                                                       in1=ub[par][:, PH:], op0=ALU.mult, op1=ALU.subtract))
                        plink(dve.tensor_tensor(fix[:, :], src[:, PH:2 * PH], C("rc")[:, g * PH:(g + 1) * PH],
                                                ALU.mult))
                        dve.tensor_tensor(dif[par][:, PH:2 * PH], fix[:, :], ub[par][:, PH:2 * PH], ALU.subtract
                                          ).then_inc(dif_ready, 1)
                    e.wait_ge(tails_turned, 1)
                    dve.tensor_copy(tails[:, NCONV * P:], pj[1][0:NTAIL, 0:G * P]).then_inc(tails_ready, 1)

        with ExitStack() as c2:
            def mat(name):
                return sb(name, [P, H, P], ctx=c2)
            wout = sb("wout", [P, 2 * H, D], ctx=c2)
            wr = sb("wr", [P, KT, G + NE], ctx=c2)
            brt = sb("brt", [P, G + NE], ctx=c2)
            lng = sb("lng", [P, D], ctx=c2)
            lnb = sb("lnb", [P, D], ctx=c2)
            stage = sb("stage", [P, NCONV, P], ctx=c2)
            sq = sb("sq", [P, 2 * DA], ctx=c2)
            ssq, rn, osum, ro = (sb(n, [P, 2 * H], ctx=c2) for n in ("ssq", "rn", "osum", "ro"))
            sc = sb("sc", [P, 4, H], ctx=c2)
            kh, kb, kbg, kd, qh, qg, vb = (mat(n) for n in ("kh", "kb", "kbg", "kd", "qh", "qg", "vb"))
            khT, kbT, qhT, qgT = (mat(n) for n in ("khT", "kbT", "qhT", "qgT"))
            gtri, dT, aT, qk, X, XT, Y = (mat(n) for n in ("gtri", "dT", "aT", "qk", "X", "XT", "Y"))
            nwT, st, vn, on, yaT, ybt = (mat(n) for n in ("nwT", "st", "vn", "on", "yaT", "ybt"))
            xt = sb("xt", [P, D], ctx=c2)
            h = sb("h", [P, D], ctx=c2)
            hT = sb("hT", [P, KT, P], ctx=c2)
            stats = sb("stats", [P, 2, 6], ctx=c2)
            mv = sb("mv", [P, 2], ctx=c2)
            rstd = sb("rstd", [P, 1], ctx=c2)
            spare = sb("spare", [P, 1], ctx=c2)
            late = qkvT[:, :, 0:SEQ]
            DIAG = NSEQ * (NS + DSEQ)
            st_s = late[:, 0:H, :].rearrange("p h (s e) -> p h s e", e=P)
            nwD, qgD = late[:, H:2 * H, 0:DIAG], late[:, 2 * H:3 * H, 0:DIAG]
            vseq = hT[0:NS, :, :]
            b = [pb(f"b{i}", [P, 512], c2) for i in range(8)]

            def heads(bank):
                return bank[:, :].rearrange("p (h d) -> p h d", d=P)

            S = phase(c2)
            LV = (2, 4, 8, 16, 32, 64)
            LV_S = (2, 4)
            wo_in, wr_in, ln_in = S("wo_in"), S("wr_in"), S("ln_in")
            stage_in, stage_v_in, yb_in, xt_in = S("stage_in"), S("stage_v_in"), S("yb_in"), S("xt_in")
            turned, sq_ready, ssq_ready, rn_ready = S("turned"), S("sq_ready"), S("ssq_ready"), S("rn_ready")
            scc, tok_ready, kk_ready = S("scc"), S("tok_ready"), S("kk_ready")
            v_turned, vb_ready = S("v_turned"), S("vb_ready")
            gtri_ready, decay_sum, decay_ready = S("gtri_ready"), S("decay_sum"), S("decay_ready")
            turned2, ch_ready, qg_ready = S("turned2"), S("ch_ready"), S("qg_ready")
            ak_done, a_ready, m1c, xt_first, x_turned2 = S("ak_done"), S("a_ready"), S("m1c"), S("xt_first"), S("x_turned2")
            y_done = [S(f"y_done{l}") for l in LV]
            y_ready = [S(f"y_ready{l}") for l in LV]
            px_done = [S(f"px_done{l}") for l in LV]
            p_done = [S(f"p_done{l}") for l in LV]
            x_ready = [S(f"x_ready{l}") for l in LV]
            xt_ready = [S(f"xt_ready{l}") for l in LV]
            w_done, nw_ready, vn_done, vn_ready = S("w_done"), S("nw_ready"), S("vn_done"), S("vn_ready")
            o_done, sd_done, st_ready = S("o_done"), S("sd_done"), S("st_ready")
            osq_ready, osum1, osum_ready, ro_ready, on_ready = (S(n) for n in (
                "osq_ready", "osum1", "osum_ready", "ro_ready", "on_ready"))
            on_turned, ya_ready, mix_done, mix_read = S("on_turned"), S("ya_ready"), S("mix_done"), S("mix_read")
            stat1, mv_ready, mv2, rstd_ready, norm_ready = (S(n) for n in (
                "stat1", "mv_ready", "mv2", "rstd_ready", "norm_ready"))
            hn, h_ready, h_out, h_turned, hT_ready = S("hn"), S("h_ready"), S("h_out"), S("h_turned"), S("hT_ready")
            lg_done, lg_ready, delta_out, sst_in = S("lg_done"), S("lg_ready"), S("delta_out"), S("sst_in")
            diag0, vseq_ready, ds_done, ds_ready, dsc = (S(n) for n in (
                "diag0", "vseq_ready", "ds_done", "ds_ready", "dsc"))

            def tiles(e, step):
                step(-1, "prompt", None, None, False)
                step(0, "prompt", "prompt", None, False)
                step(1, "prompt", "prompt", "prompt", False)
                with e.Fori(2, PT - 1) as t:
                    step(t, "prompt", "prompt", "prompt", True)
                step(PT - 1, "sample", "prompt", "prompt", True)
                step(PT, None, "sample", "prompt", True)
                step(PT + 1, None, None, "sample", True)
                step(PT + 2, None, None, None, True)

            def levels_of(invert):
                return {"prompt": LV, "sample": LV_S, None: ()}[invert]

            with nc.Block() as block:
                @block.sync
                def _(e):
                    def load_qk(t):
                        sp.dma_start(stage[:, 0:2 * H, :], qkvT[:, 0:2 * H, ds(t * P, P)]).then_inc(stage_in, 16)

                    def load_v(t):
                        sp.dma_start(stage[:, 2 * H:, :], qkvT[:, 2 * H:, ds(t * P, P)]).then_inc(stage_v_in, 16)

                    def load_yb(t):
                        sp.dma_start(ybt[:, :, :], yb_d[:, :, ds(t * P, P)].rearrange("g p t -> p g t")
                                     ).then_inc(yb_in, 16)

                    load_qk(0)
                    load_v(0)
                    load_yb(0)
                    sp.dma_start(xt[:, :], x_d[0, 0:P, :]).then_inc(xt_in, 16)
                    sp.dma_start(wout[:, :, :], w_out_d[0].rearrange("(k p) n -> p k n", p=P)).then_inc(wo_in, 16)

                    def step(t, prepare, invert, apply, route):
                        if prepare == "prompt":
                            e.wait_ge(turned, t + 2)
                            load_qk(t + 2)
                        if prepare and invert:
                            e.wait_ge(v_turned, t + 1)
                            load_v(t + 1)
                        if prepare == "sample":
                            e.wait_ge(stage_in, 16 * NT)
                            e.wait_ge(stage_v_in, 16 * NT)
                            for s in range(NSEQ):
                                sp.dma_start(st_s[:, :, s, :], sdelta_d[0, s].rearrange("h d e -> d h e")
                                             ).then_inc(sst_in, 16)
                        if invert and apply:
                            e.wait_ge(mix_done, t)
                            load_yb(t)
                            e.wait_ge(norm_ready, t)
                            if invert == "prompt":
                                sp.dma_start(xt[:, :], x_d[0, ds(t * P, P), :]).then_inc(xt_in, 16)
                            else:
                                sp.dma_start(xt[0:NS, :], xs_d.rearrange("s t d -> (s t) d")).then_inc(xt_in, 16)
                        if invert == "sample":
                            e.wait_ge(st_ready, PT + 1)
                            sp.dma_start(dp_o[0, 0].rearrange("h d e -> d h e"), st[:, :, :]).then_inc(delta_out, 16)
                        if apply:
                            e.wait_ge(h_ready, t)
                            sp.dma_start(h_d[ds(t * P - P, P), :], h[:, :]).then_inc(h_out, 16)
                    tiles(e, step)
                    for hh in range(H):
                        e.wait_ge(ds_ready, hh + 1)
                        sp.dma_start(dsm_o[0, :, hh].rearrange("s d e -> d s e"), st_s[:, hh, :, :]
                                     ).then_inc(delta_out, 16)
                    e.wait_ge(delta_out, 16 * (1 + H))
                    e.wait_ge(h_out, 16 * NT)

                @block.gpsimd
                def _(e):
                    pool.memset(st[:, :, :], 0.0).then_inc(st_ready, 1)

                    def per_head(a, t):
                        return bc(a[:, ds(t, 1), :].rearrange("p a h -> p (a h)"), P)

                    def step(t, prepare, invert, apply, route):
                        n = t + 1
                        if prepare:
                            wait(e, decay_sum, n)
                            tri = C("tri") if prepare == "prompt" else C("tri_s")
                            pool.tensor_tensor(gtri[:, :, :], mid(tri, H), per_head(gdec, n), ALU.mult
                                               ).then_inc(gtri_ready, 1)
                        if invert:
                            e.wait_ge(tok_ready, n)
                            if apply:
                                e.wait_ge(sd_done, t)
                            pool.tensor_tensor(kbg[:, :, :], kb[:, :, :], per_head(egc, t), ALU.mult)
                            pool.tensor_tensor(kd[:, :, :], kh[:, :, :], per_head(edec, t), ALU.mult
                                               ).then_inc(kk_ready, 1)
                        if apply:
                            e.wait_ge(osum_ready, t)
                            pool.tensor_tensor(ro[:, 0:H], osum[:, 0:H], mhalf[:, 0:H], ALU.pow).then_inc(ro_ready, 1)
                        if prepare:
                            e.wait_ge(ssq_ready, n + 1)
                            pool.tensor_tensor(rn[:, :], ssq[:, :], mhalf[:, 0:2 * H], ALU.pow).then_inc(rn_ready, 1)
                        if prepare and not invert:
                            e.dma_start(wr[:, :, 0:G], wrg_d[0].rearrange("(k p) n -> p k n", p=P)).then_inc(wr_in, 16)
                            e.dma_start(wr[:, :, G:], wre_d[0].rearrange("(k p) n -> p k n", p=P)).then_inc(wr_in, 16)
                            e.dma_start(brt[:, 0:G], brg_d.broadcast_to((P, G))).then_inc(wr_in, 16)
                            e.dma_start(brt[:, G:], bre_d.broadcast_to((P, NE))).then_inc(wr_in, 16)
                            e.dma_start(lng[:, :], ln1g_d.broadcast_to((P, D))).then_inc(ln_in, 16)
                            e.dma_start(lnb[:, :], ln1b_d.broadcast_to((P, D))).then_inc(ln_in, 16)
                        if prepare == "sample":
                            e.wait_ge(stage_in, 16 * NT)
                            e.wait_ge(stage_v_in, 16 * NT)
                            pool.memset(nwD, 0.0)
                            pool.memset(qgD, 0.0).then_inc(diag0, 1)
                        if apply:
                            e.wait_ge(mv2, t)
                            pool.tensor_tensor(rstd[:, :], mv[:, 1:2], mhalf[:, 0:1], ALU.pow).then_inc(rstd_ready, 1)
                            e.wait_ge(ln_in, 32)
                            e.wait_ge(norm_ready, t)
                            pool.tensor_tensor(h[:, :], h[:, :], lnb[:, :], ALU.add).then_inc(h_ready, 1)
                    tiles(e, step)

                @block.tensor
                def _(e):
                    def turn(bank, src):
                        for hh in range(H):
                            last = pe.transpose(bank[:, hh * P:(hh + 1) * P], src(hh), C("ident"))
                        return last

                    def step(t, prepare, invert, apply, route):
                        n = t + 1
                        m = NS if apply == "sample" else P
                        levels = levels_of(invert)

                        def mix(k):
                            src, kk = (ybt, k - H) if k >= H else (yaT, k)
                            for half in range(2):
                                last = pe.matmul(b[6 + half][:, :], src[:, kk, :],
                                                 wout[:, k, half * 512:(half + 1) * 512],
                                                 start=(k == H), stop=(k == H - 1))
                            return last

                        def beside_level(l):
                            if l == 0 and prepare:
                                e.wait_ge(gtri_ready, n + 1)
                                neg = C("neg") if prepare == "prompt" else C("neg_s")
                                pe.matmul(b[4][:, :], C("ones"), gtri[:, :, :].rearrange("p h t -> p (h t)"),
                                          start=True, stop=False)
                                pe.matmul(heads(b[4]), C("ident"), mid(neg, H), start=False, stop=True
                                          ).then_inc(decay_sum, 1)
                            if l == 0 and route:
                                e.wait_ge(hT_ready, t - 1)
                                e.wait_ge(wr_in, 64)
                                for k in range(KT):
                                    last = pe.matmul(b[7][:, 0:G + NE], hT[:, k, :], wr[:, k, :],
                                                     start=(k == 0), stop=(k == KT - 1))
                                last.then_inc(lg_done, 1)
                            if l == 1 and apply:
                                if route:
                                    e.wait_ge(lg_ready, t - 1)
                                e.wait_ge(wo_in, 16)
                                e.wait_ge(yb_in, 16 * t)
                                mix(H)
                                mix(H + 1)
                            if l == 2 and apply:
                                e.wait_ge(on_ready, t)
                                e.wait_ge(st_ready, t + 1 if apply == "prompt" else PT + 1)
                                turn(b[3], lambda hh: on[:, hh, :]).then_inc(on_turned, 1)
                                mix(H + 2)
                            if l == 3:
                                if prepare:
                                    e.wait_ge(stage_in, 16 * (n + 1))
                                    e.wait_ge(decay_ready, n + 1)
                                    turn(b[4], lambda hh: stage[:, hh, :])
                                    turn(b[5], lambda hh: stage[:, H + hh, :]).then_inc(turned, 1)
                                if apply:
                                    mix(H + 3)
                            if l == 4:
                                if apply:
                                    e.wait_ge(ya_ready, t)
                                if invert:
                                    e.wait_ge(stage_v_in, 16 * n)
                                    turn(b[3], lambda hh: stage[:, 2 * H + hh, :]).then_inc(v_turned, 1)
                                if apply:
                                    mix(0)
                                    mix(1)
                            if l == 5 and apply:
                                mix(2)
                                mix(3).then_inc(mix_done, 1)

                        if apply:
                            e.wait_ge(kk_ready, t)
                            e.wait_ge(vb_ready, t)
                            e.wait_ge(xt_ready[len(levels_of(apply)) - 1], t)
                            for hh in range(H):
                                last = pe.matmul(b[3][:, hh * P:(hh + 1) * P], kbg[:, hh, :], XT[:, hh, :],
                                                 start=True, stop=True)
                            last.then_inc(w_done, 1)
                        if invert:
                            e.wait_ge(tok_ready, n)
                            turn(b[0], lambda hh: kh[:, hh, :])
                            turn(b[1], lambda hh: kb[:, hh, :])
                            turn(b[2], lambda hh: qh[:, hh, :])
                            if route:
                                e.wait_ge(mix_read, t - 1)
                            turn(b[6], lambda hh: qg[:, hh, :]).then_inc(turned2, 1)
                            e.wait_ge(ch_ready, n)
                            for bank, src in ((b[0], kbT), (b[1], qhT)):
                                for hh in range(H):
                                    last = pe.matmul(bank[:, hh * P:(hh + 1) * P], khT[:, hh, :], src[:, hh, :],
                                                     start=True, stop=True)
                            last.then_inc(ak_done, 1)
                            e.wait_ge(decay_ready, n)
                        if apply:
                            e.wait_ge(nw_ready, t)
                        if apply == "prompt":
                            e.wait_ge(st_ready, t)
                            for hh in range(H):
                                c = slice(hh * P, (hh + 1) * P)
                                pe.matmul(b[4][:, c], XT[:, hh, :], vb[:, hh, :], start=True, stop=False)
                                last = pe.matmul(b[4][:, c], nwT[:, hh, :], st[:, hh, :], start=False, stop=True)
                            last.then_inc(vn_done, 1)
                            e.wait_ge(vn_ready, t)
                            e.wait_ge(qg_ready, t)
                            for hh in range(H):
                                c = slice(hh * P, (hh + 1) * P)
                                pe.matmul(b[5][:, c], qgT[:, hh, :], st[:, hh, :], start=True, stop=False)
                                last = pe.matmul(b[5][:, c], qk[:, hh, :], vn[:, hh, :], start=False, stop=True)
                            last.then_inc(o_done, 1)
                            for hh in range(H):
                                last = pe.matmul(b[3][:, hh * P:(hh + 1) * P], kd[:, hh, :], vn[:, hh, :],
                                                 start=True, stop=True)
                            last.then_inc(sd_done, 1)
                        if apply == "sample":
                            e.wait_ge(sst_in, 16 * NSEQ)
                            for hh in range(H):
                                c = slice(hh * P, (hh + 1) * P)
                                pe.matmul(b[4][0:m, c], XT[:, hh, 0:m], vb[:, hh, :], start=True, stop=False)
                                for s in range(NSEQ):
                                    last = pe.matmul(b[4][0:m, c], nwD[:, hh, s * NS:(s + 1) * NS],
                                                     st_s[:, hh, s, :], start=False, stop=(s == NSEQ - 1))
                            last.then_inc(vn_done, 1)
                            e.wait_ge(vn_ready, t)
                            e.wait_ge(qg_ready, t)
                            for hh in range(H):
                                c = slice(hh * P, (hh + 1) * P)
                                pe.matmul(b[5][0:m, c], qk[0:m, hh, 0:m], vn[0:m, hh, :], start=True, stop=False)
                                for s in range(NSEQ):
                                    last = pe.matmul(b[5][0:m, c], qgD[:, hh, s * NS:(s + 1) * NS],
                                                     st_s[:, hh, s, :], start=False, stop=(s == NSEQ - 1))
                            last.then_inc(o_done, 1)
                        if invert:
                            e.wait_ge(xt_first, n)
                            turn(b[2], lambda hh: XT[:, hh, :]).then_inc(x_turned2, 1)
                        if route:
                            if invert:
                                e.wait_ge(qg_ready, n)
                            else:
                                e.wait_ge(mix_read, t - 1)
                            e.wait_ge(h_ready, t - 1)
                            for k in range(KT):
                                bank, at = b[6 + k // H], (k % H) * P
                                last = pe.transpose(bank[:, at:at + P], h[:, k * P:(k + 1) * P], C("ident"))
                            last.then_inc(h_turned, 1)
                        elif apply:
                            e.wait_ge(qg_ready, n)
                        for l in range(len(LV)):
                            if l < len(levels):
                                e.wait_ge(x_ready[l], n)
                                for hh in range(H):
                                    last = pe.matmul(b[0][:, hh * P:(hh + 1) * P], aT[:, hh, :], X[:, hh, :],
                                                     start=True, stop=True)
                                last.then_inc(y_done[l], 1)
                            beside_level(l)
                            if l < len(levels):
                                e.wait_ge(y_ready[l], n)
                                if l > 0:
                                    e.wait_ge(xt_ready[l - 1], n)
                                if l < len(levels) - 1:
                                    for hh in range(H):
                                        last = pe.matmul(b[1][:, hh * P:(hh + 1) * P], XT[:, hh, :], Y[:, hh, :],
                                                         start=True, stop=True)
                                    last.then_inc(px_done[l], 1)
                                for hh in range(H):
                                    last = pe.matmul(b[2][:, hh * P:(hh + 1) * P], Y[:, hh, :], XT[:, hh, :],
                                                     start=True, stop=True)
                                last.then_inc(p_done[l], 1)
                        if apply == "sample":
                            for hh in range(H):
                                e.wait_ge(vseq_ready, hh + 1)
                                for half in range(2):
                                    last = pe.matmul(b[half][:, :], kd[0:m, hh, :],
                                                     vseq[:, half * H:(half + 1) * H, :].rearrange("p s e -> p (s e)"),
                                                     start=True, stop=True)
                                last.then_inc(ds_done, 1)
                                e.wait_ge(ds_ready, hh + 1)
                    tiles(e, step)

                @block.scalar
                def _(e):
                    def flat(a):
                        return a[:, :, :].rearrange("p h d -> p (h d)")

                    def step(t, prepare, invert, apply, route):
                        n = t + 1
                        m = NS if apply == "sample" else P
                        if apply:
                            e.wait_ge(w_done, t)
                        if apply == "prompt":
                            act.activation(flat(nwT), b[3][:, :], ACT.Copy, scale=-1.0).then_inc(nw_ready, 1)
                        if apply == "sample":
                            for hh in range(H):
                                last = act.activation(
                                    nwD[:, hh, :].rearrange("p (s c) -> p s c", c=NS + DSEQ)[:, :, 0:DSEQ],
                                    b[3][:, hh * P:hh * P + NS].rearrange("p (s r) -> p s r", r=DSEQ), ACT.Copy,
                                    scale=-1.0)
                            last.then_inc(nw_ready, 1)
                        if invert:
                            e.wait_ge(turned2, n)
                            act.activation(flat(khT), b[0][:, :], ACT.Copy)
                            act.activation(flat(kbT), b[1][:, :], ACT.Copy)
                            act.activation(flat(qhT), b[2][:, :], ACT.Copy).then_inc(ch_ready, 1)
                        if apply:
                            e.wait_ge(vn_done, t)
                            act.activation(flat(vn)[0:m], b[4][0:m, :], ACT.Copy).then_inc(vn_ready, 1)
                            e.wait_ge(o_done, t)
                        if invert == "prompt":
                            act.activation(flat(qgT), b[6][:, :], ACT.Copy).then_inc(qg_ready, 1)
                        if invert == "sample":
                            e.wait_ge(diag0, 1)
                            for hh in range(H):
                                last = act.activation(
                                    qgD[:, hh, :].rearrange("p (s c) -> p s c", c=NS + DSEQ)[:, :, 0:DSEQ],
                                    b[6][:, hh * P:hh * P + NS].rearrange("p (s r) -> p s r", r=DSEQ), ACT.Copy)
                            last.then_inc(qg_ready, 1)
                        if apply:
                            e.wait_ge(ssq_ready, n if invert else NT)
                            act.activation(sq[0:m, 0:DA], b[5][0:m, :], ACT.Square).then_inc(osq_ready, 1)
                        if invert:
                            e.wait_ge(x_turned2, n)
                            act.activation(flat(X), b[2][:, :], ACT.Copy).then_inc(x_ready[0], 1)
                        if route:
                            e.wait_ge(h_turned, t - 1)
                            act.activation(hT[:, 0:H, :].rearrange("p k t -> p (k t)"), b[6][:, :], ACT.Copy)
                            act.activation(hT[:, H:, :].rearrange("p k t -> p (k t)"), b[7][:, :], ACT.Copy
                                           ).then_inc(hT_ready, 1)
                        if prepare:
                            e.wait_ge(decay_sum, n + 1)
                            if invert:
                                e.wait_ge(y_ready[0], n)
                            for hh in range(H):
                                bias = ngc[:, ds(n, 1), hh:hh + 1].rearrange("p a h -> p (a h)")
                                last = act.activation(dT[:, hh, :], b[4][:, hh * P:(hh + 1) * P], ACT.Exp, bias=bias)
                            last.then_inc(decay_ready, 1)
                            e.wait_ge(turned, n + 1)
                            if apply:
                                e.wait_ge(osum_ready, t)
                            act.activation(sq[:, 0:DA], b[4][:, :], ACT.Square)
                            act.activation(sq[:, DA:], b[5][:, :], ACT.Square).then_inc(sq_ready, 1)
                    tiles(e, step)

                @block.vector
                def _(e):
                    def col(a, t):
                        return a[:, ds(t, 1), :].rearrange("p a h -> p (a h)")

                    def step(t, prepare, invert, apply, route):
                        n = t + 1
                        u = t - 1
                        m = NS if apply == "sample" else P
                        levels = levels_of(invert)

                        def beside_level(l):
                            if l == 0 and apply:
                                e.wait_ge(osq_ready, t)
                                dve.tensor_reduce(osum[0:m, 0:H], sq[0:m, 0:DA].rearrange("p (h d) -> p h d", d=P),
                                                  AX.X, ALU.add).then_inc(osum1, 1)
                                e.wait_ge(osum1, t)
                                dve.tensor_scalar(osum[0:m, 0:H], osum[0:m, 0:H], 1.0 / HD, RMS_EPS, ALU.mult, ALU.add
                                                  ).then_inc(osum_ready, 1)
                            if l == 1 and apply == "prompt":
                                e.wait_ge(sd_done, t)
                                for hh in range(H):
                                    last = dve.scalar_tensor_tensor(
                                        out=st[:, hh, :], in0=st[:, hh, :],
                                        scalar=eglast[:, ds(u, 1), hh:hh + 1].rearrange("p a h -> p (a h)"),
                                        in1=b[3][:, hh * P:(hh + 1) * P], op0=ALU.mult, op1=ALU.add)
                                last.then_inc(st_ready, 1)
                            if l == 1 and apply:
                                e.wait_ge(ro_ready, t)
                                dve.tensor_tensor(on[0:m], heads(b[5])[0:m], bc(ro[0:m, 0:H], P), ALU.mult
                                                  ).then_inc(on_ready, 1)
                            if l == 3 and apply:
                                e.wait_ge(on_turned, t)
                                dve.scalar_tensor_tensor(out=yaT[:, :, :], in0=heads(b[3]), scalar=gnw[:, :],
                                                         in1=szT[:, :, ds(u * P, P)], op0=ALU.mult, op1=ALU.mult
                                                         ).then_inc(ya_ready, 1)
                            if l == 4 and prepare:
                                e.wait_ge(sq_ready, n + 1)
                                dve.tensor_reduce(ssq[:, :], sq[:, :].rearrange("p (h d) -> p h d", d=P), AX.X, ALU.add
                                                  ).then_inc(scc, 1)
                                e.wait_ge(scc, 3 * n + 1)
                                dve.tensor_scalar(ssq[:, :], ssq[:, :], L2_EPS, None, ALU.add).then_inc(ssq_ready, 1)
                            if l == 5 and prepare:
                                e.wait_ge(rn_ready, n + 1)
                                if invert:
                                    e.wait_ge(kk_ready, n)
                                dve.tensor_scalar(sc[:, 0, :], rn[:, 0:H], HD ** -0.5, None, ALU.mult).then_inc(scc, 1)
                                dve.tensor_tensor(sc[:, 2, :], rn[:, H:], col(beta, n), ALU.mult)
                                e.wait_ge(scc, 3 * n + 2)
                                dve.tensor_tensor(sc[:, 1, :], sc[:, 0, :], col(egc, n), ALU.mult).then_inc(scc, 1)
                                dve.tensor_tensor(kh[:, :, :], heads(b[5]), bc(rn[:, H:], P), ALU.mult)
                                dve.tensor_tensor(qh[:, :, :], heads(b[4]), bc(sc[:, 0, :], P), ALU.mult)

                        if invert:
                            e.wait_ge(ak_done, n)
                            e.wait_ge(decay_ready, n)
                            dve.tensor_tensor(aT[:, :, :], heads(b[0]), dT[:, :, :], ALU.mult).then_inc(a_ready, 1)
                            e.wait_ge(a_ready, n)
                            dve.tensor_tensor(Y[:, :, :], aT[:, :, :], mid(C("m1t"), H), ALU.mult).then_inc(m1c, 1)
                            e.wait_ge(m1c, n)
                            if apply:
                                e.wait_ge(vn_done, t)
                            dve.tensor_tensor(XT[:, :, :], mid(C("ident"), H), Y[:, :, :], ALU.subtract
                                              ).then_inc(xt_first, 1)
                            if apply:
                                e.wait_ge(o_done, t)
                            dve.tensor_tensor(qk[:, :, :], heads(b[1]), dT[:, :, :], ALU.mult)
                        for l in range(len(LV)):
                            if l < len(levels):
                                e.wait_ge(y_done[l], n)
                                dve.tensor_tensor(Y[:, :, :], heads(b[0]), mid(C(f"m{levels[l]}"), H), ALU.mult
                                                  ).then_inc(y_ready[l], 1)
                            beside_level(l)
                            if l < len(levels) - 1:
                                e.wait_ge(px_done[l], n)
                                dve.tensor_tensor(X[:, :, :], X[:, :, :], heads(b[1]), ALU.subtract
                                                  ).then_inc(x_ready[l + 1], 1)
                            if l < len(levels):
                                e.wait_ge(p_done[l], n)
                                dve.tensor_tensor(XT[:, :, :], XT[:, :, :], heads(b[2]), ALU.subtract
                                                  ).then_inc(xt_ready[l], 1)
                            if l == 0 and route:
                                e.wait_ge(lg_done, t - 1)
                                dve.tensor_tensor(col(logits, t - 2), b[7][:, 0:G + NE], brt[:, :], ALU.add
                                                  ).then_inc(lg_ready, 1)
                        if prepare:
                            e.wait_ge(scc, 3 * n + 3)
                            dve.tensor_tensor(kb[:, :, :], heads(b[5]), bc(sc[:, 2, :], P), ALU.mult)
                            dve.tensor_tensor(qg[:, :, :], heads(b[4]), bc(sc[:, 1, :], P), ALU.mult
                                              ).then_inc(tok_ready, 1)
                        if invert:
                            e.wait_ge(v_turned, n)
                            dve.tensor_tensor(vb[:, :, :], heads(b[3]), bc(col(beta, t), P), ALU.mult
                                              ).then_inc(vb_ready, 1)
                        if apply:
                            e.wait_ge(mix_done, t)
                            e.wait_ge(xt_in, 16 * t)
                            for half in range(2):
                                c = slice(half * 512, (half + 1) * 512)
                                last = dve.scalar_tensor_tensor(out=xt[:, c], in0=xt[:, c], scalar=ALPHA,
                                                                in1=b[6 + half][:, :], op0=ALU.mult, op1=ALU.add)
                                last.then_inc(mix_read if half else stat1, 1)
                            e.wait_ge(stat1, 2 * t - 1)
                            dve.bn_stats(stats[:, 0, :], xt[:, 0:512])
                            e.wait_ge(mix_read, t)
                            dve.bn_stats(stats[:, 1, :], xt[:, 512:]).then_inc(stat1, 1)
                            e.wait_ge(stat1, 2 * t)
                            dve.memset(spare[:, :], 0.0)
                            dve.bn_aggr(mv[:, :], stats[:, :, :].rearrange("p a b -> p (a b)")).then_inc(mv_ready, 1)
                            e.wait_ge(mv_ready, t)
                            dve.tensor_scalar(mv[:, 1:2], mv[:, 1:2], LN_EPS, None, ALU.add).then_inc(mv2, 1)
                            e.wait_ge(rstd_ready, t)
                            if route:
                                e.wait_ge(h_turned, t - 1)
                                e.wait_ge(h_out, 16 * (t - 1))
                            dve.tensor_scalar(h[:, :], xt[:, :], mv[:, 0:1], rstd[:, :], ALU.subtract, ALU.mult
                                              ).then_inc(hn, 1)
                            e.wait_ge(ln_in, 32)
                            e.wait_ge(hn, t)
                            dve.tensor_tensor(h[:, :], h[:, :], lng[:, :], ALU.mult).then_inc(norm_ready, 1)
                        if apply == "sample":
                            for hh in range(H):
                                dve.tensor_tensor(vseq, mid(vn[0:NS, hh, :], NSEQ), bc(C("seqmask")[0:NS], P),
                                                  ALU.mult).then_inc(vseq_ready, 1)
                                eg = eglast_s[:, :, hh:hh + 1].rearrange("p s h -> p (s h)")
                                if hh == 0:
                                    e.wait_ge(o_done, NT)
                                dve.tensor_tensor(st_s[:, hh], st_s[:, hh], bc(eg, P), ALU.mult).then_inc(dsc, 1)
                                e.wait_ge(ds_done, hh + 1)
                                e.wait_ge(dsc, hh + 1)
                                for half in range(2):
                                    c = slice(half * H, (half + 1) * H)
                                    last = dve.tensor_tensor(st_s[:, hh, c, :], st_s[:, hh, c, :], heads(b[half]),
                                                             ALU.add)
                                last.then_inc(ds_ready, 1)
                    tiles(e, step)

        order = sb("order", [1, NTILES, 2], I32)
        pairs = sb("pairs", [1, 1], I32)
        wgu = [sb(f"wgu{i}", [P, KT, 2 * FE]) for i in range(2)]
        wdn = [sb(f"wdn{i}", [P, FE // P, D]) for i in range(2)]
        kept = phase(whole)
        gu_in, dn_in = ([kept(f"{n}{i}") for i in range(2)] for n in ("gu_in", "dn_in"))
        wgu_v = [w[0].rearrange("g n (k p) f -> (g n) p k f", p=P) for w in (wg_d, wu_d)]
        wdn_v = wd_d[0].rearrange("g n (k p) f -> (g n) p k f", p=P)

        def load_gu(k, expert):
            for j in range(2):
                sp.dma_start(wgu[k][:, :, j * FE:(j + 1) * FE],
                             wgu_v[j][ds(expert, 1)].rearrange("a p k f -> (a p) k f")).then_inc(gu_in[k], 16)

        def load_dn(k, expert):
            sp.dma_start(wdn[k][:, :, :], wdn_v[ds(expert, 1)].rearrange("a p k f -> (a p) k f")
                         ).then_inc(dn_in[k], 16)

        with ExitStack() as c3:
            def tmp(name, shape, dt=F32):
                return sb(name, shape, dt, ctx=c3)
            NG = [P, NT, G]
            mx, sm, pg, dl, ex = (tmp(n, [P, NT]) for n in ("mx", "sm", "pg", "dl", "ex"))
            ga, gb, ohg = tmp("ga", NG), tmp("gb", NG), tmp("ohg", NG)
            lem = tmp("lem", [P, NT, G, EPG])
            les, ea, oh1, oh2 = (tmp(n, [P, NT, EPG]) for n in ("les", "ea", "oh1", "oh2"))
            pick = [tmp(f"pick{k}", [P, NT, NE]) for k in range(2)]
            both, pos, work = (tmp(n, [P, NT, NE]) for n in ("both", "pos", "work"))
            base = tmp("base", [P, NT + 1, NE])
            slotf = tmp("slotf", [P, 2, NT])
            sloti = tmp("sloti", [P, 2, NT], I32)
            entry = tmp("entry", [P, 2, NT, 4], I32)
            nov, cuma, cumb = (tmp(n, [P, NE]) for n in ("nov", "cuma", "cumb"))
            cmpm = tmp("cmpm", [P, MAXOV, NE])
            ove, ovs = tmp("ove", [P, MAXOV]), tmp("ovs", [P, MAXOV])
            par1 = tmp("par1", [P, MAXOV // 2])
            par2 = tmp("par2", [P, 1])
            empty = tmp("empty", [P, NLIST * SLOTS // P, 4], I32)
            pp = pb("pp", [P, NT * NE], c3)
            pt = pb("pt", [P, NT * NE], c3)
            S = phase(c3)
            chn, filled, emptied = S("chn"), S("filled"), S("emptied")
            ga_ready, ex_ready, dl_ready, eex_ready = S("ga_ready"), S("ex_ready"), S("dl_ready"), S("eex_ready")
            both_ready, counted, entries_ready, listed = S("both_ready"), S("counted"), S("entries_ready"), S("listed")

            with nc.Block() as block:
                @block.sync
                def _(e):
                    e.wait_ge(filled, 2)
                    sp.dma_start(tab_d.rearrange("(p n) c -> p (n c)", p=P),
                                 empty[:, :, :].rearrange("p n c -> p (n c)")).then_inc(emptied, 16)
                    for k in range(2):
                        load_gu(k, k)
                        load_dn(k, k)
                    e.wait_ge(emptied, 16)

                @block.gpsimd
                def _(e):
                    pool.memset(empty[:, :, 0:2], SKIP).then_inc(filled, 1)
                    pool.memset(empty[:, :, 2:4], 0).then_inc(filled, 1)
                    e.wait_ge(emptied, 16)
                    e.wait_ge(entries_ready, 4)
                    for t in range(NT):
                        for k in range(2):
                            pool.indirect_dma_start(tab_d, bass.IndirectOffsetOnAxis(ap=sloti[:, k, t:t + 1], axis=0),
                                                    entry[:, k, t, :], None, bounds_check=NLIST * SLOTS - 1,
                                                    oob_is_err=False).then_inc(listed, 16)
                    e.wait_ge(listed, 16 * 2 * NT)

                @block.tensor
                def _(e):
                    e.wait_ge(both_ready, 1)
                    flat = both[:, :, :].rearrange("p t n -> p (t n)")
                    pe.matmul(pp[:, :], C("strict"), flat, start=True, stop=True)
                    pe.matmul(pt[:, :], C("ones"), flat, start=True, stop=True).then_inc(counted, 1)

                @block.scalar
                def _(e):
                    e.wait_ge(ga_ready, 1)
                    act.activation(gb[:, :, :], ga[:, :, :], ACT.Exp).then_inc(ex_ready, 1)
                    e.wait_ge(dl_ready, 1)
                    act.activation(ex[:, :], dl[:, :], ACT.Exp).then_inc(eex_ready, 1)

                @block.vector
                def _(e):
                    chain = [0]

                    def link(ins):
                        chain[0] += 1
                        ins.then_inc(chn, 1)
                        e.wait_ge(chn, chain[0])

                    def wide(a, m):
                        return mid(a, NT)

                    def first_max(values, n, top, scratch, onehot):
                        link(dve.tensor_reduce(top, values, AX.X, ALU.max))
                        link(dve.tensor_tensor(scratch, values, bc(top, n), ALU.is_equal))
                        link(dve.tensor_tensor(scratch, scratch, mid(C(f"w{n}"), NT), ALU.mult))
                        link(dve.tensor_reduce(sm[:, :], scratch, AX.X, ALU.max))
                        link(dve.tensor_tensor(onehot, scratch, bc(sm[:, :], n), ALU.is_equal))

                    lg = logits[:, :, 0:G]
                    first_max(lg, G, mx[:, :], ga[:, :, :], ohg[:, :, :])
                    dve.tensor_tensor(ga[:, :, :], lg, bc(mx[:, :], G), ALU.subtract).then_inc(ga_ready, 1)
                    e.wait_ge(ex_ready, 1)
                    link(dve.tensor_reduce(pg[:, :], gb[:, :, :], AX.X, ALU.add))
                    link(dve.reciprocal(pg[:, :], pg[:, :]))
                    le = logits[:, :, G:].rearrange("p t (g n) -> p t g n", n=EPG)
                    for t in range(NT):
                        last = dve.tensor_tensor(lem[:, t], le[:, t], bc(ohg[:, t, :], EPG), ALU.mult)
                    link(last)
                    link(dve.tensor_tensor(les[:, :, :], lem[:, :, 0, :], lem[:, :, 1, :], ALU.add))
                    link(dve.tensor_tensor(les[:, :, :], les[:, :, :], lem[:, :, 2, :], ALU.add))
                    link(dve.tensor_tensor(les[:, :, :], les[:, :, :], lem[:, :, 3, :], ALU.add))
                    first_max(les[:, :, :], EPG, mx[:, :], ea[:, :, :], oh1[:, :, :])
                    link(dve.tensor_copy(dl[:, :], mx[:, :]))
                    link(dve.scalar_tensor_tensor(out=les[:, :, :], in0=oh1[:, :, :], scalar=NEG, in1=les[:, :, :],
                                                  op0=ALU.mult, op1=ALU.add))
                    first_max(les[:, :, :], EPG, mx[:, :], ea[:, :, :], oh2[:, :, :])
                    dve.tensor_tensor(dl[:, :], mx[:, :], dl[:, :], ALU.subtract).then_inc(dl_ready, 1)
                    for k, oh in enumerate((oh1, oh2)):
                        for t in range(NT):
                            p4 = pick[k][:, t, :].rearrange("p (g n) -> p g n", n=EPG)
                            last = dve.tensor_tensor(p4, bc(ohg[:, t, :], EPG), mid(oh[:, t, :], G), ALU.mult)
                    link(last)
                    for k in range(2):
                        last = dve.tensor_scalar(pick[k][:, PT, :], pick[k][:, PT, :], C("valid")[:, PT:PT + 1], None,
                                                 ALU.mult)
                    link(last)
                    dve.tensor_tensor(both[:, :, :], pick[0][:, :, :], pick[1][:, :, :], ALU.add
                                      ).then_inc(both_ready, 1)
                    e.wait_ge(eex_ready, 1)
                    link(dve.tensor_scalar(sm[:, :], ex[:, :], 1.0, None, ALU.add))
                    link(dve.reciprocal(sm[:, :], sm[:, :]))
                    link(dve.tensor_tensor(sm[:, :], sm[:, :], pg[:, :], ALU.mult))
                    dve.tensor_copy(entry[:, 0, :, 2].bitcast(F32), sm[:, :])
                    dve.tensor_tensor(entry[:, 1, :, 2].bitcast(F32), sm[:, :], ex[:, :], ALU.mult
                                      ).then_inc(entries_ready, 1)
                    for k in range(2):
                        dve.tensor_copy(entry[:, k, :, 3], C("token"))
                        dve.tensor_copy(entry[:, k, :, 1], C("token"))
                        last = dve.tensor_scalar(entry[:, k, :, 0], C("token"), 2.0, float(k), ALU.mult, ALU.add)
                    last.then_inc(entries_ready, 1)
                    e.wait_ge(counted, 1)
                    tot = pt[:, :].rearrange("p (t n) -> p t n", n=NE)
                    link(dve.memset(base[:, 0, :], 0.0))
                    for t in range(NT):
                        link(dve.tensor_tensor(base[:, t + 1, :], base[:, t, :], tot[:, t, :], ALU.add))
                    link(dve.tensor_tensor(pos[:, :, :], base[:, 0:NT, :],
                                           pp[:, :].rearrange("p (t n) -> p t n", n=NE), ALU.add))
                    link(dve.tensor_tensor(pos[:, :, :], pos[:, :, :], mid(C("slot0"), NT), ALU.add))
                    for k in range(2):
                        link(dve.tensor_tensor(work[:, :, :], pick[k][:, :, :], pos[:, :, :], ALU.mult))
                        link(dve.tensor_reduce(slotf[:, k, :], work[:, :, :], AX.X, ALU.add))
                        link(dve.tensor_tensor(slotf[:, k, :], slotf[:, k, :], C("skip"), ALU.add))
                    dve.tensor_copy(sloti[:, :, :], slotf[:, :, :]).then_inc(entries_ready, 2)

                    cnt = base[:, NT, :]
                    link(dve.memset(nov[:, :], 0.0))
                    for j in range(1, NT):
                        link(dve.scalar_tensor_tensor(out=nov[:, :], in0=cnt, scalar=float(j * P), in1=nov[:, :],
                                                      op0=ALU.is_gt, op1=ALU.add))
                    src, dst = cuma, cumb
                    link(dve.tensor_copy(src[:, :], nov[:, :]))
                    for sh in (1, 2, 4, 8, 16):
                        dve.tensor_copy(dst[:, 0:sh], src[:, 0:sh])
                        link(dve.tensor_tensor(dst[:, sh:], src[:, sh:], src[:, 0:NE - sh], ALU.add))
                        src, dst = dst, src
                    link(dve.tensor_tensor(cmpm[:, :, :], mid(src[:, :], MAXOV), bc(C("rank"), NE), ALU.is_le))
                    link(dve.tensor_reduce(ove[:, :], cmpm[:, :, :], AX.X, ALU.add))
                    link(dve.tensor_tensor(cmpm[:, :, :], cmpm[:, :, :], mid(nov[:, :], MAXOV), ALU.mult))
                    link(dve.tensor_reduce(ovs[:, :], cmpm[:, :, :], AX.X, ALU.add))
                    link(dve.tensor_tensor(ovs[:, :], C("rank"), ovs[:, :], ALU.subtract))
                    link(dve.tensor_scalar(ovs[:, :], ovs[:, :], float(P), float(P), ALU.mult, ALU.add))
                    link(dve.scalar_tensor_tensor(out=ovs[:, :], in0=ove[:, :], scalar=float(SLOTS), in1=ovs[:, :],
                                                  op0=ALU.mult, op1=ALU.add))
                    link(dve.tensor_scalar(ovs[:, :], ovs[:, :], float(NE * SLOTS), None, ALU.min))
                    link(dve.tensor_scalar(ove[:, :], ove[:, :], float(NE - 1), None, ALU.min))
                    dve.tensor_copy(order[0:1, NE:, 0], ove[0:1, :])
                    dve.tensor_copy(order[0:1, NE:, 1], ovs[0:1, :])
                    dve.tensor_copy(order[0:1, 0:NE, 1], C("slot0")[0:1, :])
                    link(dve.tensor_scalar(order[0:1, 0:NE, 0], C("slot0")[0:1, :], 1.0 / SLOTS, 0.25, ALU.mult,
                                           ALU.add))
                    link(dve.tensor_tensor(par1[:, :], src[:, NE - 1:NE].broadcast_to((P, MAXOV // 2)), C("even"),
                                           ALU.is_gt))
                    link(dve.tensor_reduce(par2[:, :], par1[:, :], AX.X, ALU.add))
                    link(dve.tensor_scalar(pairs[0:1, :], par2[0:1, :], float(NE // 2 - 1), None, ALU.add))

        with ExitStack() as c4:
            pr = range(2)

            def two(name, shape, dt=F32):
                return [sb(f"{name}{k}", shape, dt, ctx=c4) for k in pr]
            idg, ids = two("idg", [P, 4], I32), two("ids", [P, 4], I32)
            xg, xgT = two("xg", [P, D]), two("xgT", [P, KT, P])
            sg, ac, acT = two("sg", [P, FE]), two("ac", [P, FE]), two("acT", [P, FE // P, P])
            yo = two("yo", [P, D])
            spare = sb("spare4", [P, 4], ctx=c4)
            b = [pb(f"e{i}", [P, 512], c4) for i in range(8)]
            S = phase(c4)
            S2 = lambda n: [S(f"{n}{i}") for i in pr]
            idg_in, ids_in, gathered, cleared = S2("idg_in"), S2("ids_in"), S2("gathered"), S("cleared")
            xg_turned, xgT_ready, gu_done, silu_ready = S2("xg_turned"), S2("xgT_ready"), S2("gu_done"), S2("silu_ready")
            ac_ready, ac_turned, acT_ready, dn_done = S2("ac_ready"), S2("ac_turned"), S2("acT_ready"), S2("dn_done")
            yo_ready, scattered, carried = S2("yo_ready"), S2("scattered"), S("carried")

            def pair_loop(e, head, body, tail=None):
                last = e.value_load(pairs[0:1, 0:1], min_val=NE // 2 - 1, max_val=(NTILES - 2) // 2 - 1)
                head()
                body(1)
                with e.Fori(2, last + 1) as i:
                    body(i)
                if tail:
                    tail(last)

            def tile_entry(e, i, k, field, top):
                return e.value_load(order[0:1, ds(2 * i + k, 1), field], min_val=0, max_val=top)

            with nc.Block() as block:
                @block.sync
                def _(e):
                    def load_ids(i, k):
                        row = tile_entry(e, i, k, 1, NE * SLOTS)
                        wait(e, scattered[k], 16 * i)
                        sp.dma_start(ids[k][:, :], tab_d[ds(row, P), :]).then_inc(ids_in[k], 16)

                    def head():
                        load_ids(0, 0)
                        load_ids(0, 1)
                        e.wait_ge(gu_done[0], 1)
                        load_gu(0, tile_entry(e, 1, 0, 0, NE - 1))

                    def body(i):
                        first, second, third = (tile_entry(e, i, 1, 0, NE - 1), tile_entry(e, i, 0, 0, NE - 1),
                                                tile_entry(e, i + 1, 0, 0, NE - 1))
                        e.wait_ge(gu_done[1], i)
                        load_gu(1, first)
                        e.wait_ge(dn_done[0], i)
                        load_dn(0, second)
                        load_ids(i, 0)
                        e.wait_ge(gu_done[0], i + 1)
                        load_gu(0, third)
                        e.wait_ge(dn_done[1], i)
                        load_dn(1, first)
                        load_ids(i, 1)
                    pair_loop(e, head, body)

                @block.gpsimd
                def _(e):
                    for k in pr:
                        pool.memset(xg[k][:, :], 0.0).then_inc(cleared, 1)
                    e.wait_ge(cleared, 2)

                    def carry_wait(c):
                        pool.tensor_tensor(spare[:, c:c + 1], mhalf[:, 0:1], mhalf[:, 0:1], ALU.mult).then_inc(carried, 1)

                    def gather(i, k):
                        e.wait_ge(idg_in[k], 16 * i + 16)
                        wait(e, xg_turned[k], i)
                        carry_wait(k)
                        pool.indirect_dma_start(xg[k][:, :], None, h_d,
                                                bass.IndirectOffsetOnAxis(ap=idg[k][:, 1:2], axis=0),
                                                bounds_check=TP - 1, oob_is_err=False).then_inc(gathered[k], 16)

                    def scatter(i, k):
                        e.wait_ge(yo_ready[k], 2 * i + 2)
                        carry_wait(2 + k)
                        pool.indirect_dma_start(y2_d, bass.IndirectOffsetOnAxis(ap=ids[k][:, 0:1], axis=0),
                                                yo[k][:, :], None, bounds_check=2 * TP - 1, oob_is_err=False
                                                ).then_inc(scattered[k], 16)

                    def head():
                        gather(0, 0)
                        gather(0, 1)
                        e.wait_ge(carried, 2)
                        gather(1, 0)
                        gather(1, 1)

                    def body(i):
                        e.wait_ge(carried, 4 * i)
                        gather(i + 1, 0)
                        scatter(i - 1, 0)
                        gather(i + 1, 1)
                        scatter(i - 1, 1)

                    def tail(m):
                        e.wait_ge(carried, 4 * m + 4)
                        scatter(m, 0)
                        scatter(m, 1)
                        for k in pr:
                            e.wait_ge(scattered[k], 16 * m + 16)
                            e.wait_ge(gathered[k], 16 * m + 32)
                    pair_loop(e, head, body, tail)

                @block.tensor
                def _(e):
                    def turn_x(i, k):
                        e.wait_ge(gathered[k], 16 * i + 16)
                        wait(e, xgT_ready[1 - k], 2 * i if k == 0 else 2 * i + 2)
                        for c in range(KT):
                            bank, at = b[c // H], (c % H) * P
                            last = pe.transpose(bank[:, at:at + P], xg[k][:, c * P:(c + 1) * P], C("ident"))
                        last.then_inc(xg_turned[k], 1)

                    def gate_up(i, k):
                        e.wait_ge(xgT_ready[k], 2 * i + 2)
                        e.wait_ge(gu_in[k], 32 * i + 32)
                        for c in range(KT):
                            last = pe.matmul(b[2 + k][:, :], xgT[k][:, c, :], wgu[k][:, c, :],
                                             start=(c == 0), stop=(c == KT - 1))
                        last.then_inc(gu_done[k], 1)

                    def turn_ac(i, k):
                        e.wait_ge(ac_ready[k], i + 1)
                        for c in range(FE // P):
                            last = pe.transpose(b[4 + k][:, c * P:(c + 1) * P], ac[k][:, c * P:(c + 1) * P],
                                                C("ident"))
                        last.then_inc(ac_turned[k], 1)

                    def down(i, k):
                        e.wait_ge(acT_ready[k], i + 1)
                        e.wait_ge(dn_in[k], 16 * i + 16)
                        wait(e, yo_ready[1 - k], 2 * i if k == 0 else 2 * i + 2)
                        for half in range(2):
                            for c in range(FE // P):
                                last = pe.matmul(b[6 + half][:, :], acT[k][:, c, :],
                                                 wdn[k][:, c, half * 512:(half + 1) * 512],
                                                 start=(c == 0), stop=(c == FE // P - 1))
                        last.then_inc(dn_done[k], 1)

                    def head():
                        turn_x(0, 0)
                        turn_x(0, 1)
                        gate_up(0, 0)
                        turn_ac(0, 0)

                    def body(i):
                        turn_x(i, 0)
                        gate_up(i - 1, 1)
                        down(i - 1, 0)
                        turn_ac(i - 1, 1)
                        turn_x(i, 1)
                        gate_up(i, 0)
                        down(i - 1, 1)
                        turn_ac(i, 0)

                    def tail(m):
                        gate_up(m, 1)
                        down(m, 0)
                        turn_ac(m, 1)
                        down(m, 1)
                    pair_loop(e, head, body, tail)

                def x_turned_s(e, i, k):
                    e.wait_ge(xg_turned[k], i + 1)
                    act.activation(xgT[k][:, 0:H, :].rearrange("p c t -> p (c t)"), b[0][:, :], ACT.Copy
                                   ).then_inc(xgT_ready[k], 1)
                    act.dma_start(idg[k][:, :], tab_d[ds(tile_entry(e, i + 1, k, 1, NE * SLOTS), P), :]
                                  ).then_inc(idg_in[k], 16)

                def silu(e, i, k):
                    e.wait_ge(gu_done[k], i + 1)
                    act.activation(sg[k][:, :], b[2 + k][:, 0:FE], ACT.Silu).then_inc(silu_ready[k], 1)

                def ac_turned_s(e, i, k):
                    e.wait_ge(ac_turned[k], i + 1)
                    act.activation(acT[k][:, :, :].rearrange("p c t -> p (c t)"), b[4 + k][:, 0:FE], ACT.Copy
                                   ).then_inc(acT_ready[k], 1)

                def out_s(e, i, k):
                    e.wait_ge(dn_done[k], i + 1)
                    wait(e, scattered[k], 16 * i)
                    act.activation(yo[k][:, 0:512], b[6][:, :], ACT.Copy).then_inc(yo_ready[k], 1)

                @block.scalar
                def _(e):
                    def head():
                        for k in pr:
                            act.dma_start(idg[k][:, :], tab_d[k * SLOTS:k * SLOTS + P, :]).then_inc(idg_in[k], 16)
                        x_turned_s(e, 0, 0)
                        x_turned_s(e, 0, 1)
                        silu(e, 0, 0)
                        ac_turned_s(e, 0, 0)

                    def body(i):
                        x_turned_s(e, i, 0)
                        silu(e, i - 1, 1)
                        out_s(e, i - 1, 0)
                        ac_turned_s(e, i - 1, 1)
                        x_turned_s(e, i, 1)
                        silu(e, i, 0)
                        out_s(e, i - 1, 1)
                        ac_turned_s(e, i, 0)

                    def tail(m):
                        silu(e, m, 1)
                        out_s(e, m, 0)
                        ac_turned_s(e, m, 1)
                        out_s(e, m, 1)
                    pair_loop(e, head, body, tail)

                def x_turned_v(e, i, k):
                    e.wait_ge(xg_turned[k], i + 1)
                    dve.tensor_copy(xgT[k][:, H:, :].rearrange("p c t -> p (c t)"), b[1][:, :]
                                    ).then_inc(xgT_ready[k], 1)

                def gate(e, i, k):
                    e.wait_ge(silu_ready[k], i + 1)
                    e.wait_ge(ids_in[k], 16 * i + 16)
                    dve.scalar_tensor_tensor(out=ac[k][:, :], in0=sg[k][:, :],
                                             scalar=ids[k][:, 2:3].bitcast(F32), in1=b[2 + k][:, FE:],
                                             op0=ALU.mult, op1=ALU.mult).then_inc(ac_ready[k], 1)

                def out_v(e, i, k):
                    e.wait_ge(dn_done[k], i + 1)
                    wait(e, scattered[k], 16 * i)
                    dve.tensor_copy(yo[k][:, 512:], b[7][:, :]).then_inc(yo_ready[k], 1)

                @block.vector
                def _(e):
                    def head():
                        x_turned_v(e, 0, 0)
                        x_turned_v(e, 0, 1)
                        gate(e, 0, 0)

                    def body(i):
                        x_turned_v(e, i, 0)
                        gate(e, i - 1, 1)
                        out_v(e, i - 1, 0)
                        x_turned_v(e, i, 1)
                        gate(e, i, 0)
                        out_v(e, i - 1, 1)

                    def tail(m):
                        gate(e, m, 1)
                        e.wait_ge(gu_in[0], 32 * m + 64)
                        out_v(e, m, 0)
                        out_v(e, m, 1)
                    pair_loop(e, head, body, tail)

        with ExitStack() as c5:
            pr = range(2)
            hh_, y0, res = ([sb(f"{n}{i}", [P, m * D], ctx=c5) for i in pr] for n, m in (("hin", 1), ("y0", 2), ("res", 1)))
            lng = sb("ln2g", [P, D], ctx=c5)
            lnb = sb("ln2b", [P, D], ctx=c5)
            stats = [sb(f"stats2{i}", [P, 2, 6], ctx=c5) for i in pr]
            mv = [sb(f"mv2{i}", [P, 2], ctx=c5) for i in pr]
            rstd = [sb(f"rstd2{i}", [P, 1], ctx=c5) for i in pr]
            S = phase(c5)
            S2 = lambda n: [S(f"{n}{i}") for i in pr]
            ln_in, in_ready, res_ready, chn = S("ln2_in"), S2("in_ready"), S2("res_ready"), S("chn2")
            var_ready, rstd_ready, norm_ready, out_ready, stored, gmul = (S2(n) for n in (
                "var_ready2", "rstd_ready2", "norm_ready2", "out_ready", "stored", "gmul"))

            with nc.Block() as block:
                @block.sync
                def _(e):
                    sp.dma_start(lng[:, :], ln2g_d.broadcast_to((P, D))).then_inc(ln_in, 16)
                    sp.dma_start(lnb[:, :], ln2b_d.broadcast_to((P, D))).then_inc(ln_in, 16)
                    y2_v = y2_d.rearrange("(t k) d -> t (k d)", k=2)

                    def load(t, k, m=P):
                        sp.dma_start(hh_[k][0:m, :], h_d[ds(t * P, m), :]).then_inc(in_ready[k], 16)
                        sp.dma_start(y0[k][0:m, :], y2_v[ds(t * P, m), :]).then_inc(in_ready[k], 16)
                    for k in pr:
                        load(k, k)

                    def store(i, k):
                        e.wait_ge(out_ready[k], i + 1)
                        sp.dma_start(yp_o[0, ds((2 * i + k) * P, P), :], res[k][:, :]).then_inc(stored[k], 16)
                    with e.Fori(0, PT // 2 - 1) as i:
                        for k in pr:
                            store(i, k)
                            load(2 * i + k + 2, k)
                    store(PT // 2 - 1, 0)
                    load(PT, 0, NS)
                    store(PT // 2 - 1, 1)
                    e.wait_ge(out_ready[0], PT // 2 + 1)
                    sp.dma_start(ys_o.rearrange("s t d -> (s t) d"), res[0][0:NS, :]).then_inc(stored[0], 16)
                    e.wait_ge(stored[0], 16 * (PT // 2 + 1))
                    e.wait_ge(stored[1], 16 * (PT // 2))

                def tiles5(e, step):
                    def body(i):
                        for k in pr:
                            step(i, k, P)
                    turns(e, PT // 2, body)
                    step(PT // 2, 0, NS)

                @block.gpsimd
                def _(e):
                    e.wait_ge(ln_in, 32)

                    def step(i, k, m):
                        e.wait_ge(var_ready[k], i + 1)
                        pool.tensor_tensor(rstd[k][0:m, :], mv[k][0:m, 1:2], mhalf[0:m, 0:1], ALU.pow
                                           ).then_inc(rstd_ready[k], 1)
                        e.wait_ge(norm_ready[k], i + 1)
                        pool.tensor_tensor(res[k][0:m, :], res[k][0:m, :], lnb[0:m, :], ALU.add
                                           ).then_inc(out_ready[k], 1)
                    tiles5(e, step)

                @block.vector
                def _(e):
                    e.wait_ge(ln_in, 32)

                    def step(i, k, m):
                        at = (2 * i + k) * 5 if m == P else PT * 5
                        ln = [0]

                        def link(ins):
                            ln[0] += 1
                            ins.then_inc(chn, 1)
                            e.wait_ge(chn, at + ln[0])
                        e.wait_ge(in_ready[k], 32 * i + 32)
                        wait(e, stored[k], 16 * i)
                        y, r = y0[k], res[k][0:m, :]
                        link(dve.scalar_tensor_tensor(out=r, in0=hh_[k][0:m, :], scalar=ALPHA, in1=y[0:m, 0:D],
                                                      op0=ALU.mult, op1=ALU.add))
                        link(dve.tensor_tensor(r, r, y[0:m, D:], ALU.add))
                        for half in range(2):
                            last = dve.bn_stats(stats[k][0:m, half, :], r[:, half * 512:(half + 1) * 512])
                        link(last)
                        dve.memset(y0[k][:, 0:1], 0.0)
                        link(dve.bn_aggr(mv[k][0:m, :], stats[k][0:m].rearrange("p a b -> p (a b)")))
                        dve.tensor_scalar(mv[k][0:m, 1:2], mv[k][0:m, 1:2], LN_EPS, None, ALU.add
                                          ).then_inc(var_ready[k], 1)
                        e.wait_ge(rstd_ready[k], i + 1)
                        link(dve.tensor_scalar(r, r, mv[k][0:m, 0:1], rstd[k][0:m, :], ALU.subtract, ALU.mult))
                        dve.tensor_tensor(r, r, lng[0:m, :], ALU.mult).then_inc(norm_ready[k], 1)
                    tiles5(e, step)


INPUTS = ["x_prompt", "x_sample", "state_delta", "state_conv", "state_pool", "w_in", "conv_w", "a_log", "dt_bias",
          "gdn_norm_w", "pool_w", "pool_scale", "w_out", "ln1_g", "ln1_b", "w_rg", "b_rg", "w_re", "b_re",
          "w_gate", "w_up", "w_down", "ln2_g", "ln2_b"]
OUTPUTS = [(1, SEQ, D), (NSEQ, DSEQ, D), (1, 1, H, HD, HD), (1, 1, CH, 3 * DA), (1, 1, PH, G * P),
           (1, NSEQ, H, HD, HD), (1, NSEQ, CH, 3 * DA), (1, NSEQ, PH, G * P)]


def kernel(**inputs):
    import concourse.bacc as bacc
    from concourse.bass_utils import run_bass_kernel_spmd

    nc = bacc.Bacc("TRN2", target_bir_lowering=False, num_devices=1)
    arrays = {"in_constants_dram": constants()}
    for name in INPUTS:
        arrays[f"in_{name}_dram"] = np.ascontiguousarray(inputs[name])
    args = [nc.dram_tensor(name, a.shape, mybir.dt.from_np(a.dtype), kind="ExternalInput").ap()
            for name, a in arrays.items()]
    for i, shape in enumerate(OUTPUTS):
        args.append(nc.dram_tensor(f"out_{i}_dram", shape, F32, kind="ExternalOutput").ap())
    args.append(nc.dram_tensor("pooled_dram", (G, P, TP), F32, kind="Internal").ap())
    args.append(nc.dram_tensor("h_dram", (TP, D), F32, kind="Internal").ap())
    args.append(nc.dram_tensor("picked_dram", (2 * TP, D), F32, kind="Internal").ap())
    args.append(nc.dram_tensor("lists_dram", (NLIST * SLOTS, 4), I32, kind="Internal").ap())
    build(nc, *args)
    r = run_bass_kernel_spmd(nc, [arrays], core_ids=[0])
    return tuple(r.results[0][f"out_{i}_dram"] for i in range(len(OUTPUTS)))
```

```python
from contextlib import ExitStack

import numpy as np

import concourse.bass as bass
from concourse import mybir
from concourse.bass import ds

F32 = mybir.dt.float32
I32 = mybir.dt.int32
ALU = mybir.AluOpType
ACT = mybir.ActivationFunctionType
AX = mybir.AxisListType

P = 128
D = 1024
KT = D // P
SEQ = 1024
NSEQ, DSEQ = 8, 8
NS = NSEQ * DSEQ
T = SEQ + NS
PT = SEQ // P
NT = PT + 1
TP = NT * P
H = 4
HD = 128
DA = H * HD
CW = 4
CH = CW - 1
PC = 384
NCONV = 3 * DA // P
G = 4
PH = 15
NCH = NCONV + H + G
COL_BA = 4 * DA
COL_POOL = COL_BA + 2 * H
EPG = 8
NE = G * EPG
FE = 256
ALPHA = 2.0 ** 0.25
LN_EPS, RMS_EPS, L2_EPS = 1e-5, 1e-6, 1e-6
TAIL = 16
NTAIL = TAIL + NS
SLOTS = TP
NLIST = NE + 1
MAXOV = 20
NTILES = NE + MAXOV
SKIP = 1 << 20
CSEG = CH + DSEQ
CRAW = CH + SEQ + NSEQ * CSEG
CFLAT = CRAW - CH
PSEG = PH + DSEQ
PRAW = PH + SEQ + NSEQ * PSEG
NEG = -1e30

CONST = {}


def constants():
    i = np.arange(P)
    col, row = i[None, :], i[:, None]
    seq_r, seq_c = row // DSEQ, col // DSEQ
    same = (seq_r == seq_c) & (row < NS) & (col < NS)
    parts = {
        "ident": (row == col),
        "ones": np.ones((P, P)),
        "tri": row <= col,
        "tri_s": (row <= col) & same,
        "strict": row < col,
        "same": same,
        "m1t": (col // 2 == row // 2) & (col % 2 == 1) & (row % 2 == 0),
    }
    for b in (2, 4, 8, 16, 32, 64):
        parts[f"m{b}"] = (row // (2 * b) == col // (2 * b)) & ((row // b) % 2 == 1) & ((col // b) % 2 == 0)
    parts["seqmask"] = (seq_r == np.arange(NSEQ)[None, :]) & (row < NS)
    rc = np.zeros((G, PH))
    for g in range(G):
        rc[g] = 1.0 / np.minimum(np.arange(PH) + 1, 2 << g)
    parts["rc"] = np.broadcast_to(rc.reshape(1, -1), (P, G * PH))
    parts["w4"] = np.broadcast_to(G - np.arange(G)[None, :], (P, G))
    parts["w8"] = np.broadcast_to(EPG - np.arange(EPG)[None, :], (P, EPG))
    parts["slot0"] = np.broadcast_to(SLOTS * np.arange(NE)[None, :], (P, NE))
    tok = np.arange(NT)[None, :] * P + row
    parts["token"] = tok
    parts["valid"] = tok < T
    parts["skip"] = np.where(tok < T, 0.0, float(SKIP))
    parts["rank"] = np.broadcast_to(np.arange(MAXOV)[None, :], (P, MAXOV))
    parts["even"] = np.broadcast_to(2.0 * np.arange(MAXOV // 2)[None, :], (P, MAXOV // 2))
    at, cols = 0, []
    for name, a in parts.items():
        a = np.broadcast_to(a, (P, a.shape[1])).astype(np.float32)
        CONST[name] = (at, a.shape[1])
        at += a.shape[1]
        cols.append(a)
    return np.ascontiguousarray(np.concatenate(cols, axis=1))


def build(nc, cst_d, x_d, xs_d, sdelta_d, sconv_d, spool_d, w_in_d, conv_w_d, a_log_d, dt_d, gnw_d, pool_w_d,
          pscale_d, w_out_d, ln1g_d, ln1b_d, wrg_d, brg_d, wre_d, bre_d, wg_d, wu_d, wd_d, ln2g_d, ln2b_d,
          yp_o, ys_o, dp_o, cp_o, pp_o, dsm_o, cs_o, ps_o, yb_d, h_d, y2_d, tab_d):
    pe, dve, act, pool, sp = nc.tensor, nc.vector, nc.scalar, nc.gpsimd, nc.sync
    whole = ExitStack()

    def sb(name, shape, dt=F32, ctx=whole):
        return ctx.enter_context(nc.sbuf_tensor(name, shape, dt))

    def pb(name, shape, ctx):
        return ctx.enter_context(nc.psum_tensor(name, shape, F32))

    def phase(stack):
        mine = []

        def sem(name):
            mine.append(nc.alloc_semaphore(name))
            return mine[-1]

        def give_back():
            nc.clear_and_free_semaphores(mine)
            nc.all_engine_barrier()
        stack.callback(give_back)
        return sem

    def bc(ap, n):
        return ap.unsqueeze(len(ap.shape)).broadcast_to(tuple(ap.shape) + (n,))

    def mid(ap, n):
        return ap.unsqueeze(1).broadcast_to((ap.shape[0], n) + tuple(ap.shape[1:]))

    def wait(e, semaphore, n):
        if not isinstance(n, int) or n > 0:
            e.wait_ge(semaphore, n)

    def turns(e, n, body):
        body(0)
        with e.Fori(1, n) as i:
            body(i)

    with whole:
        nconst = sum(n for _, n in CONST.values())
        cst = sb("cst", [P, nconst])

        def C(name):
            at, n = CONST[name]
            return cst[:, at:at + n]

        qkvT = sb("qkvT", [P, NCONV, TP])
        szT = sb("szT", [P, H, TP])
        beta = sb("beta", [P, NT, H])
        ngc = sb("ngc", [P, NT, H])
        gc = sb("gc", [P, NT, H])
        egc = sb("egc", [P, NT, H])
        edec = sb("edec", [P, NT, H])
        gdec = sb("gdec", [P, NT, H])
        eglast = sb("eglast", [P, NT, H])
        eglast_s = sb("eglast_s", [P, NSEQ, H])
        gnw = sb("gnw", [P, 1])
        mhalf = sb("mhalf", [P, 16])
        logits = sb("logits", [P, NT, G + NE])

        with ExitStack() as c1:
            xin_tails = sb("xin_tails", [P, 2 * D], ctx=c1)
            tails = xin_tails[0:NTAIL, :]
            xT = sb("xT", [P, KT, T], ctx=c1)
            ybT = sb("ybT", [P, G, TP], ctx=c1)
            wblk = [sb(f"wblk{i}", [P, KT, P], ctx=c1) for i in range(2)]
            wba = sb("wba", [P, KT, 2 * H], ctx=c1)
            sums_rows = sb("sums_rows", [P, 2 * PRAW], ctx=c1)
            crow = sums_rows[0:NSEQ * CH + CW, 0:NCONV * P]
            prow = sums_rows[0:NSEQ * PH + 1, NCONV * P:(NCONV + G) * P]
            psA, psB = sums_rows[:, 0:PRAW], sums_rows[:, PRAW:]
            ccol = sb("ccol", [P, NCONV, NSEQ * CH + CW], ctx=c1)
            pcol = sb("pcol", [P, G, NSEQ * PH + 1], ctx=c1)
            raw = [sb(f"raw{i}", [P, CRAW], ctx=c1) for i in range(2)]
            cv = sb("cv", [P, CRAW], ctx=c1)
            ub = [sb(f"ub{i}", [P, PRAW], ctx=c1) for i in range(2)]
            dif = [sb(f"dif{i}", [P, PRAW], ctx=c1) for i in range(2)]
            NX = 4
            xin = [xin_tails[:, i * D:(i + 1) * D] for i in range(2)] + [dif[i][:, 0:D] for i in range(2)]
            fix = sb("fix", [P, PH], ctx=c1)
            poolw = sb("poolw", [P, G, P], ctx=c1)
            tailT = sb("tailT", [P, NCONV + G, NTAIL], ctx=c1)
            ba = sb("ba", [P, NT, 2 * H], ctx=c1)
            dtb = sb("dtb", [P, H], ctx=c1)
            alog = sb("alog", [P, H], ctx=c1)
            g1 = sb("g1", [P, NT, H], ctx=c1)
            g2 = sb("g2", [P, NT, H], ctx=c1)
            g3 = sb("g3", [P, NT, H], ctx=c1)
            gseq = sb("gseq", [P, NSEQ, H], ctx=c1)
            pj = [pb(f"pj{i}", [P, 1536], c1) for i in range(2)]
            pc = pb("pc", [P, 512], c1)
            pd = pb("pd", [P, 512], c1)

            S = phase(c1)
            ident_in, cst_in, rows_in, small_in = S("ident_in"), S("cst_in"), S("rows_in"), S("small_in")
            x_in = [S(f"x_in{i}") for i in range(NX)]
            x_turned = [S(f"x_turned{i}") for i in range(2)]
            xT_ready = [S(f"xT_ready{i}") for i in range(2)]
            w_in_sem = [S(f"w_in{i}") for i in range(2)]
            proj_done = [S(f"proj_done{i}") for i in range(2)]
            proj_read = [S(f"proj_read{i}") for i in range(2)]
            hist_turned, hist_ready = S("hist_turned"), S("hist_ready")
            ba_done, ba_ready = S("ba_done"), S("ba_ready")
            zeroed = S("zeroed")
            seg_ready = [S(f"seg_ready{i}") for i in range(2)]
            tail_ready = [S(f"tail_ready{i}") for i in range(2)]
            taps, conv_done, conv_read = S("taps"), S("conv_done"), S("conv_read")
            poolc = S("poolc")
            dif_ready, mixed, yb_ready = S("dif_ready"), S("mixed"), S("yb_ready")
            tails_turned, tails_ready, state_out = S("tails_turned"), S("tails_ready"), S("state_out")
            exp1, gch = S("exp1"), S("gch")
            g_ready, gsum_done, gates_done = S("g_ready"), S("gsum_done"), S("gates_done")
            x_sample, xs_turned, xs_ready = S("x_sample"), S("xs_turned"), S("xs_ready")

            def projected(par):
                pairs = pj[par][:, 0:1024].rearrange("p (b c) -> p b c", c=512)[:, :, 0:PC]
                return pairs, pj[par][:, 1024:1024 + SEQ - 2 * PC], pj[par][:, 1024 + SEQ - 2 * PC:1024 + T - 2 * PC]

            def raw_seg(par):
                return raw[par][:, CH + SEQ:CRAW].rearrange("p (s c) -> p s c", c=CSEG)

            def ub_seg(par):
                return ub[par][:, PH + SEQ:PRAW].rearrange("p (s c) -> p s c", c=PSEG)

            with nc.Block() as block:
                @block.sync
                def _(e):
                    sp.dma_start(C("ident"), cst_d[:, 0:P]).then_inc(ident_in, 16)
                    x_v = x_d[0].rearrange("(t p) d -> t p d", p=P)

                    def load_x(i):
                        for q in range(NX):
                            wait(e, x_turned[q % 2], 2 * i + q // 2 - 1)
                            sp.dma_start(xin[q], x_v[ds(NX * i + q, 1)].rearrange("a p d -> (a p) d")
                                         ).then_inc(x_in[q], 16)
                    load_x(0)
                    sp.dma_start(cst[:, P:], cst_d[:, P:]).then_inc(cst_in, 16)
                    with e.Fori(1, PT // NX) as i:
                        load_x(i)
                    e.wait_ge(x_turned[0], (PT - NX) // 2 + 1)
                    sp.dma_start(xin[0][0:NS, :], xs_d.rearrange("s t d -> (s t) d")).then_inc(x_sample, 16)
                    w_v = w_in_d[0].rearrange("(k p) c -> p k c", p=P)

                    def block_of_columns(n, par, at):
                        wait(e, proj_done[par], n)
                        sp.dma_start(wblk[par][:, :, :], w_v[:, :, at]).then_inc(w_in_sem[par], 16)

                    def load_columns(i):
                        for par in range(2):
                            block_of_columns(i, par, ds((2 * i + par) * P, P))
                    turns(e, NCONV // 2, load_columns)
                    for g in range(G):
                        block_of_columns((NCONV + g) // 2, g % 2, slice(COL_POOL + g * P, COL_POOL + (g + 1) * P))
                    for j in range(H):
                        if j == H - 1:
                            e.wait_ge(yb_ready, 3 * G)
                            sp.dma_start(yb_d.rearrange("g p t -> p g t"), ybT[:, :, :]).then_inc(state_out, 16)
                        block_of_columns((NCONV + G + j) // 2, j % 2, slice((NCONV + j) * P, (NCONV + j + 1) * P))
                    e.wait_ge(tails_ready, 2)
                    sp.dma_start(cp_o[0, 0], tails[TAIL - CH:TAIL, 0:NCONV * P]).then_inc(state_out, 16)
                    sp.dma_start(pp_o[0, 0], tails[TAIL - PH:TAIL, NCONV * P:]).then_inc(state_out, 16)
                    for s in range(NSEQ):
                        r = TAIL + s * DSEQ
                        sp.dma_start(cs_o[0, s], tails[r + DSEQ - CH:r + DSEQ, 0:NCONV * P]).then_inc(state_out, 16)
                        sp.dma_start(ps_o[0, s, PH - DSEQ:, :], tails[r:r + DSEQ, NCONV * P:]
                                     ).then_inc(state_out, 16)
                    sp.dma_start(ps_o[0, :, 0:PH - DSEQ, :], spool_d[0, :, DSEQ:, :]).then_inc(state_out, 16)
                    e.wait_ge(state_out, 16 * (4 + 2 * NSEQ))

                @block.gpsimd
                def _(e):
                    for par in range(2):
                        pool.memset(raw[par][:, 0:CH], 0.0)
                        pool.memset(ub[par][:, 0:PH], 0.0)
                    pool.memset(qkvT[:, :, T:], 0.0)
                    pool.memset(szT[:, :, T:], 0.0)
                    pool.memset(ybT[:, :, T:], 0.0)
                    pool.memset(ba[:, :, :], 0.0)
                    pool.memset(mhalf[:, :], -0.5).then_inc(zeroed, 1)
                    e.dma_start(crow[0:NSEQ * CH, :], sconv_d[0].rearrange("s t c -> (s t) c")).then_inc(rows_in, 16)
                    e.dma_start(crow[NSEQ * CH:, :], conv_w_d[0]).then_inc(rows_in, 16)
                    e.dma_start(prow[0:NSEQ * PH, :], spool_d[0].rearrange("s t c -> (s t) c")).then_inc(rows_in, 16)
                    e.dma_start(prow[NSEQ * PH:, :], pscale_d).then_inc(rows_in, 16)
                    e.dma_start(wba[:, :, :], w_in_d[0, :, COL_BA:COL_POOL].rearrange("(k p) c -> p k c", p=P)
                                ).then_inc(small_in, 16)
                    e.dma_start(poolw[:, :, :], pool_w_d[0].rearrange("g c d -> c g d")).then_inc(small_in, 16)
                    e.dma_start(dtb[:, :], dt_d.broadcast_to((P, H))).then_inc(small_in, 16)
                    e.dma_start(alog[:, :], a_log_d.broadcast_to((P, H))).then_inc(small_in, 16)
                    e.dma_start(gnw[:, :], gnw_d.rearrange("a p -> p a")).then_inc(small_in, 16)
                    e.wait_ge(hist_ready, 2)

                    def conv_segments(par, c):
                        pool.tensor_copy(raw_seg(par)[:, :, 0:CH],
                                         ccol[:, c, 0:NSEQ * CH].rearrange("p a (s t) -> p (a s) t", t=CH)
                                         ).then_inc(seg_ready[par], 1)

                    def conv_tail(n, par, c):
                        e.wait_ge(proj_read[par], n)
                        pool.tensor_copy(tailT[:, c, 0:TAIL].rearrange("p a t -> p (a t)"),
                                         raw[par][:, CH + SEQ - TAIL:CH + SEQ])
                        pool.tensor_copy(tailT[:, c, TAIL:].rearrange("p a (s t) -> p (a s) t", t=DSEQ),
                                         raw_seg(par)[:, :, CH:]).then_inc(tail_ready[par], 1)

                    def conv_pair(i):
                        wait(e, conv_done, 2 * i)
                        for par in range(2):
                            conv_segments(par, ds(2 * i + par, 1))
                            conv_tail(i + 1, par, ds(2 * i + par, 1))
                    turns(e, NCONV // 2, conv_pair)
                    for g in range(G):
                        par = g % 2
                        if g >= 2:
                            e.wait_ge(dif_ready, g - 1)
                        pool.tensor_copy(ub_seg(par)[:, :, 0:PH],
                                         pcol[:, g, 0:NSEQ * PH].rearrange("p (s t) -> p s t", t=PH)
                                         ).then_inc(seg_ready[par], 1)
                        e.wait_ge(proj_read[par], NCONV // 2 + g // 2 + 1)
                        pool.tensor_copy(tailT[:, NCONV + g, 0:TAIL], ub[par][:, PH + SEQ - TAIL:PH + SEQ])
                        pool.tensor_copy(tailT[:, NCONV + g, TAIL:].rearrange("p (s t) -> p s t", t=DSEQ),
                                         ub_seg(par)[:, :, PH:]).then_inc(tail_ready[par], 1)

                @block.tensor
                def _(e):
                    e.wait_ge(ident_in, 16)

                    def turn_x(i):
                        for q in range(NX):
                            par = q % 2
                            e.wait_ge(x_in[q], 16 * i + 16)
                            wait(e, xT_ready[par], 2 * i + q // 2)
                            for k in range(KT):
                                last = pe.transpose(pj[par][:, k * P:(k + 1) * P], xin[q][:, k * P:(k + 1) * P],
                                                    C("ident"))
                            last.then_inc(x_turned[par], 1)
                    turns(e, PT // NX, turn_x)
                    e.wait_ge(rows_in, 64)
                    nh, npr = NSEQ * CH + CW, NSEQ * PH + 1
                    for c in range(NCONV):
                        last = pe.transpose(pc[:, c * nh:(c + 1) * nh], crow[:, c * P:(c + 1) * P],
                                            C("ident")[0:nh, 0:nh])
                    last.then_inc(hist_turned, 1)
                    for g in range(G):
                        last = pe.transpose(pd[:, g * npr:(g + 1) * npr], prow[:, g * P:(g + 1) * P],
                                            C("ident")[0:npr, 0:npr])
                    last.then_inc(hist_turned, 1)
                    e.wait_ge(x_sample, 16)
                    e.wait_ge(xT_ready[0], PT // 2)
                    for k in range(KT):
                        last = pe.transpose(pj[0][:, k * NS:(k + 1) * NS], xin[0][0:NS, k * P:(k + 1) * P],
                                            C("ident")[0:NS, 0:NS])
                    last.then_inc(xs_turned, 1)
                    e.wait_ge(xT_ready[1], PT // 2)
                    e.wait_ge(xs_ready, 1)

                    def project(par, n, maps=None):
                        e.wait_ge(w_in_sem[par], 16 * n + 16)
                        wait(e, proj_read[par], n)
                        for k in range(KT):
                            for bank, a in enumerate(range(0, T, PC)):
                                m = min(PC, T - a)
                                if maps and k == 0:
                                    e.wait_ge(yb_ready, 3 * maps - 2 + bank)
                                last = pe.matmul(pj[par][:, bank * 512:bank * 512 + m], wblk[par][:, k, :],
                                                 xT[:, k, a:a + m], start=(k == 0), stop=(k == KT - 1))
                        last.then_inc(proj_done[par], 1)

                    project(0, 0)
                    e.wait_ge(small_in, 80)
                    e.wait_ge(hist_ready, 2)
                    for t in range(NT):
                        m = min(P, T - t * P)
                        for k in range(KT):
                            last = pe.matmul(pc[0:m, t * 2 * H:(t + 1) * 2 * H], xT[:, k, t * P:t * P + m],
                                             wba[:, k, :], start=(k == 0), stop=(k == KT - 1))
                    last.then_inc(ba_done, 1)
                    project(1, 0)
                    e.wait_ge(g_ready, 1)
                    e.wait_ge(cst_in, 16)
                    nprm = PT * H
                    prompt_g = gdec[:, 0:PT, :].rearrange("p t h -> p (t h)")
                    pe.matmul(pd[:, 0:nprm], C("tri"), prompt_g, start=True, stop=True)
                    pe.matmul(pd[:, nprm:nprm + H], C("tri_s"), gdec[:, PT, :], start=True, stop=True)
                    pe.matmul(pd[:, 64:64 + nprm], C("ones"), prompt_g, start=True, stop=True)
                    pe.matmul(pd[:, 64 + nprm:64 + nprm + H], C("same"), gdec[:, PT, :], start=True, stop=True)
                    pe.matmul(pd[:, 128:128 + NSEQ * H], C("ones"), gseq[:, :, :].rearrange("p s h -> p (s h)"),
                              start=True, stop=True).then_inc(gsum_done, 1)
                    with e.Fori(1, NCONV // 2) as i:
                        for par in range(2):
                            project(par, i)

                    def pool_map(g):
                        e.wait_ge(dif_ready, g + 1)
                        e.wait_ge(proj_read[g % 2], NCONV // 2 + g // 2 + 1)
                        segs = dif[g % 2][:, PH + SEQ:PRAW].rearrange("p (s c) -> p s c", c=PSEG)
                        for h in range(2):
                            pe.matmul(pj[g % 2][:, h * 512:(h + 1) * 512], poolw[:, g, :],
                                      dif[g % 2][:, PH + h * 512:PH + (h + 1) * 512], start=True, stop=True)
                        pe.matmul(pj[g % 2][:, SEQ:T].rearrange("p (s t) -> p s t", t=DSEQ), poolw[:, g, :],
                                  segs[:, :, PH:], start=True, stop=True).then_inc(mixed, 1)
                    n0 = NCONV // 2

                    def project_pool(g):
                        project(g % 2, n0 + g // 2, g - 1 if g >= 2 else None)
                    for g in range(G):
                        project_pool(g)
                        if g >= 1:
                            pool_map(g - 1)
                    n0 = (NCONV + G) // 2
                    project(0, n0, G - 1)
                    pool_map(G - 1)
                    project(1, n0, G)
                    e.wait_ge(proj_read[0], n0 + 1)
                    e.wait_ge(gates_done, 4)
                    e.wait_ge(tail_ready[0], (NCONV + G) // 2)
                    e.wait_ge(tail_ready[1], (NCONV + G) // 2)
                    for c in range(NCONV + G):
                        bank, at = (pj[0], c * P) if c < NCONV else (pd, (c - NCONV) * P)
                        last = pe.transpose(bank[0:NTAIL, at:at + P], tailT[:, c, :], C("ident"))
                    last.then_inc(tails_turned, 1)
                    e.wait_ge(tails_ready, 2)
                    project(0, n0 + 1)
                    project(1, n0 + 1)

                @block.scalar
                def _(e):
                    with e.Fori(0, PT // 2) as i:
                        e.wait_ge(x_turned[0], i + 1)
                        act.activation(xT[:, :, ds(2 * i * P, P)],
                                       pj[0][:, 0:D].rearrange("p (k t) -> p k t", t=P), ACT.Copy
                                       ).then_inc(xT_ready[0], 1)
                    e.wait_ge(hist_turned, 1)
                    act.activation(ccol[:, :, :].rearrange("p c n -> p (c n)"),
                                   pc[:, 0:NCONV * (NSEQ * CH + CW)], ACT.Copy).then_inc(hist_ready, 1)

                    e.wait_ge(xs_turned, 1)
                    act.activation(xT[:, :, SEQ:T], pj[0][:, 0:KT * NS].rearrange("p (k t) -> p k t", t=NS),
                                   ACT.Copy).then_inc(xs_ready, 1)
                    e.wait_ge(ba_ready, 1)
                    act.activation(g2[:, :, :], ba[:, :, 0:H], ACT.Exp, scale=-1.0)
                    act.activation(g3[:, :, :], g1[:, :, :], ACT.Exp, scale=-1.0)
                    act.activation(alog[:, :], alog[:, :], ACT.Exp).then_inc(exp1, 1)
                    e.wait_ge(exp1, 1)
                    act.activation(g1[:, :, :], g3[:, :, :], ACT.Ln, bias=1.0).then_inc(exp1, 1)
                    def conv_io(i):
                        for par in range(2):
                            e.wait_ge(proj_done[par], i + 1)
                            wait(e, conv_done, 2 * i)
                            wait(e, tail_ready[par], i)
                            pairs, rest, sample = projected(par)
                            act.activation(raw[par][:, CH:CH + 2 * PC].rearrange("p (b c) -> p b c", c=PC), pairs,
                                           ACT.Copy)
                            act.activation(raw[par][:, CH + 2 * PC:CH + SEQ], rest, ACT.Copy)
                            act.activation(raw_seg(par)[:, :, CH:],
                                           sample.rearrange("p (s t) -> p s t", t=DSEQ), ACT.Copy
                                           ).then_inc(proj_read[par], 1)
                            e.wait_ge(conv_done, 2 * i + par + 1)
                            c = ds(2 * i + par, 1)
                            act.activation(qkvT[:, c, 0:SEQ].rearrange("p a t -> p (a t)"), cv[:, 0:SEQ], ACT.Silu)
                            act.activation(qkvT[:, c, SEQ:T].rearrange("p a (s t) -> p (a s) t", t=DSEQ),
                                           cv[:, CH + SEQ:].rearrange("p (s c) -> p s c", c=CSEG)[:, :, 0:DSEQ],
                                           ACT.Silu).then_inc(conv_read, 1)
                    conv_io(0)
                    e.wait_ge(gsum_done, 1)
                    sums = pd[:, 0:NT * H].rearrange("p (t h) -> p t h", h=H)
                    act.activation(egc[:, :, :], sums, ACT.Exp)
                    act.activation(gc[:, :, :], sums, ACT.Copy)
                    act.activation(ngc[:, :, :], sums, ACT.Copy, scale=-1.0).then_inc(gates_done, 1)
                    act.activation(eglast[:, :, :], pd[:, 64:64 + NT * H].rearrange("p (t h) -> p t h", h=H), ACT.Exp)
                    act.activation(eglast_s[:, :, :],
                                   pd[:, 128:128 + NSEQ * H].rearrange("p (s h) -> p s h", h=H), ACT.Exp
                                   ).then_inc(gates_done, 1)
                    e.wait_ge(gates_done, 3)
                    act.activation(edec[:, :, :], edec[:, :, :], ACT.Exp).then_inc(gates_done, 1)
                    with e.Fori(1, NCONV // 2) as i:
                        conv_io(i)

                    def silu_z(j):
                        e.wait_ge(proj_done[j % 2], (NCONV + G) // 2 + j // 2 + 1)
                        pairs, _, _ = projected(j % 2)
                        act.activation(szT[:, j, 0:2 * PC].rearrange("p (b c) -> p b c", c=PC), pairs, ACT.Silu)
                        act.activation(szT[:, j, 2 * PC:T], pj[j % 2][:, 1024:1024 + T - 2 * PC], ACT.Silu
                                       ).then_inc(proj_read[j % 2], 1)

                    def pool_out(g):
                        e.wait_ge(mixed, g + 1)
                        for a, m in ((0, 512), (512, 512), (1024, T - 1024)):
                            act.activation(ybT[:, g, a:a + m], pj[g % 2][:, a:a + m], ACT.Copy,
                                           scale=pcol[:, g, NSEQ * PH:NSEQ * PH + 1]).then_inc(yb_ready, 1)
                    for g in range(G):
                        par = g % 2
                        if g >= 2:
                            e.wait_ge(tail_ready[par], NCONV // 2 + g // 2)
                            e.wait_ge(dif_ready, g - 1)
                        e.wait_ge(proj_done[par], NCONV // 2 + g // 2 + 1)
                        pairs, rest, sample = projected(par)
                        act.activation(ub[par][:, PH:PH + 2 * PC].rearrange("p (b c) -> p b c", c=PC), pairs,
                                       ACT.Copy)
                        act.activation(ub[par][:, PH + 2 * PC:PH + SEQ], rest, ACT.Copy)
                        act.activation(ub_seg(par)[:, :, PH:],
                                       sample.rearrange("p (s t) -> p s t", t=DSEQ), ACT.Copy
                                       ).then_inc(proj_read[par], 1)
                        if g >= 1:
                            pool_out(g - 1)
                    silu_z(0)
                    pool_out(G - 1)
                    silu_z(1)
                    e.wait_ge(tails_turned, 1)
                    act.activation(tails[:, 0:NCONV * P], pj[0][0:NTAIL, :], ACT.Copy).then_inc(tails_ready, 1)
                    silu_z(2)
                    silu_z(3)

                @block.vector
                def _(e):
                    with e.Fori(0, PT // 2) as i:
                        e.wait_ge(x_turned[1], i + 1)
                        dve.tensor_copy(xT[:, :, ds((2 * i + 1) * P, P)],
                                        pj[1][:, 0:D].rearrange("p (k t) -> p k t", t=P)).then_inc(xT_ready[1], 1)
                    e.wait_ge(hist_turned, 2)
                    dve.tensor_copy(pcol[:, :, :].rearrange("p c n -> p (c n)"),
                                    pd[:, 0:G * (NSEQ * PH + 1)]).then_inc(hist_ready, 1)
                    chain = [0]

                    def link(ins):
                        chain[0] += 1
                        ins.then_inc(gch, 1)
                        e.wait_ge(gch, chain[0])
                    e.wait_ge(ba_done, 1)
                    e.wait_ge(zeroed, 1)
                    e.wait_ge(small_in, 80)
                    e.wait_ge(cst_in, 16)
                    dve.tensor_copy(ba[:, 0:PT, :].rearrange("p t c -> p (t c)"), pc[:, 0:PT * 2 * H])
                    link(dve.tensor_copy(ba[0:NS, PT, :], pc[0:NS, PT * 2 * H:NT * 2 * H]))
                    link(dve.tensor_tensor(g2[:, :, :], ba[:, :, H:], mid(dtb[:, :], NT), ALU.add))
                    link(dve.tensor_scalar(gdec[:, :, :], g2[:, :, :], 0.0, None, ALU.max))
                    dve.scalar_tensor_tensor(out=g1[:, :, :], in0=gdec[:, :, :], scalar=2.0, in1=g2[:, :, :],
                                             op0=ALU.mult, op1=ALU.subtract).then_inc(ba_ready, 1)
                    e.wait_ge(exp1, 2)
                    link(dve.tensor_scalar(g2[:, :, :], g2[:, :, :], 1.0, None, ALU.add))
                    link(dve.reciprocal(beta[:, :, :], g2[:, :, :]))
                    link(dve.tensor_tensor(gdec[:, :, :], gdec[:, :, :], g1[:, :, :], ALU.add))
                    link(dve.scalar_tensor_tensor(out=gdec[:, :, :], in0=gdec[:, :, :], scalar=-1.0,
                                                  in1=mid(alog[:, :], NT), op0=ALU.mult, op1=ALU.mult))
                    link(dve.tensor_scalar(gdec[:, PT, :], gdec[:, PT, :], C("valid")[:, PT:PT + 1], None,
                                           ALU.mult))
                    dve.tensor_tensor(gseq[:, :, :], bc(C("seqmask"), H), mid(gdec[:, PT, :], NSEQ), ALU.mult
                                      ).then_inc(g_ready, 1)

                    def convolve(i):
                        for par in range(2):
                            c = 2 * i + par
                            e.wait_ge(proj_read[par], i + 1)
                            e.wait_ge(seg_ready[par], i + 1)
                            wait(e, conv_read, c)
                            for j in range(CW):
                                w = ccol[:, ds(c, 1), NSEQ * CH + j:NSEQ * CH + j + 1].rearrange("p a b -> p (a b)")
                                out = cv[:, 0:CFLAT]
                                if j == 0:
                                    ins = dve.tensor_scalar(out, raw[par][:, 0:CFLAT], w, None, ALU.mult)
                                else:
                                    ins = dve.scalar_tensor_tensor(out=out, in0=raw[par][:, j:CFLAT + j],
                                                                   scalar=w, in1=out, op0=ALU.mult, op1=ALU.add)
                                if j < CW - 1:
                                    ins.then_inc(taps, 1)
                                    e.wait_ge(taps, c * CH + j + 1)
                            ins.then_inc(conv_done, 1)
                    convolve(0)
                    e.wait_ge(gates_done, 2)
                    dve.tensor_tensor(edec[:, :, :], pd[:, 64:64 + NT * H].rearrange("p (t h) -> p t h", h=H),
                                      ngc[:, :, :], ALU.add).then_inc(gates_done, 1)
                    with e.Fori(1, NCONV // 2) as i:
                        convolve(i)
                    chain2 = [0]

                    def plink(ins):
                        chain2[0] += 1
                        ins.then_inc(poolc, 1)
                        e.wait_ge(poolc, chain2[0])
                    for g in range(G):
                        par = g % 2
                        e.wait_ge(proj_read[par], NCONV // 2 + g // 2 + 1)
                        e.wait_ge(seg_ready[par], NCONV // 2 + g // 2 + 1)
                        if g >= 2:
                            e.wait_ge(mixed, g - 1)
                        src, bufs = ub[par], [psA, psB]
                        for lv in range(g + 1):
                            sh, dst = 1 << lv, bufs[lv % 2]
                            lo = (2 << lv) - 1
                            plink(dve.tensor_tensor(dst[:, lo:], src[:, lo:], src[:, lo - sh:PRAW - sh], ALU.add))
                            src = dst
                        plink(dve.scalar_tensor_tensor(out=dif[par][:, PH:], in0=src[:, PH:], scalar=1.0 / (2 << g),
                                                       in1=ub[par][:, PH:], op0=ALU.mult, op1=ALU.subtract))
                        plink(dve.tensor_tensor(fix[:, :], src[:, PH:2 * PH], C("rc")[:, g * PH:(g + 1) * PH],
                                                ALU.mult))
                        dve.tensor_tensor(dif[par][:, PH:2 * PH], fix[:, :], ub[par][:, PH:2 * PH], ALU.subtract
                                          ).then_inc(dif_ready, 1)
                    e.wait_ge(tails_turned, 1)
                    dve.tensor_copy(tails[:, NCONV * P:], pd[0:NTAIL, 0:G * P]).then_inc(tails_ready, 1)

        with ExitStack() as c2:
            def mat(name):
                return sb(name, [P, H, P], ctx=c2)
            wout = sb("wout", [P, 2 * H, D], ctx=c2)
            wr = sb("wr", [P, KT, G + NE], ctx=c2)
            brt = sb("brt", [P, G + NE], ctx=c2)
            lng = sb("lng", [P, D], ctx=c2)
            lnb = sb("lnb", [P, D], ctx=c2)
            stage = sb("stage", [P, NCONV, P], ctx=c2)
            sq = sb("sq", [P, 2 * DA], ctx=c2)
            ssq, rn, osum, ro = (sb(n, [P, 2 * H], ctx=c2) for n in ("ssq", "rn", "osum", "ro"))
            sc = sb("sc", [P, 4, H], ctx=c2)
            kh, kb, kbg, kd, qh, qg, vb = (mat(n) for n in ("kh", "kb", "kbg", "kd", "qh", "qg", "vb"))
            khT, kbT, qhT, qgT = (mat(n) for n in ("khT", "kbT", "qhT", "qgT"))
            gtri, dT, aT, qk, X, XT, Y = (mat(n) for n in ("gtri", "dT", "aT", "qk", "X", "XT", "Y"))
            nwT, st, vn, on, yaT, ybt = (mat(n) for n in ("nwT", "st", "vn", "on", "yaT", "ybt"))
            xt = sb("xt", [P, D], ctx=c2)
            h = sb("h", [P, D], ctx=c2)
            hT = sb("hT", [P, KT, P], ctx=c2)
            stats = sb("stats", [P, 2, 6], ctx=c2)
            mv = sb("mv", [P, 2], ctx=c2)
            rstd = sb("rstd", [P, 1], ctx=c2)
            spare = sb("spare", [P, 1], ctx=c2)
            late = qkvT[:, :, 0:SEQ]
            DIAG = NSEQ * (NS + DSEQ)
            st_s = late[:, 0:H, :].rearrange("p h (s e) -> p h s e", e=P)
            nwD, qgD = late[:, H:2 * H, 0:DIAG], late[:, 2 * H:3 * H, 0:DIAG]
            vseq = [hT[0:NS, :, :], sq[0:NS, :].rearrange("p (s e) -> p s e", e=P)]
            b = [pb(f"b{i}", [P, 512], c2) for i in range(8)]

            def heads(bank):
                return bank[:, :].rearrange("p (h d) -> p h d", d=P)

            S = phase(c2)
            LV = (2, 4, 8, 16, 32, 64)
            LV_S = (2, 4)
            wo_in, wr_in, ln_in = S("wo_in"), S("wr_in"), S("ln_in")
            stage_in, stage_v_in, yb_in, xt_in = S("stage_in"), S("stage_v_in"), S("yb_in"), S("xt_in")
            turned, sq_ready, ssq_ready, rn_ready = S("turned"), S("sq_ready"), S("ssq_ready"), S("rn_ready")
            scc, tok_ready, kk_ready = S("scc"), S("tok_ready"), S("kk_ready")
            v_turned, vb_ready = S("v_turned"), S("vb_ready")
            gtri_ready, decay_sum, decay_ready = S("gtri_ready"), S("decay_sum"), S("decay_ready")
            sum_read, exp_ready = S("sum_read"), S("exp_ready")
            turned2, ch_ready, qg_ready = S("turned2"), S("ch_ready"), S("qg_ready")
            ak_done, a_ready, m1c, xt_first, x_turned2 = S("ak_done"), S("a_ready"), S("m1c"), S("xt_first"), S("x_turned2")
            y_done = [S(f"y_done{l}") for l in LV]
            y_ready = [S(f"y_ready{l}") for l in LV]
            px_done = [S(f"px_done{l}") for l in LV]
            p_done = [S(f"p_done{l}") for l in LV]
            x_ready = [S(f"x_ready{l}") for l in LV]
            xt_ready = [S(f"xt_ready{l}") for l in LV]
            w_done, nw_ready, vn_done, vn_ready = S("w_done"), S("nw_ready"), S("vn_done"), S("vn_ready")
            o_done, sd_done, st_ready = S("o_done"), S("sd_done"), S("st_ready")
            osq_ready, osum1, osum_ready, ro_ready, on_ready = (S(n) for n in (
                "osq_ready", "osum1", "osum_ready", "ro_ready", "on_ready"))
            on_turned, ya_ready, mix_done, mix_read = S("on_turned"), S("ya_ready"), S("mix_done"), S("mix_read")
            stat1, mv_ready, mv2, rstd_ready, norm_ready = (S(n) for n in (
                "stat1", "mv_ready", "mv2", "rstd_ready", "norm_ready"))
            hn, h_ready, h_out, h_turned, hT_ready = S("hn"), S("h_ready"), S("h_out"), S("h_turned"), S("hT_ready")
            lg_done, lg_ready, delta_out, sst_in = S("lg_done"), S("lg_ready"), S("delta_out"), S("sst_in")
            diag0, vseq_ready, ds_done, ds_ready, dsc = (S(n) for n in (
                "diag0", "vseq_ready", "ds_done", "ds_ready", "dsc"))

            def tiles(e, step):
                step(-1, "prompt", None, None, False)
                step(0, "prompt", "prompt", None, False)
                step(1, "prompt", "prompt", "prompt", False)
                with e.Fori(2, PT - 1) as t:
                    step(t, "prompt", "prompt", "prompt", True)
                step(PT - 1, "sample", "prompt", "prompt", True)
                step(PT, None, "sample", "prompt", True)
                step(PT + 1, None, None, "sample", True)
                step(PT + 2, None, None, None, True)

            def levels_of(invert):
                return {"prompt": LV, "sample": LV_S, None: ()}[invert]

            with nc.Block() as block:
                @block.sync
                def _(e):
                    def load_qk(t):
                        sp.dma_start(stage[:, 0:2 * H, :], qkvT[:, 0:2 * H, ds(t * P, P)]).then_inc(stage_in, 16)

                    def load_v(t):
                        sp.dma_start(stage[:, 2 * H:, :], qkvT[:, 2 * H:, ds(t * P, P)]).then_inc(stage_v_in, 16)

                    def load_yb(t):
                        sp.dma_start(ybt[:, :, :], yb_d[:, :, ds(t * P, P)].rearrange("g p t -> p g t")
                                     ).then_inc(yb_in, 16)

                    load_qk(0)
                    load_v(0)
                    load_yb(0)
                    sp.dma_start(xt[:, :], x_d[0, 0:P, :]).then_inc(xt_in, 16)
                    sp.dma_start(wout[:, :, :], w_out_d[0].rearrange("(k p) n -> p k n", p=P)).then_inc(wo_in, 16)

                    def step(t, prepare, invert, apply, route):
                        if prepare == "prompt":
                            e.wait_ge(turned, t + 2)
                            load_qk(t + 2)
                        if prepare and invert:
                            e.wait_ge(v_turned, t + 1)
                            load_v(t + 1)
                        if prepare == "sample":
                            e.wait_ge(stage_in, 16 * NT)
                            e.wait_ge(stage_v_in, 16 * NT)
                            for s in range(NSEQ):
                                sp.dma_start(st_s[:, :, s, :], sdelta_d[0, s].rearrange("h d e -> d h e")
                                             ).then_inc(sst_in, 16)
                        if invert and apply:
                            e.wait_ge(mix_done, t)
                            load_yb(t)
                            e.wait_ge(norm_ready, t)
                            if invert == "prompt":
                                sp.dma_start(xt[:, :], x_d[0, ds(t * P, P), :]).then_inc(xt_in, 16)
                            else:
                                sp.dma_start(xt[0:NS, :], xs_d.rearrange("s t d -> (s t) d")).then_inc(xt_in, 16)
                        if invert == "sample":
                            e.wait_ge(st_ready, PT + 1)
                            sp.dma_start(dp_o[0, 0].rearrange("h d e -> d h e"), st[:, :, :]).then_inc(delta_out, 16)
                        if apply:
                            e.wait_ge(h_ready, t)
                            sp.dma_start(h_d[ds(t * P - P, P), :], h[:, :]).then_inc(h_out, 16)
                    tiles(e, step)
                    for hh in range(H):
                        e.wait_ge(ds_ready, hh + 1)
                        sp.dma_start(dsm_o[0, :, hh].rearrange("s d e -> d s e"), st_s[:, hh, :, :]
                                     ).then_inc(delta_out, 16)
                    e.wait_ge(delta_out, 16 * (1 + H))
                    e.wait_ge(h_out, 16 * NT)

                @block.gpsimd
                def _(e):
                    pool.memset(st[:, :, :], 0.0).then_inc(st_ready, 1)

                    def per_head(a, t):
                        return bc(a[:, ds(t, 1), :].rearrange("p a h -> p (a h)"), P)

                    def step(t, prepare, invert, apply, route):
                        n = t + 1
                        if prepare:
                            wait(e, decay_sum, n)
                            tri = C("tri") if prepare == "prompt" else C("tri_s")
                            pool.tensor_tensor(gtri[:, :, :], mid(tri, H), per_head(gdec, n), ALU.mult
                                               ).then_inc(gtri_ready, 1)
                        if invert:
                            e.wait_ge(tok_ready, n)
                            if apply:
                                e.wait_ge(sd_done, t)
                            pool.tensor_tensor(kbg[:, :, :], kb[:, :, :], per_head(egc, t), ALU.mult)
                            pool.tensor_tensor(kd[:, :, :], kh[:, :, :], per_head(edec, t), ALU.mult
                                               ).then_inc(kk_ready, 1)
                        if apply:
                            e.wait_ge(osum_ready, t)
                            pool.tensor_tensor(ro[:, 0:H], osum[:, 0:H], mhalf[:, 0:H], ALU.pow).then_inc(ro_ready, 1)
                        if prepare:
                            e.wait_ge(exp_ready, n + 1)
                            pool.tensor_tensor(dT[:, :, :], dT[:, :, :], mid(tri, H), ALU.mult).then_inc(decay_ready, 1)
                            e.wait_ge(ssq_ready, n + 1)
                            pool.tensor_tensor(rn[:, :], ssq[:, :], mhalf[:, 0:2 * H], ALU.pow).then_inc(rn_ready, 1)
                        if prepare and not invert:
                            e.dma_start(wr[:, :, 0:G], wrg_d[0].rearrange("(k p) n -> p k n", p=P)).then_inc(wr_in, 16)
                            e.dma_start(wr[:, :, G:], wre_d[0].rearrange("(k p) n -> p k n", p=P)).then_inc(wr_in, 16)
                            e.dma_start(brt[:, 0:G], brg_d.broadcast_to((P, G))).then_inc(wr_in, 16)
                            e.dma_start(brt[:, G:], bre_d.broadcast_to((P, NE))).then_inc(wr_in, 16)
                            e.dma_start(lng[:, :], ln1g_d.broadcast_to((P, D))).then_inc(ln_in, 16)
                            e.dma_start(lnb[:, :], ln1b_d.broadcast_to((P, D))).then_inc(ln_in, 16)
                        if prepare == "sample":
                            e.wait_ge(stage_in, 16 * NT)
                            e.wait_ge(stage_v_in, 16 * NT)
                            pool.memset(nwD, 0.0)
                            pool.memset(qgD, 0.0).then_inc(diag0, 1)
                        if apply:
                            e.wait_ge(mv2, t)
                            pool.tensor_tensor(rstd[:, :], mv[:, 1:2], mhalf[:, 0:1], ALU.pow).then_inc(rstd_ready, 1)
                        if apply == "prompt":
                            e.wait_ge(ln_in, 32)
                            e.wait_ge(norm_ready, t)
                            pool.tensor_tensor(h[:, :], h[:, :], lnb[:, :], ALU.add).then_inc(h_ready, 1)
                    tiles(e, step)

                @block.tensor
                def _(e):
                    def turn(bank, src):
                        for hh in range(H):
                            last = pe.transpose(bank[:, hh * P:(hh + 1) * P], src(hh), C("ident"))
                        return last

                    def step(t, prepare, invert, apply, route):
                        n = t + 1
                        m = NS if apply == "sample" else P
                        levels = levels_of(invert)

                        def mix(k):
                            src, kk = (ybt, k - H) if k >= H else (yaT, k)
                            for half in range(2):
                                last = pe.matmul(b[6 + half][:, :], src[:, kk, :],
                                                 wout[:, k, half * 512:(half + 1) * 512],
                                                 start=(k == H), stop=(k == H - 1))
                            return last

                        def sample_states(hh):
                            e.wait_ge(vseq_ready, hh + 1)
                            if hh >= 2:
                                e.wait_ge(ds_ready, hh - 1)
                            for half, bank in enumerate((b[0], b[1]) if hh % 2 == 0 else (b[2], b[5])):
                                last = pe.matmul(bank[:, :], kd[0:m, hh, :],
                                                 vseq[hh % 2][:, half * H:(half + 1) * H, :].rearrange(
                                                     "p s e -> p (s e)"), start=True, stop=True)
                            last.then_inc(ds_done, 1)

                        def beside_level(l):
                            if l == 0 and prepare:
                                e.wait_ge(gtri_ready, n + 1)
                                pe.matmul(b[4][:, :], C("ones"), gtri[:, :, :].rearrange("p h t -> p (h t)"),
                                          start=True, stop=True).then_inc(decay_sum, 1)
                            if l == 0 and route:
                                e.wait_ge(hT_ready, t - 1)
                                e.wait_ge(wr_in, 64)
                                for k in range(KT):
                                    last = pe.matmul(b[7][:, 0:G + NE], hT[:, k, :], wr[:, k, :],
                                                     start=(k == 0), stop=(k == KT - 1))
                                last.then_inc(lg_done, 1)
                            if l == 1 and apply:
                                if route:
                                    e.wait_ge(lg_ready, t - 1)
                                e.wait_ge(wo_in, 16)
                                e.wait_ge(yb_in, 16 * t)
                                mix(H)
                                mix(H + 1)
                            if l == 2 and apply:
                                e.wait_ge(on_ready, t)
                                e.wait_ge(st_ready, t + 1 if apply == "prompt" else PT + 1)
                                turn(b[3], lambda hh: on[:, hh, :]).then_inc(on_turned, 1)
                            if l == 2 and prepare:
                                e.wait_ge(stage_in, 16 * (n + 1))
                                e.wait_ge(sum_read, n + 1)
                                turn(b[4], lambda hh: stage[:, hh, :])
                                turn(b[5], lambda hh: stage[:, H + hh, :]).then_inc(turned, 1)
                            if l == 3 and apply:
                                mix(H + 2)
                                mix(H + 3)
                            if l == 4:
                                if apply:
                                    e.wait_ge(ya_ready, t)
                                if invert:
                                    e.wait_ge(stage_v_in, 16 * n)
                                    turn(b[3], lambda hh: stage[:, 2 * H + hh, :]).then_inc(v_turned, 1)
                                if apply:
                                    mix(0)
                                    mix(1)
                            if l == 5 and apply:
                                mix(2)
                            if apply == "sample" and l in (2, 3):
                                sample_states(l - 2)

                        if apply:
                            e.wait_ge(kk_ready, t)
                            e.wait_ge(vb_ready, t)
                            e.wait_ge(xt_ready[len(levels_of(apply)) - 1], t)
                            for hh in range(H):
                                last = pe.matmul(b[3][:, hh * P:(hh + 1) * P], kbg[:, hh, :], XT[:, hh, :],
                                                 start=True, stop=True)
                            last.then_inc(w_done, 1)
                        if invert:
                            e.wait_ge(tok_ready, n)
                            turn(b[0], lambda hh: kh[:, hh, :])
                            turn(b[1], lambda hh: kb[:, hh, :])
                            turn(b[2], lambda hh: qh[:, hh, :])
                            if route:
                                e.wait_ge(mix_read, t - 1)
                            turn(b[6], lambda hh: qg[:, hh, :]).then_inc(turned2, 1)
                            e.wait_ge(sum_read, n)
                        if apply:
                            e.wait_ge(nw_ready, t)
                        if apply == "prompt":
                            e.wait_ge(st_ready, t)
                            for hh in range(H):
                                c = slice(hh * P, (hh + 1) * P)
                                pe.matmul(b[4][:, c], XT[:, hh, :], vb[:, hh, :], start=True, stop=False)
                                last = pe.matmul(b[4][:, c], nwT[:, hh, :], st[:, hh, :], start=False, stop=True)
                            last.then_inc(vn_done, 1)
                        if invert:
                            e.wait_ge(ch_ready, n)
                            for bank, src in ((b[0], kbT), (b[1], qhT)):
                                for hh in range(H):
                                    last = pe.matmul(bank[:, hh * P:(hh + 1) * P], khT[:, hh, :], src[:, hh, :],
                                                     start=True, stop=True)
                            last.then_inc(ak_done, 1)
                        if apply == "prompt":
                            e.wait_ge(vn_ready, t)
                            e.wait_ge(qg_ready, t)
                            for hh in range(H):
                                c = slice(hh * P, (hh + 1) * P)
                                pe.matmul(b[5][:, c], qgT[:, hh, :], st[:, hh, :], start=True, stop=False)
                                last = pe.matmul(b[5][:, c], qk[:, hh, :], vn[:, hh, :], start=False, stop=True)
                            last.then_inc(o_done, 1)
                            for hh in range(H):
                                last = pe.matmul(b[3][:, hh * P:(hh + 1) * P], kd[:, hh, :], vn[:, hh, :],
                                                 start=True, stop=True)
                            last.then_inc(sd_done, 1)
                        if apply == "sample":
                            e.wait_ge(sst_in, 16 * NSEQ)
                            for hh in range(H):
                                c = slice(hh * P, (hh + 1) * P)
                                pe.matmul(b[4][0:m, c], XT[:, hh, 0:m], vb[:, hh, :], start=True, stop=False)
                                for s in range(NSEQ):
                                    last = pe.matmul(b[4][0:m, c], nwD[:, hh, s * NS:(s + 1) * NS],
                                                     st_s[:, hh, s, :], start=False, stop=(s == NSEQ - 1))
                            last.then_inc(vn_done, 1)
                            e.wait_ge(vn_ready, t)
                            e.wait_ge(qg_ready, t)
                            for hh in range(H):
                                c = slice(hh * P, (hh + 1) * P)
                                pe.matmul(b[5][0:m, c], qk[0:m, hh, 0:m], vn[0:m, hh, :], start=True, stop=False)
                                for s in range(NSEQ):
                                    last = pe.matmul(b[5][0:m, c], qgD[:, hh, s * NS:(s + 1) * NS],
                                                     st_s[:, hh, s, :], start=False, stop=(s == NSEQ - 1))
                            last.then_inc(o_done, 1)
                        if invert:
                            e.wait_ge(xt_first, n)
                            turn(b[2], lambda hh: XT[:, hh, :]).then_inc(x_turned2, 1)
                        if route:
                            if invert:
                                e.wait_ge(qg_ready, n)
                            else:
                                e.wait_ge(mix_read, t - 1)
                            e.wait_ge(h_ready, t - 1)
                            for k in range(KT):
                                bank, at = b[6 + k // H], (k % H) * P
                                last = pe.transpose(bank[:, at:at + P], h[:, k * P:(k + 1) * P], C("ident"))
                            last.then_inc(h_turned, 1)
                        elif apply:
                            e.wait_ge(qg_ready, n)
                        for l in range(len(LV)):
                            if l < len(levels):
                                e.wait_ge(x_ready[l], n)
                                for hh in range(H):
                                    last = pe.matmul(b[0][:, hh * P:(hh + 1) * P], aT[:, hh, :], X[:, hh, :],
                                                     start=True, stop=True)
                                last.then_inc(y_done[l], 1)
                            beside_level(l)
                            if l < len(levels):
                                e.wait_ge(y_ready[l], n)
                                if l > 0:
                                    e.wait_ge(xt_ready[l - 1], n)
                                if l < len(levels) - 1:
                                    for hh in range(H):
                                        last = pe.matmul(b[1][:, hh * P:(hh + 1) * P], XT[:, hh, :], Y[:, hh, :],
                                                         start=True, stop=True)
                                    last.then_inc(px_done[l], 1)
                                for hh in range(H):
                                    last = pe.matmul(b[2][:, hh * P:(hh + 1) * P], Y[:, hh, :], XT[:, hh, :],
                                                     start=True, stop=True)
                                last.then_inc(p_done[l], 1)
                        if apply:
                            mix(3).then_inc(mix_done, 1)
                        if apply == "sample":
                            sample_states(H - 2)
                            sample_states(H - 1)
                    tiles(e, step)

                @block.scalar
                def _(e):
                    def flat(a):
                        return a[:, :, :].rearrange("p h d -> p (h d)")

                    def step(t, prepare, invert, apply, route):
                        n = t + 1
                        m = NS if apply == "sample" else P
                        if apply:
                            e.wait_ge(w_done, t)
                        if apply == "prompt":
                            act.activation(flat(nwT), b[3][:, :], ACT.Copy, scale=-1.0).then_inc(nw_ready, 1)
                        if apply == "sample":
                            for hh in range(H):
                                last = act.activation(
                                    nwD[:, hh, :].rearrange("p (s c) -> p s c", c=NS + DSEQ)[:, :, 0:DSEQ],
                                    b[3][:, hh * P:hh * P + NS].rearrange("p (s r) -> p s r", r=DSEQ), ACT.Copy,
                                    scale=-1.0)
                            last.then_inc(nw_ready, 1)
                        if invert:
                            e.wait_ge(turned2, n)
                            act.activation(flat(khT), b[0][:, :], ACT.Copy)
                            act.activation(flat(kbT), b[1][:, :], ACT.Copy)
                            act.activation(flat(qhT), b[2][:, :], ACT.Copy).then_inc(ch_ready, 1)
                        if apply:
                            e.wait_ge(vn_done, t)
                            act.activation(flat(vn)[0:m], b[4][0:m, :], ACT.Copy).then_inc(vn_ready, 1)
                            e.wait_ge(o_done, t)
                        if invert == "prompt":
                            act.activation(flat(qgT), b[6][:, :], ACT.Copy).then_inc(qg_ready, 1)
                        if invert == "sample":
                            e.wait_ge(diag0, 1)
                            for hh in range(H):
                                last = act.activation(
                                    qgD[:, hh, :].rearrange("p (s c) -> p s c", c=NS + DSEQ)[:, :, 0:DSEQ],
                                    b[6][:, hh * P:hh * P + NS].rearrange("p (s r) -> p s r", r=DSEQ), ACT.Copy)
                            last.then_inc(qg_ready, 1)
                        if apply:
                            e.wait_ge(ssq_ready, n if invert else NT)
                            act.activation(sq[0:m, 0:DA], b[5][0:m, :], ACT.Square).then_inc(osq_ready, 1)
                        if invert:
                            e.wait_ge(x_turned2, n)
                            act.activation(flat(X), b[2][:, :], ACT.Copy).then_inc(x_ready[0], 1)
                        if route:
                            e.wait_ge(h_turned, t - 1)
                            act.activation(hT[:, 0:H, :].rearrange("p k t -> p (k t)"), b[6][:, :], ACT.Copy)
                            act.activation(hT[:, H:, :].rearrange("p k t -> p (k t)"), b[7][:, :], ACT.Copy
                                           ).then_inc(hT_ready, 1)
                        if prepare:
                            e.wait_ge(decay_sum, n + 1)
                            if invert:
                                e.wait_ge(y_ready[0], n)
                            for hh in range(H):
                                last = act.activation(dT[:, hh, :], b[4][:, hh * P:(hh + 1) * P], ACT.Relu, scale=-1.0,
                                                      bias=gc[:, ds(n, 1), hh:hh + 1].rearrange("p a h -> p (a h)"))
                            last.then_inc(sum_read, 1)
                            e.wait_ge(sum_read, n + 1)
                            act.activation(flat(dT), flat(dT), ACT.Exp, scale=-1.0).then_inc(exp_ready, 1)
                            e.wait_ge(turned, n + 1)
                            if apply:
                                e.wait_ge(osum_ready, t)
                            act.activation(sq[:, 0:DA], b[4][:, :], ACT.Square)
                            act.activation(sq[:, DA:], b[5][:, :], ACT.Square).then_inc(sq_ready, 1)
                    tiles(e, step)

                @block.vector
                def _(e):
                    def col(a, t):
                        return a[:, ds(t, 1), :].rearrange("p a h -> p (a h)")

                    def step(t, prepare, invert, apply, route):
                        n = t + 1
                        u = t - 1
                        m = NS if apply == "sample" else P
                        levels = levels_of(invert)

                        def scale_states(hh):
                            if hh >= 2:
                                e.wait_ge(ds_done, hh - 1)
                            dve.tensor_tensor(vseq[hh % 2], mid(vn[0:NS, hh, :], NSEQ), bc(C("seqmask")[0:NS], P),
                                              ALU.mult).then_inc(vseq_ready, 1)
                            eg = eglast_s[:, :, hh:hh + 1].rearrange("p s h -> p (s h)")
                            e.wait_ge(o_done, NT)
                            dve.tensor_tensor(st_s[:, hh], st_s[:, hh], bc(eg, P), ALU.mult).then_inc(dsc, 1)

                        def add_states(hh):
                            e.wait_ge(ds_done, hh + 1)
                            e.wait_ge(dsc, hh + 1)
                            for half, bank in enumerate((b[0], b[1]) if hh % 2 == 0 else (b[2], b[5])):
                                c = slice(half * H, (half + 1) * H)
                                last = dve.tensor_tensor(st_s[:, hh, c, :], st_s[:, hh, c, :], heads(bank), ALU.add)
                            last.then_inc(ds_ready, 1)

                        def beside_level(l):
                            if l == 0 and apply:
                                e.wait_ge(osq_ready, t)
                                dve.tensor_reduce(osum[0:m, 0:H], sq[0:m, 0:DA].rearrange("p (h d) -> p h d", d=P),
                                                  AX.X, ALU.add).then_inc(osum1, 1)
                                e.wait_ge(osum1, t)
                                dve.tensor_scalar(osum[0:m, 0:H], osum[0:m, 0:H], 1.0 / HD, RMS_EPS, ALU.mult, ALU.add
                                                  ).then_inc(osum_ready, 1)
                            if l == 1 and apply == "prompt":
                                e.wait_ge(sd_done, t)
                                for hh in range(H):
                                    last = dve.scalar_tensor_tensor(
                                        out=st[:, hh, :], in0=st[:, hh, :],
                                        scalar=eglast[:, ds(u, 1), hh:hh + 1].rearrange("p a h -> p (a h)"),
                                        in1=b[3][:, hh * P:(hh + 1) * P], op0=ALU.mult, op1=ALU.add)
                                last.then_inc(st_ready, 1)
                            if l == 1 and apply:
                                e.wait_ge(ro_ready, t)
                                dve.tensor_tensor(on[0:m], heads(b[5])[0:m], bc(ro[0:m, 0:H], P), ALU.mult
                                                  ).then_inc(on_ready, 1)
                            if l == 3 and apply:
                                e.wait_ge(on_turned, t)
                                dve.scalar_tensor_tensor(out=yaT[:, :, :], in0=heads(b[3]), scalar=gnw[:, :],
                                                         in1=szT[:, :, ds(u * P, P)], op0=ALU.mult, op1=ALU.mult
                                                         ).then_inc(ya_ready, 1)
                            if apply == "sample" and l in (1, 2):
                                scale_states(l - 1)
                            if apply == "sample" and l in (3, 4):
                                scale_states(l - 1)
                                add_states(l - 3)
                            if l == 3 and prepare:
                                e.wait_ge(sq_ready, n + 1)
                                dve.tensor_reduce(ssq[:, :], sq[:, :].rearrange("p (h d) -> p h d", d=P), AX.X, ALU.add
                                                  ).then_inc(scc, 1)
                                e.wait_ge(scc, 3 * n + 1)
                                dve.tensor_scalar(ssq[:, :], ssq[:, :], L2_EPS, None, ALU.add).then_inc(ssq_ready, 1)
                            if l == 4 and prepare:
                                e.wait_ge(rn_ready, n + 1)
                                if invert:
                                    e.wait_ge(kk_ready, n)
                                dve.tensor_scalar(sc[:, 0, :], rn[:, 0:H], HD ** -0.5, None, ALU.mult).then_inc(scc, 1)
                                dve.tensor_tensor(sc[:, 2, :], rn[:, H:], col(beta, n), ALU.mult)
                                e.wait_ge(scc, 3 * n + 2)
                                dve.tensor_tensor(sc[:, 1, :], sc[:, 0, :], col(egc, n), ALU.mult).then_inc(scc, 1)
                                dve.tensor_tensor(kh[:, :, :], heads(b[5]), bc(rn[:, H:], P), ALU.mult)
                                dve.tensor_tensor(qh[:, :, :], heads(b[4]), bc(sc[:, 0, :], P), ALU.mult)

                            if l == 5 and prepare:
                                e.wait_ge(scc, 3 * n + 3)
                                dve.tensor_tensor(kb[:, :, :], heads(b[5]), bc(sc[:, 2, :], P), ALU.mult)
                                dve.tensor_tensor(qg[:, :, :], heads(b[4]), bc(sc[:, 1, :], P), ALU.mult
                                                  ).then_inc(tok_ready, 1)
                            if l == 5 and invert:
                                e.wait_ge(v_turned, n)
                                dve.tensor_tensor(vb[:, :, :], heads(b[3]), bc(col(beta, t), P), ALU.mult
                                                  ).then_inc(vb_ready, 1)

                        if invert:
                            e.wait_ge(ak_done, n)
                            e.wait_ge(decay_ready, n)
                            dve.tensor_tensor(aT[:, :, :], heads(b[0]), dT[:, :, :], ALU.mult).then_inc(a_ready, 1)
                            e.wait_ge(a_ready, n)
                            dve.tensor_tensor(Y[:, :, :], aT[:, :, :], mid(C("m1t"), H), ALU.mult).then_inc(m1c, 1)
                            e.wait_ge(m1c, n)
                            if apply:
                                e.wait_ge(vn_done, t)
                            dve.tensor_tensor(XT[:, :, :], mid(C("ident"), H), Y[:, :, :], ALU.subtract
                                              ).then_inc(xt_first, 1)
                            if apply:
                                e.wait_ge(o_done, t)
                            dve.tensor_tensor(qk[:, :, :], heads(b[1]), dT[:, :, :], ALU.mult)
                        for l in range(len(LV)):
                            if l < len(levels):
                                e.wait_ge(y_done[l], n)
                                dve.tensor_tensor(Y[:, :, :], heads(b[0]), mid(C(f"m{levels[l]}"), H), ALU.mult
                                                  ).then_inc(y_ready[l], 1)
                            beside_level(l)
                            if l < len(levels) - 1:
                                e.wait_ge(px_done[l], n)
                                dve.tensor_tensor(X[:, :, :], X[:, :, :], heads(b[1]), ALU.subtract
                                                  ).then_inc(x_ready[l + 1], 1)
                            if l < len(levels):
                                e.wait_ge(p_done[l], n)
                                dve.tensor_tensor(XT[:, :, :], XT[:, :, :], heads(b[2]), ALU.subtract
                                                  ).then_inc(xt_ready[l], 1)
                            if l == 0 and route:
                                e.wait_ge(lg_done, t - 1)
                                dve.tensor_tensor(col(logits, t - 2), b[7][:, 0:G + NE], brt[:, :], ALU.add
                                                  ).then_inc(lg_ready, 1)
                        if apply:
                            e.wait_ge(mix_done, t)
                            e.wait_ge(xt_in, 16 * t)
                            for half in range(2):
                                c = slice(half * 512, (half + 1) * 512)
                                last = dve.scalar_tensor_tensor(out=xt[:, c], in0=xt[:, c], scalar=ALPHA,
                                                                in1=b[6 + half][:, :], op0=ALU.mult, op1=ALU.add)
                                last.then_inc(mix_read if half else stat1, 1)
                            e.wait_ge(stat1, 2 * t - 1)
                            dve.bn_stats(stats[:, 0, :], xt[:, 0:512])
                            e.wait_ge(mix_read, t)
                            dve.bn_stats(stats[:, 1, :], xt[:, 512:]).then_inc(stat1, 1)
                            e.wait_ge(stat1, 2 * t)
                            dve.memset(spare[:, :], 0.0)
                            dve.bn_aggr(mv[:, :], stats[:, :, :].rearrange("p a b -> p (a b)")).then_inc(mv_ready, 1)
                            e.wait_ge(mv_ready, t)
                            dve.tensor_scalar(mv[:, 1:2], mv[:, 1:2], LN_EPS, None, ALU.add).then_inc(mv2, 1)
                            e.wait_ge(rstd_ready, t)
                            if route:
                                e.wait_ge(h_turned, t - 1)
                                e.wait_ge(h_out, 16 * (t - 1))
                            dve.tensor_scalar(h[:, :], xt[:, :], mv[:, 0:1], rstd[:, :], ALU.subtract, ALU.mult
                                              ).then_inc(hn, 1)
                            e.wait_ge(ln_in, 32)
                            e.wait_ge(hn, t)
                            dve.tensor_tensor(h[:, :], h[:, :], lng[:, :], ALU.mult).then_inc(norm_ready, 1)
                        if apply == "sample":
                            e.wait_ge(norm_ready, NT)
                            dve.tensor_tensor(h[:, :], h[:, :], lnb[:, :], ALU.add).then_inc(h_ready, 1)
                        if apply == "sample":
                            add_states(H - 2)
                            add_states(H - 1)
                    tiles(e, step)

        order = sb("order", [1, NTILES, 2], I32)
        pairs = sb("pairs", [1, 1], I32)
        wgu = [[sb(f"wgu{s}{i}", [P, KT, 2 * FE]) for i in range(2)] for s in range(2)]
        spare_sz = szT[:, :, :].rearrange("p h t -> p (h t)")
        wdn = [[sb(f"wdn{i}", [P, FE // P, D])[:, :, :] for i in range(2)],
               [spare_sz[:, i * 2 * D:(i + 1) * 2 * D].rearrange("p (c d) -> p c d", d=D) for i in range(2)]]
        hres = qkvT[:, :, :].rearrange("p c t -> p (c t)")[:, 0:NT * D].rearrange("p (t d) -> p t d", d=D)
        kept = phase(whole)
        gu_in, dn_in = ([[kept(f"{n}{s}{i}") for i in range(2)] for s in range(2)] for n in ("gu_in", "dn_in"))
        wgu_v = [w[0].rearrange("g n (k p) f -> (g n) p k f", p=P) for w in (wg_d, wu_d)]
        wdn_v = wd_d[0].rearrange("g n (k p) f -> (g n) p k f", p=P)

        def load_gu(s, k, expert):
            for j in range(2):
                sp.dma_start(wgu[s][k][:, :, j * FE:(j + 1) * FE],
                             wgu_v[j][ds(expert, 1)].rearrange("a p k f -> (a p) k f")).then_inc(gu_in[s][k], 16)

        def load_dn(s, k, expert):
            sp.dma_start(wdn[s][k], wdn_v[ds(expert, 1)].rearrange("a p k f -> (a p) k f")
                         ).then_inc(dn_in[s][k], 16)

        with ExitStack() as c3:
            def tmp(name, shape, dt=F32):
                return sb(name, shape, dt, ctx=c3)
            NG = [P, NT, G]
            mx, sm, pg, dl, ex = (tmp(n, [P, NT]) for n in ("mx", "sm", "pg", "dl", "ex"))
            ga, gb, ohg = tmp("ga", NG), tmp("gb", NG), tmp("ohg", NG)
            lem = tmp("lem", [P, NT, G, EPG])
            les, ea, oh1, oh2 = (tmp(n, [P, NT, EPG]) for n in ("les", "ea", "oh1", "oh2"))
            pick = [tmp(f"pick{k}", [P, NT, NE]) for k in range(2)]
            both, pos, work = (tmp(n, [P, NT, NE]) for n in ("both", "pos", "work"))
            base = tmp("base", [P, NT + 1, NE])
            slotf = tmp("slotf", [P, 2, NT])
            sloti = tmp("sloti", [P, 2, NT], I32)
            entry = tmp("entry", [P, 2, NT, 4], I32)
            nov, cuma, cumb = (tmp(n, [P, NE]) for n in ("nov", "cuma", "cumb"))
            cmpm = tmp("cmpm", [P, MAXOV, NE])
            ove, ovs = tmp("ove", [P, MAXOV]), tmp("ovs", [P, MAXOV])
            par1 = tmp("par1", [P, MAXOV // 2])
            par2 = tmp("par2", [P, 1])
            empty = tmp("empty", [P, NLIST * SLOTS // P, 4], I32)
            pp = pb("pp", [P, NT * NE], c3)
            pt = pb("pt", [P, NT * NE], c3)
            S = phase(c3)
            chn, filled, emptied, hres_in = S("chn"), S("filled"), S("emptied"), S("hres_in")
            ga_ready, ex_ready, dl_ready, eex_ready = S("ga_ready"), S("ex_ready"), S("dl_ready"), S("eex_ready")
            both_ready, counted, entries_ready, listed = S("both_ready"), S("counted"), S("entries_ready"), S("listed")

            with nc.Block() as block:
                @block.sync
                def _(e):
                    e.wait_ge(filled, 2)
                    sp.dma_start(tab_d.rearrange("(p n) c -> p (n c)", p=P),
                                 empty[:, :, :].rearrange("p n c -> p (n c)")).then_inc(emptied, 16)
                    for k in range(2):
                        load_gu(1, k, k)
                        load_dn(1, k, k)
                    for t in range(NT):
                        sp.dma_start(hres[:, t, :], h_d[t * P:(t + 1) * P, :]).then_inc(hres_in, 16)
                    e.wait_ge(emptied, 16)
                    e.wait_ge(hres_in, 16 * NT)

                @block.gpsimd
                def _(e):
                    pool.memset(empty[:, :, 0:2], SKIP).then_inc(filled, 1)
                    pool.memset(empty[:, :, 2:4], 0).then_inc(filled, 1)
                    e.wait_ge(emptied, 16)
                    for k in range(2):
                        e.wait_ge(entries_ready, 3 + k)
                        for t in range(NT):
                            pool.indirect_dma_start(tab_d, bass.IndirectOffsetOnAxis(ap=sloti[:, k, t:t + 1], axis=0),
                                                    entry[:, k, t, :], None, bounds_check=NLIST * SLOTS - 1,
                                                    oob_is_err=False).then_inc(listed, 16)
                    e.wait_ge(listed, 16 * 2 * NT)

                @block.tensor
                def _(e):
                    e.wait_ge(both_ready, 1)
                    flat = both[:, :, :].rearrange("p t n -> p (t n)")
                    pe.matmul(pp[:, :], C("strict"), flat, start=True, stop=True)
                    pe.matmul(pt[:, :], C("ones"), flat, start=True, stop=True).then_inc(counted, 1)

                @block.scalar
                def _(e):
                    e.wait_ge(ga_ready, 1)
                    act.activation(gb[:, :, :], ga[:, :, :], ACT.Exp).then_inc(ex_ready, 1)
                    e.wait_ge(dl_ready, 1)
                    act.activation(ex[:, :], dl[:, :], ACT.Exp).then_inc(eex_ready, 1)

                @block.vector
                def _(e):
                    chain = [0]

                    def link(ins):
                        chain[0] += 1
                        ins.then_inc(chn, 1)
                        e.wait_ge(chn, chain[0])

                    def wide(a, m):
                        return mid(a, NT)

                    def first_max(values, n, top, scratch, onehot):
                        link(dve.tensor_reduce(top, values, AX.X, ALU.max))
                        link(dve.tensor_tensor(scratch, values, bc(top, n), ALU.is_equal))
                        link(dve.tensor_tensor(scratch, scratch, mid(C(f"w{n}"), NT), ALU.mult))
                        link(dve.tensor_reduce(sm[:, :], scratch, AX.X, ALU.max))
                        link(dve.tensor_tensor(onehot, scratch, bc(sm[:, :], n), ALU.is_equal))

                    lg = logits[:, :, 0:G]
                    first_max(lg, G, mx[:, :], ga[:, :, :], ohg[:, :, :])
                    dve.tensor_tensor(ga[:, :, :], lg, bc(mx[:, :], G), ALU.subtract).then_inc(ga_ready, 1)
                    e.wait_ge(ex_ready, 1)
                    link(dve.tensor_reduce(pg[:, :], gb[:, :, :], AX.X, ALU.add))
                    link(dve.reciprocal(pg[:, :], pg[:, :]))
                    le = logits[:, :, G:].rearrange("p t (g n) -> p t g n", n=EPG)
                    link(dve.tensor_tensor(lem[:, :, :, :], le, bc(ohg[:, :, :], EPG), ALU.mult))
                    link(dve.tensor_tensor(les[:, :, :], lem[:, :, 0, :], lem[:, :, 1, :], ALU.add))
                    link(dve.tensor_tensor(les[:, :, :], les[:, :, :], lem[:, :, 2, :], ALU.add))
                    link(dve.tensor_tensor(les[:, :, :], les[:, :, :], lem[:, :, 3, :], ALU.add))
                    first_max(les[:, :, :], EPG, mx[:, :], ea[:, :, :], oh1[:, :, :])
                    link(dve.tensor_copy(dl[:, :], mx[:, :]))
                    link(dve.scalar_tensor_tensor(out=les[:, :, :], in0=oh1[:, :, :], scalar=NEG, in1=les[:, :, :],
                                                  op0=ALU.mult, op1=ALU.add))
                    first_max(les[:, :, :], EPG, mx[:, :], ea[:, :, :], oh2[:, :, :])
                    dve.tensor_tensor(dl[:, :], mx[:, :], dl[:, :], ALU.subtract).then_inc(dl_ready, 1)
                    for k, oh in enumerate((oh1, oh2)):
                        p4 = pick[k][:, :, :].rearrange("p t (g n) -> p t g n", n=EPG)
                        last = dve.tensor_tensor(p4, bc(ohg[:, :, :], EPG),
                                                 oh[:, :, :].unsqueeze(2).broadcast_to((P, NT, G, EPG)), ALU.mult)
                    link(last)
                    for k in range(2):
                        last = dve.tensor_scalar(pick[k][:, PT, :], pick[k][:, PT, :], C("valid")[:, PT:PT + 1], None,
                                                 ALU.mult)
                    link(last)
                    dve.tensor_tensor(both[:, :, :], pick[0][:, :, :], pick[1][:, :, :], ALU.add
                                      ).then_inc(both_ready, 1)
                    e.wait_ge(eex_ready, 1)
                    link(dve.tensor_scalar(sm[:, :], ex[:, :], 1.0, None, ALU.add))
                    link(dve.reciprocal(sm[:, :], sm[:, :]))
                    link(dve.tensor_tensor(sm[:, :], sm[:, :], pg[:, :], ALU.mult))
                    dve.tensor_copy(entry[:, 0, :, 2].bitcast(F32), sm[:, :])
                    dve.tensor_tensor(entry[:, 1, :, 2].bitcast(F32), sm[:, :], ex[:, :], ALU.mult
                                      ).then_inc(entries_ready, 1)
                    for k in range(2):
                        dve.tensor_copy(entry[:, k, :, 3], C("token"))
                        dve.tensor_copy(entry[:, k, :, 1], C("token"))
                        last = dve.tensor_scalar(entry[:, k, :, 0], C("token"), 2.0, float(k), ALU.mult, ALU.add)
                    last.then_inc(entries_ready, 1)
                    e.wait_ge(counted, 1)
                    tot = pt[:, :].rearrange("p (t n) -> p t n", n=NE)
                    link(dve.memset(base[:, 0, :], 0.0))
                    for t in range(NT):
                        link(dve.tensor_tensor(base[:, t + 1, :], base[:, t, :], tot[:, t, :], ALU.add))
                    link(dve.tensor_tensor(pos[:, :, :], base[:, 0:NT, :],
                                           pp[:, :].rearrange("p (t n) -> p t n", n=NE), ALU.add))
                    link(dve.tensor_tensor(pos[:, :, :], pos[:, :, :], mid(C("slot0"), NT), ALU.add))
                    for k in range(2):
                        link(dve.tensor_tensor(work[:, :, :], pick[k][:, :, :], pos[:, :, :], ALU.mult))
                        link(dve.tensor_reduce(slotf[:, k, :], work[:, :, :], AX.X, ALU.add))
                        link(dve.tensor_tensor(slotf[:, k, :], slotf[:, k, :], C("skip"), ALU.add))
                        dve.tensor_copy(sloti[:, k, :], slotf[:, k, :]).then_inc(entries_ready, 1)

                    cnt = base[:, NT, :]
                    link(dve.memset(nov[:, :], 0.0))
                    for j in range(1, NT):
                        link(dve.scalar_tensor_tensor(out=nov[:, :], in0=cnt, scalar=float(j * P), in1=nov[:, :],
                                                      op0=ALU.is_gt, op1=ALU.add))
                    src, dst = cuma, cumb
                    link(dve.tensor_copy(src[:, :], nov[:, :]))
                    for sh in (1, 2, 4, 8, 16):
                        dve.tensor_copy(dst[:, 0:sh], src[:, 0:sh])
                        link(dve.tensor_tensor(dst[:, sh:], src[:, sh:], src[:, 0:NE - sh], ALU.add))
                        src, dst = dst, src
                    link(dve.tensor_tensor(cmpm[:, :, :], mid(src[:, :], MAXOV), bc(C("rank"), NE), ALU.is_le))
                    link(dve.tensor_reduce(ove[:, :], cmpm[:, :, :], AX.X, ALU.add))
                    link(dve.tensor_tensor(cmpm[:, :, :], cmpm[:, :, :], mid(nov[:, :], MAXOV), ALU.mult))
                    link(dve.tensor_reduce(ovs[:, :], cmpm[:, :, :], AX.X, ALU.add))
                    link(dve.tensor_tensor(ovs[:, :], C("rank"), ovs[:, :], ALU.subtract))
                    link(dve.tensor_scalar(ovs[:, :], ovs[:, :], float(P), float(P), ALU.mult, ALU.add))
                    link(dve.scalar_tensor_tensor(out=ovs[:, :], in0=ove[:, :], scalar=float(SLOTS), in1=ovs[:, :],
                                                  op0=ALU.mult, op1=ALU.add))
                    link(dve.tensor_scalar(ovs[:, :], ovs[:, :], float(NE * SLOTS), None, ALU.min))
                    link(dve.tensor_scalar(ove[:, :], ove[:, :], float(NE - 1), None, ALU.min))
                    dve.tensor_copy(order[0:1, NE:, 0], ove[0:1, :])
                    dve.tensor_copy(order[0:1, NE:, 1], ovs[0:1, :])
                    dve.tensor_copy(order[0:1, 0:NE, 1], C("slot0")[0:1, :])
                    link(dve.tensor_scalar(order[0:1, 0:NE, 0], C("slot0")[0:1, :], 1.0 / SLOTS, 0.25, ALU.mult,
                                           ALU.add))
                    link(dve.tensor_tensor(par1[:, :], src[:, NE - 1:NE].broadcast_to((P, MAXOV // 2)), C("even"),
                                           ALU.is_gt))
                    link(dve.tensor_reduce(par2[:, :], par1[:, :], AX.X, ALU.add))
                    link(dve.tensor_scalar(pairs[0:1, :], par2[0:1, :], 1.0, None, ALU.max))

        with ExitStack() as c4:
            pr = range(2)

            def two(name, shape, dt=F32):
                return [sb(f"{name}{k}", shape, dt, ctx=c4) for k in pr]
            idg = two("idg", [P, 4], I32)
            ids = [two(f"ids{s}", [P, 4], I32) for s in pr]
            xg, xgT = two("xg", [P, D]), two("xgT", [P, KT, P])
            sg, ac, acT = two("sg", [P, FE]), two("ac", [P, FE]), two("acT", [P, FE // P, P])
            yo = two("yo", [P, D])
            spare = sb("spare4", [P, 4], ctx=c4)
            b = [pb(f"e{i}", [P, 512], c4) for i in range(8)]
            S = phase(c4)
            S2 = lambda n: [S(f"{n}{i}") for i in pr]
            idg_in, gathered, cleared = S2("idg_in"), S2("gathered"), S("cleared")
            ids_in = [S2(f"ids_in{s}") for s in pr]
            xg_turned, xgT_ready, gu_done, silu_ready = S2("xg_turned"), S2("xgT_ready"), S2("gu_done"), S2("silu_ready")
            ac_ready, ac_turned, acT_ready, dn_done = S2("ac_ready"), S2("ac_turned"), S2("acT_ready"), S2("dn_done")
            yo_ready, scattered, carried = S2("yo_ready"), S2("scattered"), S("carried")

            def pair_loop(e, head, body, tail=None):
                main = NE // 2
                more = e.value_load(pairs[0:1, 0:1], min_val=1, max_val=MAXOV // 2 - 1)
                head()
                body(1, (0, 0), (1, 0))
                with e.Fori(1, main // 2) as j:
                    body(2 * j, (1, j), (0, j - 1))
                    body(2 * j + 1, (0, j), (1, j))
                with e.Fori(0, more) as q:
                    body(q + main, (0, q + main // 2), (0, q + main // 2 - 1))
                if tail:
                    tail(more + main - 1, (0, more + main // 2 - 1))

            def tile_entry(e, i, k, field, top):
                return e.value_load(order[0:1, ds(2 * i + k, 1), field], min_val=0, max_val=top)

            with nc.Block() as block:
                @block.sync
                def _(e):
                    def load_ids(i, k, s, free):
                        row = tile_entry(e, i, k, 1, NE * SLOTS)
                        wait(e, scattered[k], free)
                        sp.dma_start(ids[s][k][:, :], tab_d[ds(row, P), :]).then_inc(ids_in[s][k], 16)

                    def head():
                        load_ids(0, 0, 1, 0)
                        load_ids(0, 1, 1, 0)

                    def body(i, now, before):
                        s = now[0]
                        if isinstance(i, int) and i == 1:
                            for k in pr:
                                e.wait_ge(gathered[k], 32)
                                load_gu(0, k, 2 + k)
                                load_dn(0, k, 2 + k)
                                load_ids(1, k, 0, 0)
                            return
                        free = i if before[0] == s else i - 1
                        for k in pr:
                            expert = tile_entry(e, i, k, 0, NE - 1)
                            e.wait_ge(gu_done[k], free)
                            load_gu(s, k, expert)
                            e.wait_ge(dn_done[k], free)
                            load_dn(s, k, expert)
                            load_ids(i, k, s, 16 * free)
                    pair_loop(e, head, body)

                @block.gpsimd
                def _(e):
                    for k in pr:
                        pool.memset(xg[k][:, :], 0.0).then_inc(cleared, 1)
                    e.wait_ge(cleared, 2)

                    def carry_wait(c):
                        pool.tensor_tensor(spare[:, c:c + 1], mhalf[:, 0:1], mhalf[:, 0:1], ALU.mult).then_inc(carried, 1)

                    def gather(i, k):
                        e.wait_ge(idg_in[k], 16 * i + 16)
                        wait(e, xg_turned[k], i)
                        carry_wait(k)
                        pool.indirect_dma_start(xg[k][:, :], None, h_d,
                                                bass.IndirectOffsetOnAxis(ap=idg[k][:, 1:2], axis=0),
                                                bounds_check=TP - 1, oob_is_err=False).then_inc(gathered[k], 16)

                    def scatter(i, k, used):
                        e.wait_ge(yo_ready[k], 2 * i + 2)
                        carry_wait(2 + k)
                        pool.indirect_dma_start(y2_d, bass.IndirectOffsetOnAxis(ap=ids[used[0]][k][:, 0:1], axis=0),
                                                yo[k][:, :], None, bounds_check=2 * TP - 1, oob_is_err=False
                                                ).then_inc(scattered[k], 16)

                    def head():
                        gather(0, 0)
                        gather(0, 1)
                        e.wait_ge(carried, 2)
                        gather(1, 0)
                        gather(1, 1)

                    def body(i, now, before):
                        e.wait_ge(carried, 4 * i)
                        gather(i + 1, 0)
                        scatter(i - 1, 0, before)
                        gather(i + 1, 1)
                        scatter(i - 1, 1, before)

                    def tail(m, now):
                        e.wait_ge(carried, 4 * m + 4)
                        scatter(m, 0, now)
                        scatter(m, 1, now)
                        for k in pr:
                            e.wait_ge(scattered[k], 16 * m + 16)
                            e.wait_ge(gathered[k], 16 * m + 32)
                    pair_loop(e, head, body, tail)

                @block.tensor
                def _(e):
                    def turn_x(i, k):
                        e.wait_ge(gathered[k], 16 * i + 16)
                        wait(e, xgT_ready[1 - k], 2 * i if k == 0 else 2 * i + 2)
                        for c in range(KT):
                            bank, at = b[c // H], (c % H) * P
                            last = pe.transpose(bank[:, at:at + P], xg[k][:, c * P:(c + 1) * P], C("ident"))
                        last.then_inc(xg_turned[k], 1)

                    def gate_up(i, k, used):
                        s, uses = used
                        e.wait_ge(xgT_ready[k], 2 * i + 2)
                        e.wait_ge(gu_in[s][k], 32 * uses + 32)
                        for c in range(KT):
                            last = pe.matmul(b[2 + k][:, :], xgT[k][:, c, :], wgu[s][k][:, c, :],
                                             start=(c == 0), stop=(c == KT - 1))
                        last.then_inc(gu_done[k], 1)

                    def turn_ac(i, k):
                        e.wait_ge(ac_ready[k], i + 1)
                        for c in range(FE // P):
                            last = pe.transpose(b[4 + k][:, c * P:(c + 1) * P], ac[k][:, c * P:(c + 1) * P],
                                                C("ident"))
                        last.then_inc(ac_turned[k], 1)

                    def down(i, k, used):
                        s, uses = used
                        e.wait_ge(acT_ready[k], i + 1)
                        e.wait_ge(dn_in[s][k], 16 * uses + 16)
                        wait(e, yo_ready[1 - k], 2 * i if k == 0 else 2 * i + 2)
                        for half in range(2):
                            for c in range(FE // P):
                                last = pe.matmul(b[6 + half][:, :], acT[k][:, c, :],
                                                 wdn[s][k][:, c, half * 512:(half + 1) * 512],
                                                 start=(c == 0), stop=(c == FE // P - 1))
                        last.then_inc(dn_done[k], 1)

                    def head():
                        turn_x(0, 0)
                        turn_x(0, 1)
                        gate_up(0, 0, (1, 0))
                        turn_ac(0, 0)

                    def body(i, now, before):
                        turn_x(i, 0)
                        gate_up(i - 1, 1, before)
                        down(i - 1, 0, before)
                        turn_ac(i - 1, 1)
                        turn_x(i, 1)
                        gate_up(i, 0, now)
                        down(i - 1, 1, before)
                        turn_ac(i, 0)

                    def tail(m, now):
                        gate_up(m, 1, now)
                        down(m, 0, now)
                        turn_ac(m, 1)
                        down(m, 1, now)
                    pair_loop(e, head, body, tail)

                def x_turned_s(e, i, k):
                    e.wait_ge(xg_turned[k], i + 1)
                    act.activation(xgT[k][:, 0:H, :].rearrange("p c t -> p (c t)"), b[0][:, :], ACT.Copy
                                   ).then_inc(xgT_ready[k], 1)
                    act.dma_start(idg[k][:, :], tab_d[ds(tile_entry(e, i + 1, k, 1, NE * SLOTS), P), :]
                                  ).then_inc(idg_in[k], 16)

                def silu(e, i, k):
                    e.wait_ge(gu_done[k], i + 1)
                    act.activation(sg[k][:, :], b[2 + k][:, 0:FE], ACT.Silu).then_inc(silu_ready[k], 1)

                def ac_turned_s(e, i, k):
                    e.wait_ge(ac_turned[k], i + 1)
                    act.activation(acT[k][:, :, :].rearrange("p c t -> p (c t)"), b[4 + k][:, 0:FE], ACT.Copy
                                   ).then_inc(acT_ready[k], 1)

                def out_s(e, i, k):
                    e.wait_ge(dn_done[k], i + 1)
                    wait(e, scattered[k], 16 * i)
                    act.activation(yo[k][:, 0:512], b[6][:, :], ACT.Copy).then_inc(yo_ready[k], 1)

                @block.scalar
                def _(e):
                    def head():
                        for k in pr:
                            act.dma_start(idg[k][:, :], tab_d[k * SLOTS:k * SLOTS + P, :]).then_inc(idg_in[k], 16)
                        x_turned_s(e, 0, 0)
                        x_turned_s(e, 0, 1)
                        silu(e, 0, 0)
                        ac_turned_s(e, 0, 0)

                    def body(i, now, before):
                        x_turned_s(e, i, 0)
                        silu(e, i - 1, 1)
                        out_s(e, i - 1, 0)
                        ac_turned_s(e, i - 1, 1)
                        x_turned_s(e, i, 1)
                        silu(e, i, 0)
                        out_s(e, i - 1, 1)
                        ac_turned_s(e, i, 0)

                    def tail(m, now):
                        silu(e, m, 1)
                        out_s(e, m, 0)
                        ac_turned_s(e, m, 1)
                        out_s(e, m, 1)
                    pair_loop(e, head, body, tail)

                def x_turned_v(e, i, k):
                    e.wait_ge(xg_turned[k], i + 1)
                    dve.tensor_copy(xgT[k][:, H:, :].rearrange("p c t -> p (c t)"), b[1][:, :]
                                    ).then_inc(xgT_ready[k], 1)

                def gate(e, i, k, used):
                    s, uses = used
                    e.wait_ge(silu_ready[k], i + 1)
                    e.wait_ge(ids_in[s][k], 16 * uses + 16)
                    dve.scalar_tensor_tensor(out=ac[k][:, :], in0=sg[k][:, :],
                                             scalar=ids[s][k][:, 2:3].bitcast(F32), in1=b[2 + k][:, FE:],
                                             op0=ALU.mult, op1=ALU.mult).then_inc(ac_ready[k], 1)

                def out_v(e, i, k):
                    e.wait_ge(dn_done[k], i + 1)
                    wait(e, scattered[k], 16 * i)
                    dve.tensor_copy(yo[k][:, 512:], b[7][:, :]).then_inc(yo_ready[k], 1)

                @block.vector
                def _(e):
                    def head():
                        x_turned_v(e, 0, 0)
                        x_turned_v(e, 0, 1)
                        gate(e, 0, 0, (1, 0))

                    def body(i, now, before):
                        x_turned_v(e, i, 0)
                        gate(e, i - 1, 1, before)
                        out_v(e, i - 1, 0)
                        x_turned_v(e, i, 1)
                        gate(e, i, 0, now)
                        out_v(e, i - 1, 1)

                    def tail(m, now):
                        gate(e, m, 1, now)
                        out_v(e, m, 0)
                        out_v(e, m, 1)
                    pair_loop(e, head, body, tail)

        with ExitStack() as c5:
            NB = 3
            pr = range(NB)

            def each(name, shape):
                return [sb(f"{name}{k}", shape, ctx=c5) for k in pr]
            picked, res = each("picked", [P, 2 * D]), each("res", [P, D])
            lng = sb("ln2g", [P, D], ctx=c5)
            lnb = sb("ln2b", [P, D], ctx=c5)
            stats, mv = each("stats2", [P, 2, 6]), each("mv2", [P, 2])
            rstd, shift = each("rstd2", [P, 1]), each("shift2", [P, 1])
            spare = sb("spare5", [P, 1], ctx=c5)
            ysum = [pb(f"ysum{k}", [P, D], c5) for k in pr]
            S = phase(c5)
            S2 = lambda n: [S(f"{n}{i}") for i in pr]
            ln_in, chn = S("ln2_in"), S("chn2")
            in_ready, summed, ysum_read, var_ready, rstd1, rstd_ready, norm_ready, g_ready, out_ready, stored = (
                S2(n) for n in ("in_ready", "summed", "ysum_read", "var_ready2", "rstd1", "rstd_ready2", "norm_ready2",
                                "g_ready2", "out_ready", "stored"))

            with nc.Block() as block:
                @block.sync
                def _(e):
                    y2_v = y2_d.rearrange("(t k) d -> t (k d)", k=2)

                    def load(i, k, m=P):
                        wait(e, summed[k], i)
                        sp.dma_start(picked[k][0:m, :], y2_v[ds((NB * i + k) * P, m), :]).then_inc(in_ready[k], 16)

                    load(0, 0)
                    load(0, 1)
                    sp.dma_start(lng[:, :], ln2g_d.broadcast_to((P, D))).then_inc(ln_in, 16)
                    sp.dma_start(lnb[:, :], ln2b_d.broadcast_to((P, D))).then_inc(ln_in, 16)
                    load(0, 2)
                    with e.Fori(1, NT // NB - 1) as i:
                        for k in pr:
                            load(i, k)
                    for k in pr:
                        load(NT // NB - 1, k, P if k < NB - 1 else NS)
                    for k in pr:
                        e.wait_ge(stored[k], 16 * (NT // NB))

                def done(i, k):
                    return hres[:, ds(NB * i + k, 1), :].rearrange("p a d -> p (a d)")

                def rounds(e, step):
                    def body(i):
                        for k in pr:
                            step(i, k)
                    turns(e, NT // NB, body)

                @block.gpsimd
                def _(e):
                    e.wait_ge(ln_in, 32)

                    def step(i, k):
                        e.wait_ge(var_ready[k], i + 1)
                        pool.tensor_tensor(rstd[k][:, :], mv[k][:, 1:2], mhalf[:, 0:1], ALU.pow).then_inc(rstd1[k], 1)
                        e.wait_ge(rstd1[k], i + 1)
                        pool.tensor_tensor(shift[k][:, :], mv[k][:, 0:1], rstd[k][:, :], ALU.mult
                                           ).then_inc(rstd_ready[k], 1)

                    def add_bias(i, k):
                        e.wait_ge(g_ready[k], i + 1)
                        pool.tensor_tensor(done(i, k), done(i, k), lnb[:, :], ALU.add).then_inc(out_ready[k], 1)

                    def both(i, k):
                        step(i, k)
                        if k > 0:
                            add_bias(i, k - 1)
                        elif not isinstance(i, int):
                            add_bias(i - 1, NB - 1)
                    rounds(e, both)
                    add_bias(NT // NB - 1, NB - 1)

                @block.tensor
                def _(e):
                    def step(i, k):
                        e.wait_ge(in_ready[k], 16 * i + 16)
                        wait(e, ysum_read[k], i)
                        for half in range(2):
                            for pick in range(2):
                                at = pick * D + half * 512
                                last = pe.matmul(ysum[k][:, half * 512:(half + 1) * 512], C("ident"),
                                                 picked[k][:, at:at + 512], start=(pick == 0), stop=(pick == 1))
                        last.then_inc(summed[k], 1)
                    rounds(e, step)

                @block.scalar
                def _(e):
                    def step(i, k):
                        e.wait_ge(rstd_ready[k], i + 1)
                        act.activation(done(i, k), res[k][:, :], ACT.Identity, scale=rstd[k][:, :],
                                       bias=shift[k][:, :]).then_inc(norm_ready[k], 1)

                    def store(i, k):
                        e.wait_ge(out_ready[k], i + 1)
                        act.dma_start(yp_o[0, ds((NB * i + k) * P, P), :], done(i, k)).then_inc(stored[k], 16)

                    def both(i, k):
                        step(i, k)
                        if k > 0:
                            store(i, k - 1)
                        elif not isinstance(i, int):
                            store(i - 1, NB - 1)
                    rounds(e, both)
                    e.wait_ge(out_ready[NB - 1], NT // NB)
                    act.dma_start(ys_o.rearrange("s t d -> (s t) d"), hres[0:NS, NT - 1, :]
                                  ).then_inc(stored[NB - 1], 16)

                @block.vector
                def _(e):
                    def front(i, k):
                        at = (NB * i + k) * 2
                        ln = [0]

                        def link(ins):
                            ln[0] += 1
                            ins.then_inc(chn, 1)
                            e.wait_ge(chn, at + ln[0])
                        e.wait_ge(summed[k], i + 1)
                        wait(e, norm_ready[k], i)
                        r = res[k][:, :]
                        dve.scalar_tensor_tensor(out=r, in0=done(i, k), scalar=ALPHA, in1=ysum[k][:, :],
                                                 op0=ALU.mult, op1=ALU.add).then_inc(ysum_read[k], 1)
                        e.wait_ge(ysum_read[k], i + 1)
                        for half in range(2):
                            last = dve.bn_stats(stats[k][:, half, :], r[:, half * 512:(half + 1) * 512])
                        link(last)
                        dve.memset(spare[:, :], 0.0)
                        link(dve.bn_aggr(mv[k][:, :], stats[k][:, :, :].rearrange("p a b -> p (a b)")))
                        dve.tensor_scalar(mv[k][:, 0:1], mv[k][:, 0:1], -1.0, None, ALU.mult)
                        dve.tensor_scalar(mv[k][:, 1:2], mv[k][:, 1:2], LN_EPS, None, ALU.add
                                          ).then_inc(var_ready[k], 1)

                    def scale(i, k):
                        if k == 0 and isinstance(i, int):
                            e.wait_ge(ln_in, 32)
                        e.wait_ge(norm_ready[k], i + 1)
                        dve.tensor_tensor(done(i, k), done(i, k), lng[:, :], ALU.mult).then_inc(g_ready[k], 1)

                    def both(i, k):
                        front(i, k)
                        if k > 0:
                            scale(i, k - 1)
                        elif not isinstance(i, int):
                            scale(i - 1, NB - 1)
                    rounds(e, both)
                    scale(NT // NB - 1, NB - 1)


INPUTS = ["x_prompt", "x_sample", "state_delta", "state_conv", "state_pool", "w_in", "conv_w", "a_log", "dt_bias",
          "gdn_norm_w", "pool_w", "pool_scale", "w_out", "ln1_g", "ln1_b", "w_rg", "b_rg", "w_re", "b_re",
          "w_gate", "w_up", "w_down", "ln2_g", "ln2_b"]
OUTPUTS = [(1, SEQ, D), (NSEQ, DSEQ, D), (1, 1, H, HD, HD), (1, 1, CH, 3 * DA), (1, 1, PH, G * P),
           (1, NSEQ, H, HD, HD), (1, NSEQ, CH, 3 * DA), (1, NSEQ, PH, G * P)]


def kernel(**inputs):
    import concourse.bacc as bacc
    from concourse.bass_utils import run_bass_kernel_spmd

    nc = bacc.Bacc("TRN2", target_bir_lowering=False, num_devices=1)
    arrays = {"in_constants_dram": constants()}
    for name in INPUTS:
        arrays[f"in_{name}_dram"] = np.ascontiguousarray(inputs[name])
    args = [nc.dram_tensor(name, a.shape, mybir.dt.from_np(a.dtype), kind="ExternalInput").ap()
            for name, a in arrays.items()]
    for i, shape in enumerate(OUTPUTS):
        args.append(nc.dram_tensor(f"out_{i}_dram", shape, F32, kind="ExternalOutput").ap())
    args.append(nc.dram_tensor("pooled_dram", (G, P, TP), F32, kind="Internal").ap())
    args.append(nc.dram_tensor("h_dram", (TP, D), F32, kind="Internal").ap())
    args.append(nc.dram_tensor("picked_dram", (2 * TP, D), F32, kind="Internal").ap())
    args.append(nc.dram_tensor("lists_dram", (NLIST * SLOTS, 4), I32, kind="Internal").ap())
    build(nc, *args)
    r = run_bass_kernel_spmd(nc, [arrays], core_ids=[0])
    return tuple(r.results[0][f"out_{i}_dram"] for i in range(len(OUTPUTS)))
```
